# Optimizing a Trainium2 kernel written in Bass

```python
import jax
import jax.numpy as jnp
from jax import lax
import numpy as np
import jax, jax.numpy as jnp

D_MODEL = 2048
BATCH = 1
SEQ = 256
DEPTH = 1

A_HEADS = 8
A_KV_HEADS = 2
A_HEAD_DIM = 128
IDX_HEADS = 16
IDX_DIM = 64
TOPK_MAX = 256
M_HEADS = 8
M_Q_LORA = 512
M_KV_LORA = 256
M_NOPE = 128
M_ROPE = 64
M_V = 128
D_FF = 5632
CONV_W = 3
ROPE_THETA = 500000.0
ROT_FRACTION = 4
EPS = 1e-6
Q_BLOCK = 128
N_ADA = 6
IN_SIZES = (A_HEADS * A_HEAD_DIM, A_KV_HEADS * A_HEAD_DIM, A_KV_HEADS * A_HEAD_DIM,
            IDX_HEADS * IDX_DIM, IDX_DIM, IDX_HEADS,
            M_Q_LORA, M_KV_LORA, M_ROPE,
            D_MODEL, D_MODEL)
IN_DIM = sum(IN_SIZES)
IDX_W_SCALE = (IDX_HEADS * IDX_DIM) ** -0.5


def rms_norm(t, g):
    tf = t.astype(jnp.float32)
    y = tf * lax.rsqrt(jnp.mean(tf * tf, axis=-1, keepdims=True) + EPS)
    return (y * g.astype(jnp.float32)).astype(t.dtype)

def rope_tables(pos, rot_dim):
    inv = ROPE_THETA ** (-jnp.arange(0, rot_dim, 2, dtype=jnp.float32) / rot_dim)
    ang = pos[..., None] * inv
    return jnp.cos(ang)[:, :, None, :], jnp.sin(ang)[:, :, None, :]

def apply_rope(t, cos, sin):
    r = cos.shape[-1] * 2
    tf = t[..., :r].astype(jnp.float32)
    t1, t2 = tf[..., : r // 2], tf[..., r // 2:]
    rot = jnp.concatenate([t1 * cos - t2 * sin, t2 * cos + t1 * sin], axis=-1).astype(t.dtype)
    return jnp.concatenate([rot, t[..., r:]], axis=-1)

def split_cols(t, sizes):
    offsets = np.cumsum(sizes)[:-1]
    return jnp.split(t, [int(o) for o in offsets], axis=-1)

def to_blocks(t, nb):
    b = t.shape[0]
    return jnp.moveaxis(t.reshape((b, nb, Q_BLOCK) + t.shape[2:]), 1, 0)

def from_blocks(t):
    nb, b, tq = t.shape[:3]
    return jnp.moveaxis(t, 0, 1).reshape((b, nb * tq) + t.shape[3:])

def dsa_attention(q, k, v, qi, ki, wi):
    B, S, H, dh = q.shape
    G = k.shape[2]
    n_sel = min(TOPK_MAX, S // 4)
    nb = S // Q_BLOCK
    key_pos = jnp.arange(S)
    scale = dh ** -0.5

    def block(args):
        q_b, qi_b, wi_b, start = args
        q_pos = start + jnp.arange(Q_BLOCK)
        causal = key_pos[None, :] <= q_pos[:, None]
        dots = jnp.einsum('bthd,bsd->bths', qi_b, ki, preferred_element_type=jnp.float32)
        score = jnp.einsum('bths,bth->bts', jax.nn.relu(dots), wi_b.astype(jnp.float32))
        score = jnp.where(causal[None], score, -jnp.inf)
        _, sel = lax.top_k(score, n_sel)
        valid = sel <= q_pos[None, :, None]
        k_sel = jax.vmap(lambda kk, ii: kk[ii])(k, sel)
        v_sel = jax.vmap(lambda vv, ii: vv[ii])(v, sel)
        qg = q_b.reshape(B, Q_BLOCK, G, H // G, dh)
        logits = jnp.einsum('btgrd,btkgd->btgrk', qg, k_sel,
                            preferred_element_type=jnp.float32) * scale
        logits = jnp.where(valid[:, :, None, None, :], logits, -jnp.inf)
        p = jax.nn.softmax(logits, axis=-1).astype(v.dtype)
        o = jnp.einsum('btgrk,btkgd->btgrd', p, v_sel)
        return o.reshape(B, Q_BLOCK, H * dh)

    starts = jnp.arange(nb) * Q_BLOCK
    out = lax.map(block, (to_blocks(q, nb), to_blocks(qi, nb), to_blocks(wi, nb), starts))
    return from_blocks(out)

def causal_dense_attention(q, k, v):
    B, S, H, dqk = q.shape
    dv = v.shape[-1]
    nb = S // Q_BLOCK
    key_pos = jnp.arange(S)
    scale = dqk ** -0.5

    def block(args):
        q_b, start = args
        q_pos = start + jnp.arange(Q_BLOCK)
        causal = key_pos[None, :] <= q_pos[:, None]
        logits = jnp.einsum('bthd,bshd->bhts', q_b, k, preferred_element_type=jnp.float32) * scale
        logits = jnp.where(causal[None, None], logits, -jnp.inf)
        p = jax.nn.softmax(logits, axis=-1).astype(v.dtype)
        return jnp.einsum('bhts,bshd->bthd', p, v).reshape(B, Q_BLOCK, H * dv)

    starts = jnp.arange(nb) * Q_BLOCK
    out = lax.map(block, (to_blocks(q, nb), starts))
    return from_blocks(out)

def parallel_mixers(h, w_in, g_qa, g_ka, g_mq_lat, w_mq_up, g_mkv_lat, w_mkv_up,
                    g_qm, g_km, w_pa, w_pb, w_o, rope_a, rope_i, rope_m):
    B, S, _ = h.shape
    proj = h @ w_in
    (qa, ka, va, qi, ki, wi, mq_lat, mkv_lat, mk_rope, gate_a, gate_b) = split_cols(proj, IN_SIZES)

    qa = apply_rope(rms_norm(qa.reshape(B, S, A_HEADS, A_HEAD_DIM), g_qa), *rope_a)
    ka = apply_rope(rms_norm(ka.reshape(B, S, A_KV_HEADS, A_HEAD_DIM), g_ka), *rope_a)
    va = va.reshape(B, S, A_KV_HEADS, A_HEAD_DIM)
    qi = apply_rope(qi.reshape(B, S, IDX_HEADS, IDX_DIM), *rope_i)
    ki = apply_rope(ki[:, :, None, :], *rope_i)[:, :, 0, :]
    o_a = dsa_attention(qa, ka, va, qi, ki, wi * IDX_W_SCALE)

    mq = (rms_norm(mq_lat, g_mq_lat) @ w_mq_up).reshape(B, S, M_HEADS, M_NOPE + M_ROPE)
    mkv = (rms_norm(mkv_lat, g_mkv_lat) @ w_mkv_up).reshape(B, S, M_HEADS, M_NOPE + M_V)
    mk_nope, mv = mkv[..., :M_NOPE], mkv[..., M_NOPE:]
    mk_r = jnp.broadcast_to(mk_rope[:, :, None, :], (B, S, M_HEADS, M_ROPE))
    mk = rms_norm(jnp.concatenate([mk_nope, mk_r], axis=-1), g_km)
    mq = rms_norm(mq, g_qm)
    mq = jnp.concatenate([mq[..., :M_NOPE], apply_rope(mq[..., M_NOPE:], *rope_m)], axis=-1)
    mk = jnp.concatenate([mk[..., :M_NOPE], apply_rope(mk[..., M_NOPE:], *rope_m)], axis=-1)
    o_b = causal_dense_attention(mq, mk, mv)

    merged = jax.nn.sigmoid(gate_a) * (o_a @ w_pa) + jax.nn.sigmoid(gate_b) * (o_b @ w_pb)
    return merged @ w_o

def conv_ffn(h, w_up, w_conv, b_conv, w_down):
    S = h.shape[1]
    u = h @ w_up
    up = jnp.pad(u, ((0, 0), (CONV_W - 1, 0), (0, 0)))
    conv = b_conv
    for j in range(CONV_W):
        conv = conv + w_conv[j] * up[:, j:j + S]
    gate, val = jnp.split(conv, 2, axis=-1)
    return (jax.nn.silu(gate) * val) @ w_down

def first_inputs(seed: int = 0) -> dict:
    key = jax.random.key(seed)
    ks = jax.random.split(key, 24)
    f32 = jnp.float32

    def nrm(k, shape, scale):
        return jax.random.normal(k, shape, f32) * scale

    def gain(k, shape):
        return 1.0 + 0.02 * jax.random.normal(k, shape, f32)

    L, D = DEPTH, D_MODEL
    x = nrm(ks[0], (BATCH, SEQ, D), 1.0)
    c = nrm(ks[1], (BATCH, D), 1.0)
    offset = jax.random.randint(ks[2], (BATCH, 1), 0, 1024, dtype=jnp.int32)
    positions = (jnp.arange(SEQ, dtype=jnp.int32)[None, :] + offset).astype(jnp.int32)
    return {
        'x': x,
        'c': c,
        'positions': positions,
        'g_attn': gain(ks[3], (L, D)),
        'g_ffn': gain(ks[4], (L, D)),
        'w_ada': nrm(ks[5], (L, D, N_ADA * D), 0.5 * D ** -0.5),
        'b_ada': nrm(ks[6], (L, N_ADA * D), 0.01),
        'w_in': nrm(ks[7], (L, D, IN_DIM), D ** -0.5),
        'g_qa': gain(ks[8], (L, A_HEAD_DIM)),
        'g_ka': gain(ks[9], (L, A_HEAD_DIM)),
        'g_mq_lat': gain(ks[10], (L, M_Q_LORA)),
        'w_mq_up': nrm(ks[11], (L, M_Q_LORA, M_HEADS * (M_NOPE + M_ROPE)), M_Q_LORA ** -0.5),
        'g_mkv_lat': gain(ks[12], (L, M_KV_LORA)),
        'w_mkv_up': nrm(ks[13], (L, M_KV_LORA, M_HEADS * (M_NOPE + M_V)), M_KV_LORA ** -0.5),
        'g_qm': gain(ks[14], (L, M_NOPE + M_ROPE)),
        'g_km': gain(ks[15], (L, M_NOPE + M_ROPE)),
        'w_pa': nrm(ks[16], (L, A_HEADS * A_HEAD_DIM, D), (A_HEADS * A_HEAD_DIM) ** -0.5),
        'w_pb': nrm(ks[17], (L, M_HEADS * M_V, D), (M_HEADS * M_V) ** -0.5),
        'w_o': nrm(ks[18], (L, D, D), D ** -0.5),
        'w_up': nrm(ks[19], (L, D, 2 * D_FF), D ** -0.5),
        'w_conv': nrm(ks[20], (L, CONV_W, 2 * D_FF), CONV_W ** -0.5),
        'b_conv': nrm(ks[21], (L, 2 * D_FF), 0.01),
        'w_down': nrm(ks[22], (L, D_FF, D), D_FF ** -0.5),
    }

def first_block(x, c, positions, g_attn, g_ffn, w_ada, b_ada, w_in, g_qa, g_ka,
              g_mq_lat, w_mq_up, g_mkv_lat, w_mkv_up, g_qm, g_km, w_pa, w_pb, w_o,
              w_up, w_conv, b_conv, w_down):
    pos = positions.astype(jnp.float32)
    rope_a = rope_tables(pos, A_HEAD_DIM // ROT_FRACTION)
    rope_i = rope_tables(pos, IDX_DIM // ROT_FRACTION)
    rope_m = rope_tables(pos, M_ROPE)
    c_act = jax.nn.silu(c)
    for l in range(DEPTH):
        mod = (c_act @ w_ada[l] + b_ada[l])[:, None, :]
        sh_a, sc_a, gt_a, sh_f, sc_f, gt_f = jnp.split(mod, N_ADA, axis=-1)
        h = rms_norm(x, g_attn[l]) * (1.0 + sc_a) + sh_a
        y = parallel_mixers(h, w_in[l], g_qa[l], g_ka[l], g_mq_lat[l], w_mq_up[l],
                            g_mkv_lat[l], w_mkv_up[l], g_qm[l], g_km[l], w_pa[l], w_pb[l],
                            w_o[l], rope_a, rope_i, rope_m)
        x = x + gt_a * y
        h = rms_norm(x, g_ffn[l]) * (1.0 + sc_f) + sh_f
        x = x + gt_f * conv_ffn(h, w_up[l], w_conv[l], b_conv[l], w_down[l])
    return x


N_MIXERS = 3
GRID_W = 64
BRANCH_W = D_MODEL
NORM_EPS = 1e-6

POOL_WINDOWS = (2, 4, 8, 16)
N_POOL_GROUPS = 4
POOL_GROUP_DIM = BRANCH_W // N_POOL_GROUPS

GLA_HEADS = 4
GLA_KEY_W = D_MODEL // 2
GLA_VAL_W = BRANCH_W
GLA_DK = GLA_KEY_W // GLA_HEADS
GLA_DV = GLA_VAL_W // GLA_HEADS
GLA_LOWRANK = 16
GLA_TAU = 16.0
GLA_CHUNK = 64

ATTN_HEAD_DIM = 128
ATTN_HEADS = BRANCH_W // ATTN_HEAD_DIM
ATTN_KV_HEADS = 4
ATTN_GROUP = ATTN_HEADS // ATTN_KV_HEADS
ATTN_Q_W = ATTN_HEADS * ATTN_HEAD_DIM
ATTN_KV_W = ATTN_KV_HEADS * ATTN_HEAD_DIM
ATTN_BLOCK = 128
ROPE_AXIS_DIM = ATTN_HEAD_DIM // 2
ROPE_THETA_2 = 10000.0


def rms_norm_2(x, eps=NORM_EPS):
    xf = x.astype(jnp.float32)
    return (xf * lax.rsqrt(jnp.mean(xf * xf, axis=-1, keepdims=True) + eps)).astype(x.dtype)

def ada_modulation(c, w, b):
    m = jnp.dot(jax.nn.silu(c), w) + b
    shift, scale, gate = jnp.split(m, 3, axis=-1)
    return shift[:, None], scale[:, None], gate[:, None]

def centred_window_mean(u, w):
    T = u.shape[1]
    csum = jnp.cumsum(u.astype(jnp.float32), axis=1)
    P = jnp.concatenate([jnp.zeros_like(csum[:, :1]), csum], axis=1)
    t = jnp.arange(T)
    lo = jnp.maximum(t - w // 2, 0)
    hi = jnp.minimum(t + w // 2, T)
    cnt = (hi - lo).astype(jnp.float32)
    return ((P[:, hi] - P[:, lo]) / cnt[None, :, None]).astype(u.dtype)

def pool_mixer(h, w_in, w_grp, scale, w_out):
    B, T, _ = h.shape
    u, g = jnp.split(h @ w_in, 2, axis=-1)
    ug = u.reshape(B, T, N_POOL_GROUPS, POOL_GROUP_DIM)
    pooled = jnp.stack(
        [centred_window_mean(ug[:, :, i], w) - ug[:, :, i] for i, w in enumerate(POOL_WINDOWS)],
        axis=2)
    y = jnp.einsum('btgc,gcd->btgd', pooled, w_grp).reshape(B, T, BRANCH_W) * scale
    return (y * jax.nn.silu(g)) @ w_out

def gla_chunked_scan(q, k, v, log_a, include_diag):
    B, T, H, DK = q.shape
    DV = v.shape[-1]
    nc = T // GLA_CHUNK

    def to_chunks(z):
        return z.astype(jnp.float32).reshape(B, nc, GLA_CHUNK, H, z.shape[-1]).transpose(1, 0, 3, 2, 4)

    qc, kc, vc, ac = to_chunks(q), to_chunks(k), to_chunks(v), to_chunks(log_a)
    mask = jnp.tril(jnp.ones((GLA_CHUNK, GLA_CHUNK), dtype=bool), 0 if include_diag else -1)

    def step(S, inp):
        qi, ki, vi, ai = inp
        b = jnp.cumsum(ai, axis=2)
        o_inter = jnp.einsum('bhcd,bhde->bhce', qi * jnp.exp(b), S)
        diff = b[:, :, :, None, :] - b[:, :, None, :, :]
        decay = jnp.exp(jnp.where(mask[:, :, None], diff, -jnp.inf))
        A = jnp.sum(qi[:, :, :, None, :] * ki[:, :, None, :, :] * decay, axis=-1)
        o_intra = jnp.einsum('bhij,bhje->bhie', A, vi)
        b_last = b[:, :, -1:, :]
        S_new = jnp.exp(b_last[:, :, 0, :])[..., None] * S + jnp.einsum(
            'bhjd,bhje->bhde', ki * jnp.exp(b_last - b), vi)
        return S_new, o_inter + o_intra

    S0 = jnp.zeros((B, H, DK, DV), jnp.float32)
    _, o = lax.scan(step, S0, (qc, kc, vc, ac))
    return o.transpose(1, 0, 3, 2, 4).reshape(B, T, H, DV)

def gla_mixer(h, w_in, fwd_w1, fwd_w2, fwd_b, bwd_w1, bwd_w2, bwd_b, norm_g, w_out):
    B, T, _ = h.shape
    q, k, v, g = jnp.split(h @ w_in, [GLA_KEY_W, 2 * GLA_KEY_W, 2 * GLA_KEY_W + GLA_VAL_W], axis=-1)
    q = (q * GLA_DK ** -0.5).reshape(B, T, GLA_HEADS, GLA_DK)
    k = k.reshape(B, T, GLA_HEADS, GLA_DK)
    v = v.reshape(B, T, GLA_HEADS, GLA_DV)

    def log_decay(w1, w2, b):
        z = ((h @ w1) @ w2 + b).astype(jnp.float32)
        return (jax.nn.log_sigmoid(z) / GLA_TAU).reshape(B, T, GLA_HEADS, GLA_DK)

    rev = lambda z: z[:, ::-1]
    o_fwd = gla_chunked_scan(q, k, v, log_decay(fwd_w1, fwd_w2, fwd_b), include_diag=True)
    o_bwd = rev(gla_chunked_scan(rev(q), rev(k), rev(v), rev(log_decay(bwd_w1, bwd_w2, bwd_b)),
                                 include_diag=False))
    o = (rms_norm_2(o_fwd + o_bwd) * norm_g).reshape(B, T, GLA_VAL_W).astype(h.dtype)
    return (o * jax.nn.silu(g)) @ w_out

def axial_rope_tables(T):
    rows = T // GRID_W
    t = jnp.arange(T)
    row = (t // GRID_W - rows // 2).astype(jnp.float32)
    col = (t % GRID_W - GRID_W // 2).astype(jnp.float32)
    inv = ROPE_THETA_2 ** (-jnp.arange(0, ROPE_AXIS_DIM, 2, dtype=jnp.float32) / ROPE_AXIS_DIM)
    ang = jnp.concatenate([row[:, None] * inv, col[:, None] * inv], axis=-1)
    return jnp.cos(ang), jnp.sin(ang)

def apply_rope_2(x, cos, sin):
    shp = (cos.shape[0],) + (1,) * (x.ndim - 3) + (cos.shape[1],)
    cos = cos.reshape(shp).astype(x.dtype)
    sin = sin.reshape(shp).astype(x.dtype)
    xr = x.reshape(x.shape[:-1] + (-1, 2))
    x0, x1 = xr[..., 0], xr[..., 1]
    return jnp.stack([x0 * cos - x1 * sin, x0 * sin + x1 * cos], axis=-1).reshape(x.shape)

def attn_mixer(h, w_in, q_norm_g, k_norm_g, w_out):
    B, T, _ = h.shape
    q, k, v, g = jnp.split(h @ w_in, [ATTN_Q_W, ATTN_Q_W + ATTN_KV_W, ATTN_Q_W + 2 * ATTN_KV_W], axis=-1)
    q = rms_norm_2(q.reshape(B, T, ATTN_KV_HEADS, ATTN_GROUP, ATTN_HEAD_DIM)) * q_norm_g
    k = rms_norm_2(k.reshape(B, T, ATTN_KV_HEADS, ATTN_HEAD_DIM)) * k_norm_g
    v = v.reshape(B, T, ATTN_KV_HEADS, ATTN_HEAD_DIM)
    cos, sin = axial_rope_tables(T)
    q = apply_rope_2(q, cos, sin) * ATTN_HEAD_DIM ** -0.5
    k = apply_rope_2(k, cos, sin)
    nb = T // ATTN_BLOCK
    qb = q.reshape(B, nb, ATTN_BLOCK, ATTN_KV_HEADS, ATTN_GROUP, ATTN_HEAD_DIM).transpose(1, 0, 2, 3, 4, 5)

    def block(qi):
        s = jnp.einsum('bqkgd,bskd->bkgqs', qi, k, preferred_element_type=jnp.float32)
        p = jax.nn.softmax(s, axis=-1).astype(v.dtype)
        return jnp.einsum('bkgqs,bskd->bqkgd', p, v)

    o = lax.map(block, qb).transpose(1, 0, 2, 3, 4, 5).reshape(B, T, ATTN_Q_W)
    return (o * jax.nn.silu(g)) @ w_out

def second_inputs(seed: int = 0) -> dict:
    key = jax.random.key(seed)
    ks = iter(jax.random.split(key, 40))
    n_pool = len(range(0, DEPTH, N_MIXERS))
    n_gla = len(range(1, DEPTH, N_MIXERS))
    n_attn = len(range(2, DEPTH, N_MIXERS))
    D = D_MODEL

    def nrm(shape, scale):
        return jax.random.normal(next(ks), shape, jnp.float32) * scale

    def gain(shape):
        return 1.0 + 0.1 * jax.random.normal(next(ks), shape, jnp.float32)

    return {
        "x": nrm((BATCH, SEQ, D), 1.0),
        "c": nrm((BATCH, D), 1.0),
        "w_mod": nrm((DEPTH, D, 3 * D), 0.5 * D ** -0.5),
        "b_mod": nrm((DEPTH, 3 * D), 0.02),
        "pool_w_in": nrm((n_pool, D, 2 * BRANCH_W), D ** -0.5),
        "pool_w_grp": nrm((n_pool, N_POOL_GROUPS, POOL_GROUP_DIM, POOL_GROUP_DIM), POOL_GROUP_DIM ** -0.5),
        "pool_scale": gain((n_pool, BRANCH_W)),
        "pool_w_out": nrm((n_pool, BRANCH_W, D), BRANCH_W ** -0.5),
        "gla_w_in": nrm((n_gla, D, 2 * GLA_KEY_W + 2 * GLA_VAL_W), D ** -0.5),
        "gla_fwd_w1": nrm((n_gla, D, GLA_LOWRANK), D ** -0.5),
        "gla_fwd_w2": nrm((n_gla, GLA_LOWRANK, GLA_KEY_W), GLA_LOWRANK ** -0.5),
        "gla_fwd_b": nrm((n_gla, GLA_KEY_W), 0.1),
        "gla_bwd_w1": nrm((n_gla, D, GLA_LOWRANK), D ** -0.5),
        "gla_bwd_w2": nrm((n_gla, GLA_LOWRANK, GLA_KEY_W), GLA_LOWRANK ** -0.5),
        "gla_bwd_b": nrm((n_gla, GLA_KEY_W), 0.1),
        "gla_norm_g": gain((n_gla, GLA_DV)),
        "gla_w_out": nrm((n_gla, GLA_VAL_W, D), GLA_VAL_W ** -0.5),
        "attn_w_in": nrm((n_attn, D, 2 * ATTN_Q_W + 2 * ATTN_KV_W), D ** -0.5),
        "attn_q_norm_g": gain((n_attn, ATTN_HEAD_DIM)),
        "attn_k_norm_g": gain((n_attn, ATTN_HEAD_DIM)),
        "attn_w_out": nrm((n_attn, ATTN_Q_W, D), ATTN_Q_W ** -0.5),
        "final_norm_g": gain((D,)),
    }

def second_block(x, c, w_mod, b_mod, pool_w_in, pool_w_grp, pool_scale, pool_w_out,
              gla_w_in, gla_fwd_w1, gla_fwd_w2, gla_fwd_b, gla_bwd_w1, gla_bwd_w2, gla_bwd_b,
              gla_norm_g, gla_w_out, attn_w_in, attn_q_norm_g, attn_k_norm_g, attn_w_out,
              final_norm_g):
    for i in range(DEPTH):
        shift, scale, gate = ada_modulation(c, w_mod[i], b_mod[i])
        h = rms_norm_2(x) * (1.0 + scale) + shift
        kind, j = i % N_MIXERS, i // N_MIXERS
        if kind == 0:
            y = pool_mixer(h, pool_w_in[j], pool_w_grp[j], pool_scale[j], pool_w_out[j])
        elif kind == 1:
            y = gla_mixer(h, gla_w_in[j], gla_fwd_w1[j], gla_fwd_w2[j], gla_fwd_b[j],
                          gla_bwd_w1[j], gla_bwd_w2[j], gla_bwd_b[j], gla_norm_g[j], gla_w_out[j])
        else:
            y = attn_mixer(h, attn_w_in[j], attn_q_norm_g[j], attn_k_norm_g[j], attn_w_out[j])
        x = x + gate * y
    return rms_norm_2(x) * final_norm_g


def setup_inputs(seed=0):
    out = dict(first_inputs(seed))
    for name, value in second_inputs(seed + 1).items():
        if name != "x":
            out[name + "_2"] = value
    return out


def reference(
    x, c, positions, g_attn, g_ffn, w_ada, b_ada, w_in, g_qa, g_ka, g_mq_lat, w_mq_up,
    g_mkv_lat, w_mkv_up, g_qm, g_km, w_pa, w_pb, w_o, w_up, w_conv, b_conv, w_down, c_2,
    w_mod_2, b_mod_2, pool_w_in_2, pool_w_grp_2, pool_scale_2, pool_w_out_2, gla_w_in_2,
    gla_fwd_w1_2, gla_fwd_w2_2, gla_fwd_b_2, gla_bwd_w1_2, gla_bwd_w2_2, gla_bwd_b_2,
    gla_norm_g_2, gla_w_out_2, attn_w_in_2, attn_q_norm_g_2, attn_k_norm_g_2, attn_w_out_2,
    final_norm_g_2,
):
    x = first_block(
        x, c, positions, g_attn, g_ffn, w_ada, b_ada, w_in, g_qa, g_ka, g_mq_lat, w_mq_up,
        g_mkv_lat, w_mkv_up, g_qm, g_km, w_pa, w_pb, w_o, w_up, w_conv, b_conv, w_down,
    )
    return second_block(
        x, c_2, w_mod_2, b_mod_2, pool_w_in_2, pool_w_grp_2, pool_scale_2, pool_w_out_2,
        gla_w_in_2, gla_fwd_w1_2, gla_fwd_w2_2, gla_fwd_b_2, gla_bwd_w1_2, gla_bwd_w2_2,
        gla_bwd_b_2, gla_norm_g_2, gla_w_out_2, attn_w_in_2, attn_q_norm_g_2, attn_k_norm_g_2,
        attn_w_out_2, final_norm_g_2,
    )


_drawn_inputs = setup_inputs


def setup_inputs(seed=0):
    import zlib

    import numpy as np

    out = dict(_drawn_inputs(seed))
    spreads = {}
    factors = {'g_attn': 8.0,
     'g_ffn': 8.0,
     'b_ada': 5.739,
     'g_qa': 8.0,
     'g_ka': 8.0,
     'g_mq_lat': 8.0,
     'g_mkv_lat': 8.0,
     'g_qm': 8.0,
     'g_km': 8.0,
     'b_conv': 33.552,
     'b_mod_2': 19.59,
     'pool_scale_2': 25.824}
    for name, (base, spread) in spreads.items():
        noise = np.random.default_rng([zlib.crc32(name.encode()), seed]).standard_normal(out[name].shape)
        drawn = base * np.exp(spread * noise) if base else spread * noise
        out[name] = jnp.asarray(drawn.astype(out[name].dtype))
    for name, factor in factors.items():
        out[name] = (out[name] * factor).astype(out[name].dtype)
    return out
```

```python
from contextlib import ExitStack

import numpy as np

import concourse.bass as bass
from concourse import mybir

F32 = mybir.dt.float32
F32R = mybir.dt.float32r
I32 = mybir.dt.int32
ALU = mybir.AluOpType
ACT = mybir.ActivationFunctionType
AX = mybir.AxisListType.X

P = 128
D = 2048
S = 256
TOK = S // P
NC = 512
RAW, RING = 8, 4
D_FF = 5632
H, HD, ROT = 8, 128, 32
GROUPS = 2
IH, ID, IROT = 16, 64, 16
NOPE, MROT, MV = 128, 64, 128
MD = NOPE + MROT
QLORA, KVLORA = 512, 256
TOPK = 64
THETA = 500000.0
EPS = 1e-6
MASKED = -1e30
TAKEN = -3e38
WINDOWS = (2, 4, 8, 16)
TWO_PI = 6.283185307179586
PI_HI = 6.28125
PI_MID = float(np.float32(TWO_PI - PI_HI))
PI_LO = float(TWO_PI - PI_HI - PI_MID)
ROUND = 12582912.0

C_QA, C_KA, C_QI, C_KI, C_MQ, C_MKV, C_GATE = 0, 1024, 1536, 2560, 2640, 3152, 3472

PHASES = {}
_t = _c = 0
for _name, _n, _k in (("in", 7, 8), ("mq", 4, 2), ("mkv", 4, 1), ("gate", 8, 8), ("proj", 8, 4), ("wo", 4, 8),
                      ("up0", 8, 8), ("down0", 4, 8), ("up1", 8, 8), ("down1", 4, 8), ("up2", 6, 8), ("down2", 4, 6),
                      ("pin", 8, 8), ("grp", 4, 2), ("pout", 4, 8)):
    PHASES[_name] = (_t, _c, _n, _k)
    _t += _n * _k
    _c += _n
TILES = _t

V_GATTN, V_GFFN, V_SHA, V_SCA, V_SHF, V_SCF, V_SH2, V_SC2 = range(0, 128, 16)
V_PSCALE, V_GMQ, V_GMKV = 128, 144, 148
NVEC = 150

SH_A, SC_A, SH_F, SC_F, GT_A, GT_F, SH_2, SC_2, GT_2 = range(9)
REGION_SRC = [(0, 0), (0, 1), (0, 3), (0, 4), (0, 2), (0, 5), (1, 0), (1, 1), (1, 2)]


PAIRS = (4, 4, 3)
UPDATES = {"wo": 0, "down0": 4, "down1": 8, "down2": 12, "pout": 16}
PI_IN = 3.1415925

class Order:

    def __init__(self, eng, sem):
        self.eng, self.sem, self.base, self.n = eng, sem, 0, 0

    def link(self, ins):
        self.n += 1
        ins.then_inc(self.sem, 1)
        self.eng.wait_ge(self.sem, self.base + self.n)

    def enter(self, i, per):
        self.outer, self.per = self.base + self.n, per
        self.base, self.n = i * per + self.outer, 0

    def leave(self, trips):
        assert self.n == self.per, self.n
        self.base, self.n = self.outer + self.per * trips, 0


def build(nc, A, out):
    ctx = ExitStack()
    with ctx:
        def sb(name, shape, dt=F32, stack=ctx):
            return stack.enter_context(nc.sbuf_tensor(name, shape, dt))

        def sem(name):
            return ctx.enter_context(nc.semaphore(name))

        raw = sb("raw", [P, RAW, 2, NC])
        whi = sb("whi", [P, RING, 2, NC], F32R)
        wlo = sb("wlo", [P, RING, 2, NC], F32R)
        sa_hi = sb("sa_hi", [P, 16, S], F32R)
        sa_lo = sb("sa_lo", [P, 16, S], F32R)
        ada_ring = sb("ada_ring", [P, 2, D])
        ada_acc = sb("ada_acc", [P, D])
        vecs = sb("vecs", [P, NVEC])
        cvec = sb("cvec", [P, 4, 88])
        ident = sb("ident", [P, P])
        ones = sb("ones", [P, P])
        diag = sb("diag", [P, TOK, P])
        cact = sb("cact", [P, 2, 16])
        mod_s = sb("mod_s", [P, 16])
        mod_b = sb("mod_b", [P, 16])
        stat = sb("stat", [P, 2, TOK])
        ssq = sb("ssq", [P, TOK, 4])
        rstd = sb("rstd", [P, TOK])

        with ExitStack() as st:
            xs = sb("xs", [P, TOK, D], stack=st)
            start_ring = sb("start_ring", [P, 4, D], stack=st)
            vstage = sb("vstage", [P, 6, P], stack=st)
            craw = sb("craw", [P, 2, 16], stack=st)
            start_tmp = sb("start_tmp", [P, 2, 512], stack=st)
            sqdump = sb("sqdump", [P, D], stack=st)
        with ExitStack() as st:
            pq = sb("pq", [P, 2 * H, HD], stack=st)
            pkv = sb("pkv", [P, TOK, 512], stack=st)
            pm = sb("pm", [P, TOK, 400], stack=st)
            p2 = sb("p2", [P, 3072], stack=st)
            mkv = sb("mkv", [P, 2 * H, 256], stack=st)
            gains = sb("gains", [P, 640], stack=st)
            posf = sb("posf", [P, 2, TOK], stack=st)
            tabs = sb("tabs", [P, 2, TOK, 56], stack=st)
            causal = sb("causal", [P, TOK, S], stack=st)
            selbias = sb("selbias", [P, TOK, S], stack=st)
            kT = sb("kT", [P, GROUPS, S], stack=st)
            kbase = sb("kbase", [P, TOK, MROT], stack=st)
            hstat = sb("hstat", [P, 2, 56], stack=st)
            smax = sb("smax", [P, 2, 2, TOK], stack=st)
            with ExitStack() as prep:
                lat_hi = sb("lat_hi", [P, 6, S], F32R, stack=prep)
                lat_lo = sb("lat_lo", [P, 6, S], F32R, stack=prep)
                tmp = sb("tmp", [P, 3072], stack=prep)
                kirep = sb("kirep", [P, TOK, P], stack=prep)
                kiT = sb("kiT", [P, S], stack=prep)
                m8 = sb("m8", [P, 8], stack=prep)
            with ExitStack() as hd:
                gstage = sb("gstage", [P, 2, TOK, NC], stack=hd)
                qsA = sb("qsA", [P, TOK, HD], stack=hd)
                qsB = sb("qsB", [P, TOK, MD], stack=hd)
                ksB = sb("ksB", [P, TOK, MD], stack=hd)
                qTA = sb("qTA", [P, S], stack=hd)
                nT = sb("nT", [P, 2, S], stack=hd)
                rT = sb("rT", [P, 2, S], stack=hd)
                prA = sb("prA", [P, TOK, S], stack=hd)
                prB = sb("prB", [P, TOK, S], stack=hd)
                pTA = sb("pTA", [P, 384], stack=hd)
                pTB = sb("pTB", [P, 384], stack=hd)
                vA = sb("vA", [P, TOK, HD], stack=hd)
                vB = sb("vB", [P, TOK, MV], stack=hd)
        sb_hi = sb("sb_hi", [P, 16, S], F32R)
        sb_lo = sb("sb_lo", [P, 16, S], F32R)
        X = sb("X", [P, TOK, D])
        gt = sb("gt", [P, D])
        U = sb("U", [P, 2, TOK, NC])
        cv = sb("cv", [P, 8, S])
        gv = sb("gv", [P, 4, S])

        acc = [[ctx.enter_context(nc.psum_tensor(f"acc{a}{b}", [P, NC], F32)) for b in range(TOK)] for a in range(2)]
        M = [ctx.enter_context(nc.psum_tensor(f"misc{a}", [P, NC], F32)) for a in range(4)]
        gates_dram = nc.dram_tensor("gates_dram", (8, P, TOK, NC), F32, kind="Internal").ap()

        raw_landed = [sem(f"raw_landed{i}") for i in range(RAW)]
        hi_ready, lo_ready, tile_used, chunk_evac = sem("hi_ready"), sem("lo_ready"), sem("tile_used"), sem("chunk_evac")
        ada_landed = [sem(f"ada_landed{i}") for i in range(2)]
        start_landed = [sem(f"start_landed{i}") for i in range(4)]
        ada_used, region_summed, mod_ready, gt_ready = sem("ada_used"), sem("region_summed"), sem("mod_ready"), sem("gt_ready")
        consts_landed, vec_landed, x_landed, ones_ready = sem("consts_landed"), sem("vec_landed"), sem("x_landed"), sem("ones_ready")
        vec_turned, vec_ready, c_ready = sem("vec_turned"), sem("vec_ready"), sem("c_ready")
        ssq_cleared, xsq_done, ms_ready, sqrt_ready, diag_ready = (sem(n) for n in (
            "ssq_cleared", "xsq_done", "ms_ready", "sqrt_ready", "diag_ready"))
        nrm_turned, nrm_evac, nrm_hi, nrm_lo = sem("nrm_turned"), sem("nrm_evac"), sem("nrm_hi"), sem("nrm_lo")
        dve_order, att_landed, ang_ready, tab_ready = sem("dve_order"), sem("att_landed"), sem("ang_ready"), sem("tab_ready")
        qi_roped, qi_turned, qi_evac = sem("qi_roped"), sem("qi_turned"), sem("qi_evac")
        dots_ready, relu_ready, relu_used = sem("dots_ready"), sem("relu_ready"), sem("relu_used")
        k_normed, k_turned, k_evac = sem("k_normed"), sem("k_turned"), sem("k_evac")
        hs_ms, hs_sqrt, att_prepared = sem("hs_ms"), sem("hs_sqrt"), sem("att_prepared")
        q_staged, k_staged, head_turned, turned_act, turned_dve = (sem(n) for n in (
            "q_staged", "k_staged", "head_turned", "turned_act", "turned_dve"))
        logits_ready, maxedA, maxedB, expA, expB, probs_ready = (sem(n) for n in (
            "logits_ready", "maxedA", "maxedB", "expA", "expB", "probs_ready"))
        pT_ready, pTA_evac, pTB_evac, o_ready, oA_evac, oB_evac = (sem(n) for n in (
            "pT_ready", "pTA_evac", "pTB_evac", "o_ready", "oA_evac", "oB_evac"))
        gstage_free = [sem(f"gstage_free{i}") for i in range(2)]
        gate_loaded = [sem(f"gate_loaded{i}") for i in range(2)]
        o_hi, o_lo, res_landed, bias_landed = sem("o_hi"), sem("o_lo"), sem("res_landed"), sem("bias_landed")
        m_ready, m_turned, m_hi, m_lo, x_updated = (sem(n) for n in ("m_ready", "m_turned", "m_hi", "m_lo", "x_updated"))
        u_ready, u_turned, cv_based, cv_done, silu_done = (sem(n) for n in ("u_ready", "u_turned", "cv_based", "cv_done", "silu_done"))
        gv_ready, f_hi, f_lo = sem("gv_ready"), sem("f_hi"), sem("f_lo")
        pmat_landed, fg_landed, p_turned, p_hi, p_lo = (sem(n) for n in ("pmat_landed", "fg_landed", "p_turned", "p_hi", "p_lo"))
        y_turned, y_scaled, y_hi, y_lo, out_ready, out_stored = (sem(n) for n in (
            "y_turned", "y_scaled", "y_hi", "y_lo", "out_ready", "out_stored"))

        W = {n: A[n][0].rearrange("(k p) n -> p k n", p=P) for n in
             ("w_in", "w_mq_up", "w_mkv_up", "w_pa", "w_pb", "w_o", "w_up", "w_down", "pool_w_in_2", "pool_w_out_2")}
        w_grp = A["pool_w_grp_2"][0].rearrange("g (k p) n -> p g k n", p=P)
        ada_src = [A["w_ada"][0].rearrange("(p t) n -> p t n", t=16), A["w_mod_2"][0].rearrange("(p t) n -> p t n", t=16)]
        xv = A["x"][0].rearrange("(t p) n -> p t n", p=P)
        outv = out[0].rearrange("(t p) n -> p t n", p=P)
        qi = p2[:, 0:2048].rearrange("p (t h d) -> p t h d", t=TOK, h=IH)
        mql = p2[:, 2048:3072].rearrange("p (t d) -> p t d", t=TOK)
        mq = p2[:, :].rearrange("p (a d) -> p a d", d=MD)
        oTA = pq[:, :, :].rearrange("p (h t) d -> p h (t d)", t=TOK)
        oTB = p2[:, :].rearrange("p (h x) -> p h x", h=H)
        qiT = mkv
        merged = cv[:, 0:4, :].rearrange("p a n -> p (a n)").rearrange("p (t n) -> p t n", t=TOK)
        gv2 = gv[:, :, :].rearrange("p a n -> p (a n)").rearrange("p (t n) -> p t n", t=TOK)
        fgain = cv[:, :, :].rearrange("p a n -> p (a n)")
        lat_tmp = tmp[:, 0:1024].rearrange("p (a n) -> p a n", a=2)

        def bank2(m):
            return m[:, :].rearrange("p (a n) -> p a n", a=2)

        block = ctx.enter_context(nc.Block())

        @block.sync
        def _(sp):
            def tile_in(tb, off, src):
                if tb >= RAW:
                    sp.wait_ge(lo_ready, tb - RAW + 1 + off)
                sp.dma_start(raw[:, tb % RAW, :, :], src).then_inc(raw_landed[tb % RAW], 16)

            sp.dma_start(craw[:, 0, :], A["c"][0].rearrange("(p t) -> p t", t=16)).then_inc(consts_landed, 16)
            sp.dma_start(craw[:, 1, :], A["c_2"][0].rearrange("(p t) -> p t", t=16)).then_inc(consts_landed, 16)
            for j in range(4):
                sp.dma_start(start_ring[:, j, :], ada_src[0][:, j, 0:D]).then_inc(start_landed[j], 16)
            sp.dma_start(ident[:, :], A["identity"]).then_inc(vec_landed, 16)
            for v, name, lo, n in ((V_GATTN, "g_attn", 0, 16), (V_GFFN, "g_ffn", 0, 16), (V_SHA, "b_ada", 0, 32),
                                   (V_SHF, "b_ada", 3 * D, 32), (V_SH2, "b_mod_2", 0, 32)):
                sp.dma_start(vstage[v:v + n, 0, :],
                             A[name][0, lo:lo + n * P].rearrange("(a b) -> a b", b=P)).then_inc(vec_landed, 16)
            for v, name, n in ((0, "pool_scale_2", 16), (16, "g_mq_lat", 4), (20, "g_mkv_lat", 2)):
                sp.dma_start(vstage[v:v + n, 1, :], A[name][0].rearrange("(a b) -> a b", b=P)).then_inc(vec_landed, 16)
            for j in range(3):
                sp.dma_start(vstage[0:88, 2 + j, :], A["w_conv"][0, j].rearrange("(a b) -> a b", b=P)).then_inc(vec_landed, 16)
            sp.dma_start(vstage[0:88, 5, :], A["b_conv"][0].rearrange("(a b) -> a b", b=P)).then_inc(vec_landed, 16)
            sp.dma_start(xs[:, :, :], xv).then_inc(x_landed, 16)
            for first, trips, lo in ((4, 3, 0), (16, 4, D)):
                with sp.Fori(0, trips) as i:
                    for j in range(4):
                        sp.wait_ge(ada_used, i * 4 + (first + j - 3))
                        sp.dma_start(start_ring[:, j, :],
                                     ada_src[0][:, bass.ds(i * 4 + (first % 16 + j), 1), lo:lo + D]
                                     .rearrange("p a n -> p (a n)")).then_inc(start_landed[j], 16)

            cols = [None, C_QI, C_QI + NC, C_MQ, C_KA, C_QA, C_QA + NC]
            t = 0
            for c in range(7):
                for k in range(8):
                    wk = W["w_in"][:, 2 * k:2 * k + 2, :]
                    if c:
                        tile_in(t, 0, wk[:, :, cols[c]:cols[c] + NC])
                    else:
                        sp.dma_start(raw[:, t, :, 0:432], wk[:, :, C_GATE - 432:C_GATE]).then_inc(raw_landed[t], 16)
                        sp.dma_start(raw[:, t, :, 432:512], wk[:, :, C_KI:C_KI + 80]).then_inc(raw_landed[t], 16)
                    t += 1
            for c in range(4):
                lo = min(2 * MD * c, 8 * MD - NC)
                for k in range(2):
                    tile_in(t, 0, W["w_mq_up"][:, 2 * k:2 * k + 2, lo:lo + NC])
                    t += 1
            for c in range(4):
                tile_in(t, 0, W["w_mkv_up"][:, 0:2, c * NC:(c + 1) * NC])
                t += 1

            def cut(w, j, c, base=0, first=0):
                return w[:, first + 2 * j:first + 2 * j + 2, bass.ds(c * NC + base, NC)]

            def stream(name, w, base=0, first=0):
                t0, _, n, k = PHASES[name]
                assert k == 8
                with sp.Fori(0, n) as i:
                    for j in range(8):
                        tile_in(t0 + j, i * 8, cut(w, j, i, base, first))

            stream("gate", W["w_in"], C_GATE)
            with sp.Fori(0, 4) as i:
                for j in range(8):
                    tile_in(PHASES["proj"][0] + j, i * 8, cut(W["w_pa"] if j < 4 else W["w_pb"], j % 4, i))
            stream("wo", W["w_o"])
            for part, pairs in enumerate(PAIRS):
                with sp.Fori(0, pairs) as i:
                    for j in range(16):
                        tile_in(PHASES[f"up{part}"][0] + j, i * 16,
                                cut(W["w_up"], j % 8, i, 4 * part * NC + (D_FF if j >= 8 else 0)))
                if part < 2:
                    stream(f"down{part}", W["w_down"], 0, 16 * part)
            t = PHASES["down2"][0]
            for c in range(4):
                for j in range(6):
                    tile_in(t, 0, W["w_down"][:, 32 + 2 * j:34 + 2 * j, c * NC:(c + 1) * NC])
                    t += 1
            stream("pin", W["pool_w_in_2"])
            t = PHASES["grp"][0]
            for g in range(4):
                for j in range(2):
                    tile_in(t, 0, w_grp[:, g, 2 * j:2 * j + 2, :])
                    t += 1
            stream("pout", W["pool_w_out_2"])
            for tk in range(TOK):
                sp.wait_ge(out_ready, tk + 1)
                sp.dma_start(outv[:, tk, :], X[:, tk, :]).then_inc(out_stored, 16)
            sp.wait_ge(out_stored, 16 * TOK)

        @block.gpsimd
        def _(pool):
            nc.gpsimd.memset(ones[:, :], 1.0).then_inc(ones_ready, 1)

            def ada_in(n, off=0):
                src, reg = REGION_SRC[n // 16]
                if n >= 34:
                    pool.wait_ge(ada_used, n - 1 + off)
                tile = ada_src[src][:, bass.ds(off + n % 16, 1), reg * D:(reg + 1) * D].rearrange("p a n -> p (a n)")
                pool.dma_start(ada_ring[:, n % 2, :], tile).then_inc(ada_landed[n % 2], 16)

            ada_in(32)
            ada_in(33)
            pool.wait_ge(nrm_lo, 8)
            pool.dma_start(causal[:, :, :], A["causal"]).then_inc(att_landed, 16)
            col = 0
            for name, n in (("g_qa", HD), ("g_ka", HD), ("g_qm", MD), ("g_km", MD)):
                pool.dma_start(gains[:, col:col + n], A[name].broadcast_to([P, n])).then_inc(att_landed, 16)
                col += n
            pool.dma_start(posf[:, 0, :].bitcast(I32), A["positions"].rearrange("a (t p) -> p (a t)", p=P),
                           allow_slow_non_contiguous=True).then_inc(att_landed, 16)
            pool.dma_start(tabs[:, 1, 0, :], A["inv_freq"].broadcast_to([P, 56])).then_inc(att_landed, 16)
            for n in range(34, 48):
                ada_in(n)
            with pool.Fori(0, 8) as i:
                for j in range(2):
                    ada_in(48 + j, i * 2)
            pool.wait_ge(o_lo, 4)
            for g in gstage_free:
                pool.wait_ge(g, 16 * 5)
            pool.dma_start(U[:, 0, :, :], gates_dram[0]).then_inc(gate_loaded[0], 16)
            pool.dma_start(U[:, 1, :, :], gates_dram[4]).then_inc(gate_loaded[1], 16)
            pool.dma_start(gt[:, :], A["b_ada"][:, 2 * D:3 * D].broadcast_to([P, D])).then_inc(bias_landed, 16)
            pool.dma_start(X[:, :, :], xv).then_inc(res_landed, 16)
            _, c0, _, _ = PHASES["proj"]
            with pool.Fori(0, 3) as i:
                for cc in range(2):
                    for j in range(2):
                        ada_in(64 + 2 * cc + j, i * 4)
                    pool.wait_ge(chunk_evac, i * 2 + (c0 + cc + 1))
                    pool.dma_start(U[:, cc, :, :], gates_dram[bass.ds(i + (4 * cc + 1), 1), :, :, :]
                                   .rearrange("a p t n -> p (a t) n")).then_inc(gate_loaded[cc], 16)
            for n in range(76, 80):
                ada_in(n)
            pool.wait_ge(x_updated, 4)
            pool.dma_start(gt[:, :], A["b_ada"][:, 5 * D:6 * D].broadcast_to([P, D])).then_inc(bias_landed, 16)
            for r in (GT_F, SH_2, SC_2, GT_2):
                with pool.Fori(0, 8) as i:
                    for j in range(2):
                        ada_in(16 * r + j, i * 2)
            pool.wait_ge(f_lo, sum(PAIRS))
            pool.dma_start(cv[:, :, :], A["pool_matrix"]).then_inc(pmat_landed, 16)
            pool.wait_ge(x_updated, 16)
            pool.dma_start(gt[:, :], A["b_mod_2"][:, 2 * D:3 * D].broadcast_to([P, D])).then_inc(bias_landed, 16)
            pool.wait_ge(p_turned, 8)
            pool.dma_start(fgain, A["final_norm_g_2"].rearrange("(a n) -> a n", a=1).broadcast_to([P, D])).then_inc(fg_landed, 16)

        @block.scalar
        def _(act):
            def split(tb, off=0):
                if tb >= TILES:
                    return
                act.wait_ge(raw_landed[tb % RAW], 16 * (tb // RAW + 2) + off * 2)
                if tb >= RING:
                    act.wait_ge(tile_used, tb - RING + 1 + off)
                nc.scalar.copy(whi[:, tb % RING, :, :], raw[:, tb % RAW, :, :]).then_inc(hi_ready, 1)

            norms = [0]

            def sqrt_of_norm():
                norms[0] += 1
                act.wait_ge(ms_ready, norms[0])
                nc.scalar.activation(stat[:, 1, :], stat[:, 0, :], ACT.Sqrt).then_inc(sqrt_ready, 1)

            pairs = [0]

            def norm_hi(tmpv, hi, k0, npair):
                for b in range(npair):
                    act.wait_ge(nrm_evac, pairs[0] + 1)
                    nc.scalar.copy(hi[:, k0 + 2 * b:k0 + 2 * b + 2, :].rearrange("p a n -> p (a n)"),
                                   tmpv[:, pairs[0] % 2, :]).then_inc(nrm_hi, 1)
                    pairs[0] += 1

            def chunk_of(name, c, i=0, per=1):
                t0, c0, _, k = PHASES[name]
                act.wait_ge(tile_used, i * (per * k) + (t0 + (c + 1) * k))
                return acc[(c0 + c) % 2]

            act.wait_ge(consts_landed, 32)
            nc.scalar.activation(cact[:, :, :], craw[:, :, :], ACT.Silu).then_inc(c_ready, 1)
            act.wait_ge(x_landed, 16)
            act.wait_ge(ssq_cleared, 1)
            for t in range(TOK):
                if t:
                    act.wait_ge(xsq_done, t)
                nc.scalar.activation(sqdump[:, :], xs[:, t, :], ACT.Square, accum_out=ssq[:, t, 0:1]).then_inc(xsq_done, 1)
            sqrt_of_norm()
            for t in range(RING):
                split(t)
            norm_hi(start_tmp, sa_hi, 0, 8)

            for c in range(7):
                for j in range(8):
                    split(8 * c + j + RING)
                pair = chunk_of("in", c)
                for t in range(TOK):
                    ps = pair[t][:, :]
                    if c == 0:
                        dst, ps = pm[:, t, :], pair[t][:, 112:512]
                    elif c < 3:
                        dst, ps = qi[:, t, 8 * (c - 1):8 * c, :], ps.rearrange("p (h d) -> p h d", d=ID)
                    elif c == 3:
                        dst = mql[:, t, :]
                    elif c == 4:
                        dst = pkv[:, t, :]
                    else:
                        dst = pq[:, :, :].rearrange("p (h t) d -> p t h d", t=TOK)[:, t, 4 * (c - 5):4 * (c - 4), :]
                        ps = ps.rearrange("p (h d) -> p h d", d=HD)
                    last = nc.scalar.copy(dst, ps)
                last.then_inc(chunk_evac, 1)
                if c == 0:
                    act.wait_ge(ang_ready, 1)
                    nc.scalar.activation(tabs[:, :, :, :], tabs[:, :, :, :], ACT.Sin).then_inc(tab_ready, 1)

            for b in range(4):
                act.wait_ge(qi_turned, b + 1)
                nc.scalar.copy(qiT[:, 2 * b:2 * b + 2, :].rearrange("p a n -> p (a n)"), M[b][:, :]).then_inc(qi_evac, 1)
            act.wait_ge(qi_turned, 5)
            nc.scalar.copy(kiT[:, :], M[0][:, 0:S]).then_inc(qi_evac, 1)
            sqrt_of_norm()
            norm_hi(lat_tmp, lat_hi, 0, 2)
            sqrt_of_norm()
            norm_hi(lat_tmp, lat_hi, 4, 1)
            for h in range(IH):
                act.wait_ge(dots_ready, h + 1)
                if h >= 4:
                    act.wait_ge(relu_used, h - 3)
                nc.scalar.activation(tmp[:, 1024 + 512 * (h % 4):1536 + 512 * (h % 4)], M[h % 4][:, :],
                                     ACT.Relu).then_inc(relu_ready, 1)
            act.wait_ge(hs_ms, 1)
            nc.scalar.activation(hstat[:, 1, 0:4], hstat[:, 0, 0:4], ACT.Sqrt).then_inc(hs_sqrt, 1)
            act.wait_ge(k_turned, 1)
            nc.scalar.copy(kT[:, :, :].rearrange("p a n -> p (a n)"), M[0][:, :]).then_inc(k_evac, 1)

            t0 = PHASES["mq"][0]
            for c in range(4):
                for j in range(2):
                    split(t0 + 2 * c + j + RING)
                pair = chunk_of("mq", c)
                skip = 2 * MD * c - min(2 * MD * c, 8 * MD - NC)
                for t in range(TOK):
                    last = nc.scalar.copy(mq[:, :, :].rearrange("p (h t) d -> p t h d", t=TOK)[:, t, 2 * c:2 * c + 2, :],
                                          pair[t][:, skip:skip + 2 * MD].rearrange("p (h d) -> p h d", d=MD))
                last.then_inc(chunk_evac, 1)
            t0 = PHASES["mkv"][0]
            for c in range(4):
                split(t0 + c + RING)
                pair = chunk_of("mkv", c)
                for t in range(TOK):
                    last = nc.scalar.copy(mkv[:, :, :].rearrange("p (h t) d -> p t h d", t=TOK)[:, t, 2 * c:2 * c + 2, :],
                                          pair[t][:, :].rearrange("p (h d) -> p h d", d=256))
                last.then_inc(chunk_evac, 1)
            for i, lo in enumerate((4, 20, 36)):
                act.wait_ge(hs_ms, 2 + i)
                nc.scalar.activation(hstat[:, 1, lo:lo + 16], hstat[:, 0, lo:lo + 16], ACT.Sqrt).then_inc(hs_sqrt, 1)
            act.wait_ge(att_prepared, 1)

            t0, c0, _, _ = PHASES["gate"]
            for free in gstage_free:
                act.sem_inc(free, 16)
            for g in range(GROUPS):
                with act.Fori(0, 2) as i:
                    for cc in range(2):
                        tb, off, h = t0 + 32 * g + 8 * cc + RING, i * 16, i * 2 + (4 * g + cc)
                        split(tb, off)
                        nc.scalar.copy(qsA[:, :, :], pq[:, bass.ds(h * 2, 2), :])
                        nc.scalar.copy(qsB[:, :, :], mq[:, bass.ds(h * 2, 2), :])
                        nc.scalar.copy(vA[:, :, :], pkv[:, :, 256 + g * HD:256 + (g + 1) * HD])
                        nc.scalar.copy(vB[:, :, :], mkv[:, bass.ds(h * 2, 2), NOPE:NOPE + MV]).then_inc(q_staged, 1)
                        split(tb + 1, off)
                        act.wait_ge(head_turned, h + 1)
                        nc.scalar.copy(qTA[:, :], M[0][:, 0:S])
                        nc.scalar.copy(nT[:, :, :].rearrange("p a n -> p (a n)"), M[2][:, :]).then_inc(turned_act, 1)
                        split(tb + 2, off)
                        split(tb + 3, off)
                        for b, (maxed, pr, done) in enumerate(((maxedA, prA, expA), (maxedB, prB, expB))):
                            act.wait_ge(maxed, h + 1)
                            nc.scalar.activation(pr[:, 0, :], pr[:, 0, :], ACT.Exp, bias=smax[:, b, 0, 0:1],
                                                 accum_out=smax[:, b, 1, 0:1])
                            nc.scalar.activation(pr[:, 1, :], pr[:, 1, :], ACT.Exp, bias=smax[:, b, 0, 1:2],
                                                 accum_out=smax[:, b, 1, 1:2]).then_inc(done, 1)
                        split(tb + 4, off)
                        act.wait_ge(pT_ready, h * 2 + 1)
                        nc.scalar.copy(pTA[:, :], M[0][:, 0:384]).then_inc(pTA_evac, 1)
                        split(tb + 5, off)
                        split(tb + 6, off)
                        split(tb + 7, off)
                        act.wait_ge(o_ready, h * 2 + 1)
                        nc.scalar.copy(oTA[:, bass.ds(h, 1), :].rearrange("p a n -> p (a n)"), M[1][:, 0:S]).then_inc(oA_evac, 1)
                        pair = chunk_of("gate", 4 * g + cc, i, 2)
                        act.wait_ge(gstage_free[cc], i * 16 + (32 * g + 16))
                        for t in range(TOK):
                            last = nc.scalar.activation(gstage[:, cc, t, :], pair[t][:, :], ACT.Sigmoid)
                        last.then_inc(chunk_evac, 1)
                        act.wait_ge(chunk_evac, i * 2 + (c0 + 4 * g + cc + 1))
                        act.dma_start(gates_dram[bass.ds(h, 1), :, :, :].rearrange("a p t n -> p (a t) n"),
                                      gstage[:, cc, :, :]).then_inc(gstage_free[cc], 16)

            act.wait_ge(oB_evac, H)
            act.wait_ge(oA_evac, H)
            for b in range(2):
                nc.scalar.copy(sa_hi[:, 4 * b:4 * b + 4, :], oTA[:, 4 * b:4 * b + 4, :]).then_inc(o_hi, 1)
            for b in range(2):
                nc.scalar.copy(sa_hi[:, 8 + 4 * b:12 + 4 * b, :], oTB[:, 4 * b:4 * b + 4, 0:S]).then_inc(o_hi, 1)

            def merged_hi(n):
                for q in range(2):
                    act.wait_ge(m_turned, n * 2 + (q + 1))
                    nc.scalar.copy(sb_hi[:, bass.ds(n * 4 + 2 * q, 2), :], bank2(M[q])).then_inc(m_hi, 1)

            t0 = PHASES["proj"][0] + RING
            for j in range(8):
                split(t0 + j)
            with act.Fori(0, 3) as i:
                for j in range(8):
                    split(t0 + 8 + j, i * 8)
                    if j == 3:
                        merged_hi(i)
            merged_hi(3)

            def squares(name, c, i=0):
                act.wait_ge(x_updated, i * 2 + (UPDATES[name] + c + 1))
                for t in range(TOK):
                    last = nc.scalar.activation(U[:, 0, t, :], X[:, t, bass.ds(i * 2 * NC + c * NC, NC)], ACT.Square,
                                                accum_out=ssq[:, t, bass.ds(i * 2 + c, 1)])
                last.then_inc(xsq_done, 1)

            def out_product(name, square):
                t0, _, _, k = PHASES[name]
                with act.Fori(0, 2) as i:
                    for c in range(2):
                        for j in range(8):
                            split(t0 + 8 * c + j + RING, i * 16)
                        if square:
                            squares(name, c, i)

            out_product("wo", True)
            sqrt_of_norm()
            norm_hi(gv2, sa_hi, 0, 8)

            def conv_base(side, pg):
                for q in range(2):
                    act.wait_ge(u_turned, pg * 4 + (2 * side + q + 1))
                    for b in range(2):
                        col = pg * 4 + (44 * side + 2 * q + b)
                        last = nc.scalar.activation(cv[:, 4 * side + 2 * q + b, :], M[2 * side + q][:, b * S:(b + 1) * S],
                                                    ACT.Identity, bias=cvec[:, 3, bass.ds(col, 1)], scale=cvec[:, 2, bass.ds(col, 1)])
                last.then_inc(cv_based, 1)

            def ffn_hi(pg, pl):
                act.wait_ge(gv_ready, pg + 1)
                nc.scalar.copy(sb_hi[:, bass.ds(pl * 4, 4), :], gv[:, :, :]).then_inc(f_hi, 1)

            def up_pair(part, i, shift, first):
                t0 = PHASES[f"up{part}"][0] + 16 * shift
                off = i * 16
                pl = i + shift
                pg = i + (shift + 4 * part)
                for j in range(4):
                    split(t0 + RING + j, off)
                if not first:
                    conv_base(1, i + (shift + 4 * part - 1))
                split(t0 + RING + 4, off)
                split(t0 + RING + 5, off)
                if not first:
                    ffn_hi(i + (shift + 4 * part - 1), i + (shift - 1))
                split(t0 + RING + 6, off)
                split(t0 + RING + 7, off)
                pair = chunk_of(f"up{part}", 2 * shift, i, 2)
                for t in range(TOK):
                    last = nc.scalar.copy(U[:, 0, t, :], pair[t][:, :])
                last.then_inc(chunk_evac, 1)
                for j in range(4):
                    split(t0 + RING + 8 + j, off)
                conv_base(0, pg)
                split(t0 + RING + 12, off)
                split(t0 + RING + 13, off)
                act.wait_ge(cv_done, pg * 2 + 1)
                nc.scalar.activation(cv[:, 0:4, :], cv[:, 0:4, :], ACT.Silu).then_inc(silu_done, 1)
                split(t0 + RING + 14, off)
                split(t0 + RING + 15, off)
                pair = chunk_of(f"up{part}", 2 * shift + 1, i, 2)
                for t in range(TOK):
                    last = nc.scalar.copy(U[:, 1, t, :], pair[t][:, :])
                last.then_inc(chunk_evac, 1)

            for part, n in enumerate(PAIRS):
                up_pair(part, 0, 0, True)
                with act.Fori(0, n - 1) as i:
                    up_pair(part, i, 1, False)
                conv_base(1, 4 * part + n - 1)
                ffn_hi(4 * part + n - 1, n - 1)
                if part < 2:
                    out_product(f"down{part}", False)
            t0 = PHASES["down2"][0]
            for c in range(4):
                for j in range(6):
                    split(t0 + 6 * c + j + RING)
                squares("down2", c)

            sqrt_of_norm()
            norm_hi(gv2, sa_hi, 0, 8)

            def pooled_hi(c):
                for q in range(2):
                    act.wait_ge(p_turned, 2 * c + q + 1)
                    nc.scalar.copy(sb_hi[:, 4 * c + 2 * q:4 * c + 2 * q + 2, :], bank2(M[2 * (c % 2) + q])).then_inc(p_hi, 1)

            t0 = PHASES["pin"][0] + RING
            for c in range(4):
                for j in range(4):
                    split(t0 + 8 * c + j)
                if c:
                    pooled_hi(c - 1)
                for j in range(4, 8):
                    split(t0 + 8 * c + j)
                pair = chunk_of("pin", c)
                for t in range(TOK):
                    last = nc.scalar.copy(U[:, c % 2, t, :], pair[t][:, :])
                last.then_inc(chunk_evac, 1)
            pooled_hi(3)
            act.wait_ge(ada_used, 144)
            with act.Fori(0, 2) as i:
                for cc in range(2):
                    for j in range(8):
                        split(t0 + 32 + 8 * cc + j, i * 16)
                    pair = chunk_of("pin", 4 + cc, i, 2)
                    for t in range(TOK):
                        last = nc.scalar.activation(ada_ring[:, t, bass.ds(i * 2 * NC + cc * NC, NC)], pair[t][:, :], ACT.Silu)
                    last.then_inc(chunk_evac, 1)
            t0 = PHASES["grp"][0] + RING
            for g in range(4):
                split(t0 + 2 * g)
                split(t0 + 2 * g + 1)
                act.wait_ge(y_scaled, g + 1)
                nc.scalar.copy(sa_hi[:, 4 * g:4 * g + 4, :], gv[:, :, :]).then_inc(y_hi, 1)
            t0 = PHASES["pout"][0] + RING
            for c in range(4):
                for j in range(8):
                    split(t0 + 8 * c + j)
                squares("pout", c)
            sqrt_of_norm()

        @block.vector
        def _(dve):
            V = nc.vector
            order = Order(dve, dve_order)
            link = order.link

            def split(tb, off=0):
                if tb >= TILES:
                    return
                dve.wait_ge(hi_ready, tb + 1 + off)
                V.tensor_tensor(wlo[:, tb % RING, :, :], raw[:, tb % RAW, :, :], whi[:, tb % RING, :, :].bitcast(F32),
                                ALU.subtract).then_inc(lo_ready, 1)

            def ada_begin(r):
                if r:
                    dve.wait_ge(region_summed, r)
                link(V.memset(ada_acc[:, :], 0.0))

            def ada(n, off=0):
                src = REGION_SRC[n // 16][0]
                if n < 32:
                    dve.wait_ge(start_landed[n % 4], 16 * (n // 4 + 1) + off * 4)
                    tile = start_ring[:, n % 4, :]
                else:
                    dve.wait_ge(ada_landed[n % 2], 16 * ((n - 32) // 2 + 1) + off * 8)
                    tile = ada_ring[:, n % 2, :]
                if n:
                    dve.wait_ge(ada_used, n + off)
                V.scalar_tensor_tensor(out=ada_acc[:, :], in0=tile, scalar=cact[:, src, bass.ds(off + n % 16, 1)],
                                       in1=ada_acc[:, :], op0=ALU.mult, op1=ALU.add).then_inc(ada_used, 1)

            def shift_ready(r, v):
                dve.wait_ge(region_summed, r + 1)
                V.tensor_tensor(mod_b[:, :], M[0][:, 0:16], vecs[:, v:v + 16], ALU.add).then_inc(mod_ready, 1)

            def scale_ready(r, v, gain=None):
                dve.wait_ge(region_summed, r + 1)
                last = V.scalar_tensor_tensor(out=mod_s[:, :], in0=M[0][:, 0:16], scalar=1.0, in1=vecs[:, v:v + 16],
                                              op0=ALU.add, op1=ALU.add)
                if gain is not None:
                    link(last)
                    last = V.tensor_tensor(mod_s[:, :], mod_s[:, :], vecs[:, gain:gain + 16], ALU.mult)
                last.then_inc(mod_ready, 1)

            def gate_ready(r, k):
                dve.wait_ge(bias_landed, 16 * k)
                dve.wait_ge(region_summed, r + 1)
                for n in range(4):
                    last = V.tensor_tensor(gt[:, n * NC:(n + 1) * NC], M[n][:, :], gt[:, n * NC:(n + 1) * NC], ALU.add)
                last.then_inc(gt_ready, 1)

            norms = [0]

            def norm_of(sumsq, width, with_diag=True):
                V.tensor_scalar(stat[:, 0, :], sumsq, 1.0 / width, EPS, ALU.mult, ALU.add).then_inc(ms_ready, 1)
                norms[0] += 1
                dve.wait_ge(sqrt_ready, norms[0])
                link(V.reciprocal(rstd[:, :], stat[:, 1, :]))
                if with_diag:
                    for t in range(TOK):
                        last = V.tensor_scalar(diag[:, t, :], ident[:, :], rstd[:, t:t + 1], None, ALU.mult)
                    last.then_inc(diag_ready, 1)

            def norm_x(squares, with_diag=True):
                dve.wait_ge(xsq_done, squares)
                link(V.reduce_sum(rstd[:, :], ssq[:, :, :], AX))
                norm_of(rstd[:, :], D, with_diag)

            pairs = [0]

            def norm_lo(tmpv, hi, lo, k0, npair, scale, bias):
                def low(b, p):
                    dve.wait_ge(nrm_hi, p + 1)
                    V.tensor_tensor(lo[:, k0 + 2 * b:k0 + 2 * b + 2, :].rearrange("p a n -> p (a n)"), tmpv[:, p % 2, :],
                                    hi[:, k0 + 2 * b:k0 + 2 * b + 2, :].rearrange("p a n -> p (a n)").bitcast(F32),
                                    ALU.subtract).then_inc(nrm_lo, 1)

                p0 = pairs[0]
                for b in range(npair):
                    p = p0 + b
                    dve.wait_ge(nrm_turned, p + 1)
                    if b >= 2:
                        dve.wait_ge(nrm_lo, p - 1)
                    for kk in range(2):
                        k = 2 * b + kk
                        if bias is None:
                            last = V.tensor_scalar(tmpv[:, p % 2, kk * S:(kk + 1) * S], M[b % 4][:, kk * S:(kk + 1) * S],
                                                   scale[:, k:k + 1], None, ALU.mult)
                        else:
                            last = V.tensor_scalar(tmpv[:, p % 2, kk * S:(kk + 1) * S], M[b % 4][:, kk * S:(kk + 1) * S],
                                                   scale[:, k:k + 1], bias[:, k:k + 1], ALU.mult, ALU.add)
                    last.then_inc(nrm_evac, 1)
                    if b:
                        low(b - 1, p - 1)
                low(npair - 1, p0 + npair - 1)
                pairs[0] += npair
                dve.wait_ge(nrm_lo, pairs[0])

            V.memset(ssq[:, :, :], 0.0).then_inc(ssq_cleared, 1)
            ada_begin(0)
            dve.wait_ge(c_ready, 1)
            ada(0)
            ada(1)
            ada(2)
            ada(3)
            with dve.Fori(0, 3) as i:
                for j in range(4):
                    ada(4 + j, i * 4)
            dve.wait_ge(vec_turned, 1)
            V.tensor_copy(vecs[:, :], M[1][:, 0:NVEC]).then_inc(vec_ready, 1)
            dve.wait_ge(vec_turned, 2)
            V.tensor_copy(cvec[:, :, :].rearrange("p a n -> p (a n)"), M[2][:, 0:352]).then_inc(vec_ready, 1)
            dve.wait_ge(vec_ready, 2)
            shift_ready(SH_A, V_SHA)
            ada_begin(1)
            with dve.Fori(0, 4) as i:
                for j in range(4):
                    ada(16 + j, i * 4)
            norm_x(TOK)
            scale_ready(SC_A, V_SCA, V_GATTN)
            dve.wait_ge(mod_ready, 2)
            for t in range(RING):
                split(t)
            norm_lo(start_tmp, sa_hi, sa_lo, 0, 8, mod_s, mod_b)

            ada_begin(2)
            for j in range(8):
                split(RING + j)
            ada(32)
            ada(33)
            dve.wait_ge(att_landed, 16 * 7)
            link(V.tensor_copy(posf[:, 1, :], posf[:, 0, :].bitcast(I32)))
            for t in range(TOK):
                last = V.tensor_scalar(tabs[:, 0, t, :], tabs[:, 1, 0, :], posf[:, 1, t:t + 1], None, ALU.mult)
            link(last)
            link(V.tensor_copy(tabs[:, 1, :, :], tabs[:, 0, :, :]))
            kv = tmp[:, 0:224].rearrange("p (a t n) -> p a t n", a=2, t=TOK)
            for a, turn in ((0, 0.25), (1, 0.0)):
                link(V.tensor_scalar(kv[:, a], tabs[:, a, :, :], 1.0 / TWO_PI, turn, ALU.mult, ALU.add))
            link(V.tensor_scalar(kv, kv, ROUND, None, ALU.add))
            link(V.tensor_scalar(kv, kv, ROUND, None, ALU.subtract))
            flat = tabs[:, :, :, :].rearrange("p a t n -> p (a t n)")
            for part in (PI_HI, PI_MID, PI_LO):
                link(V.scalar_tensor_tensor(out=flat, in0=tmp[:, 0:224], scalar=-part, in1=flat, op0=ALU.mult, op1=ALU.add))
            link(V.tensor_scalar(tabs[:, 0, :, :], tabs[:, 0, :, :], TWO_PI / 4, None, ALU.add))
            V.tensor_scalar(flat, flat, PI_IN, -PI_IN, ALU.min, ALU.max).then_inc(ang_ready, 1)
            with dve.Fori(0, 3) as i:
                for cc in range(2):
                    for j in range(8):
                        split(8 + 8 * cc + RING + j, i * 16)
                    ada(34 + 2 * cc, i * 4)
                    ada(35 + 2 * cc, i * 4)
            ada(46)
            ada(47)
            shift_ready(SH_F, V_SHF)

            def rope(v, tab, half, tmpv, axis, shape, done=None):
                co, si = (tabs[:, a, :, tab:tab + half].unsqueeze(axis).broadcast_to([P, *shape, half]) for a in range(2))
                n = shape[0] * shape[1] * half
                a, b, c, d = (tmpv[:, k * n:(k + 1) * n].rearrange("p (x y n) -> p x y n", x=shape[0], y=shape[1]) for k in range(4))
                v1, v2 = v[:, :, :, 0:half], v[:, :, :, half:2 * half]
                V.tensor_tensor(a, v1, co, ALU.mult)
                V.tensor_tensor(b, v2, si, ALU.mult)
                V.tensor_tensor(c, v2, co, ALU.mult)
                link(V.tensor_tensor(d, v1, si, ALU.mult))
                V.tensor_tensor(v1, a, b, ALU.subtract)
                last = V.tensor_tensor(v2, c, d, ALU.add)
                if done is None:
                    link(last)
                else:
                    last.then_inc(done, 1)

            def sum_squares(v, dst, width):
                sq = tmp[:, 0:v.shape[1] * width].rearrange("p (a n) -> p a n", n=width)
                link(V.tensor_tensor(sq, v, v, ALU.mult))
                link(V.reduce_sum(dst, sq, AX))

            hs = [0]

            def head_rstd(lo, n, width):
                V.tensor_scalar(hstat[:, 0, lo:lo + n], hstat[:, 0, lo:lo + n], 1.0 / width, EPS, ALU.mult, ALU.add).then_inc(hs_ms, 1)
                hs[0] += 1
                dve.wait_ge(hs_sqrt, hs[0])
                link(V.reciprocal(hstat[:, 1, lo:lo + n], hstat[:, 1, lo:lo + n]))

            def scale_heads(v, lo, gain, width):
                n = v.shape[1]
                link(V.tensor_tensor(v, v, hstat[:, 1, lo:lo + n].unsqueeze(2).broadcast_to([P, n, width]), ALU.mult))
                link(V.tensor_tensor(v, v, gains[:, gain:gain + width].unsqueeze(1).broadcast_to([P, n, width]), ALU.mult))

            dve.wait_ge(chunk_evac, 7)
            dve.wait_ge(tab_ready, 1)
            rope(qi, 16, 8, tmp, 2, (TOK, IH))
            ki = pm[:, :, 320:384]
            rope(ki.unsqueeze(2), 16, 8, tmp, 2, (TOK, 1))
            V.tensor_copy(kirep[:, :, 0:ID], ki)
            V.tensor_copy(kirep[:, :, ID:2 * ID], ki).then_inc(qi_roped, 1)
            link(V.tensor_scalar(pm[:, :, 384:400], pm[:, :, 384:400], float(IH * ID) ** -0.5, None, ALU.mult))
            for v, width, npair, k0, vec in ((mql, QLORA, 2, 0, V_GMQ), (pm[:, :, 0:KVLORA], KVLORA, 1, 4, V_GMKV)):
                sum_squares(v, rstd[:, :], width)
                norm_of(rstd[:, :], width)
                norm_lo(lat_tmp, lat_hi, lat_lo, k0, npair, vecs[:, vec:vec + 2 * npair], None)
            for h in range(IH):
                dve.wait_ge(relu_ready, h + 1)
                if h:
                    dve.wait_ge(relu_used, h)
                for t in range(TOK):
                    r = tmp[:, 1024 + 512 * (h % 4) + S * t:1024 + 512 * (h % 4) + S * (t + 1)]
                    last = V.scalar_tensor_tensor(out=selbias[:, t, :], in0=r, scalar=pm[:, t, 384 + h:385 + h],
                                                  in1=causal[:, t, :] if h == 0 else selbias[:, t, :], op0=ALU.mult, op1=ALU.add)
                last.then_inc(relu_used, 1)
            dve.wait_ge(relu_used, IH)
            for t in range(TOK):
                for _ in range(TOPK // 8):
                    link(V.max(out=m8[:, :], in_=selbias[:, t, :]))
                    link(V.match_replace(out=selbias[:, t, :], in_to_replace=m8[:, :], in_values=selbias[:, t, :], imm_value=TAKEN))
            link(V.tensor_scalar(selbias[:, :, :], selbias[:, :, :], TAKEN / 2, MASKED, ALU.is_gt, ALU.mult))
            link(V.tensor_tensor(selbias[:, :, :], selbias[:, :, :], causal[:, :, :], ALU.add))
            for t in range(TOK):
                sum_squares(pkv[:, t, 0:256].rearrange("p (g d) -> p g d", g=GROUPS), hstat[:, 0, 2 * t:2 * t + 2], HD)
            head_rstd(0, 4, HD)
            for t in range(TOK):
                scale_heads(pkv[:, t, 0:256].rearrange("p (g d) -> p g d", g=GROUPS), 2 * t, HD, HD)
            rope(pkv[:, :, 0:256].rearrange("p t (g d) -> p t g d", g=GROUPS), 0, 16, tmp, 2, (TOK, GROUPS), k_normed)
            dve.wait_ge(k_normed, 1)

            def heads4(v):
                return v.rearrange("p (h t) d -> p h t d", t=TOK)

            t0 = PHASES["mq"][0]
            for j in range(12):
                split(t0 + RING + j)
            sum_squares(pq[:, :, :], hstat[:, 0, 4:20], HD)
            head_rstd(4, 16, HD)
            scale_heads(pq[:, :, :], 4, 0, HD)
            rope(heads4(pq[:, :, :]), 0, 16, tmp, 1, (H, TOK))
            dve.wait_ge(chunk_evac, 15)
            sum_squares(mq[:, :, :], hstat[:, 0, 20:36], MD)
            head_rstd(20, 16, MD)
            scale_heads(mq[:, :, :], 20, 2 * HD, MD)
            rope(heads4(mq[:, :, :])[:, :, :, NOPE:MD], 24, 32, tmp, 1, (H, TOK))
            kr = pm[:, :, KVLORA:KVLORA + MROT]
            sum_squares(mkv[:, :, 0:NOPE], hstat[:, 0, 36:52], NOPE)
            sum_squares(kr, hstat[:, 0, 52:54], MROT)
            link(V.tensor_tensor(hstat[:, 0, 36:52].rearrange("p (h t) -> p h t", t=TOK), hstat[:, 0, 36:52].rearrange("p (h t) -> p h t", t=TOK),
                                 hstat[:, 0, 52:54].unsqueeze(1).broadcast_to([P, H, TOK]), ALU.add))
            head_rstd(36, 16, MD)
            link(V.tensor_tensor(mkv[:, :, 0:NOPE], mkv[:, :, 0:NOPE],
                                 gains[:, 448:448 + NOPE].unsqueeze(1).broadcast_to([P, 2 * H, NOPE]), ALU.mult))
            link(V.tensor_tensor(kbase[:, :, :], kr, gains[:, 448 + NOPE:640].unsqueeze(1).broadcast_to([P, TOK, MROT]), ALU.mult))
            rope(kbase[:, :, :].unsqueeze(2), 24, 32, tmp, 2, (TOK, 1), att_prepared)
            dve.wait_ge(att_prepared, 1)
            ada_begin(3)

            t0, c0, _, _ = PHASES["gate"]
            for g in range(GROUPS):
                with dve.Fori(0, 2) as i:
                    order.enter(i, 8)
                    for cc in range(2):
                        tb, off, h = t0 + 32 * g + 8 * cc + RING, i * 16, i * 2 + (4 * g + cc)
                        split(tb, off)
                        for t in range(TOK):
                            r = hstat[:, 1, bass.ds(h * 2 + (36 + t), 1)]
                            V.tensor_scalar(ksB[:, t, 0:NOPE], mkv[:, bass.ds(h * 2 + t, 1), 0:NOPE].rearrange("p a n -> p (a n)"), r, None, ALU.mult)
                            last = V.tensor_scalar(ksB[:, t, NOPE:MD], kbase[:, t, :], r, None, ALU.mult)
                        last.then_inc(k_staged, 1)
                        split(tb + 1, off)
                        dve.wait_ge(head_turned, h + 1)
                        V.tensor_copy(rT[0:MROT, :, :].rearrange("p a n -> p (a n)"), M[3][0:MROT, :]).then_inc(turned_dve, 1)
                        split(tb + 2, off)
                        for b, (pr, bank, bias, width, maxed) in enumerate(((prA, M[1], selbias, HD, maxedA), (prB, M[3], causal, MD, maxedB))):
                            dve.wait_ge(logits_ready, h * 2 + (b + 1))
                            link(V.scalar_tensor_tensor(out=pr[:, :, :].rearrange("p a n -> p (a n)"), in0=bank[:, :], scalar=float(width) ** -0.5,
                                                        in1=bias[:, :, :].rearrange("p a n -> p (a n)"), op0=ALU.mult, op1=ALU.add))
                            V.tensor_reduce(smax[:, b, 0, :], pr[:, :, :], AX, ALU.max, negate=True).then_inc(maxed, 1)
                        split(tb + 3, off)
                        for b, (pr, done) in enumerate(((prA, expA), (prB, expB))):
                            dve.wait_ge(done, h + 1)
                            link(V.reciprocal(smax[:, b, 1, :], smax[:, b, 1, :]))
                            for t in range(TOK):
                                last = V.tensor_scalar(pr[:, t, :], pr[:, t, :], smax[:, b, 1, t:t + 1], None, ALU.mult)
                            last.then_inc(probs_ready, 1)
                        split(tb + 4, off)
                        dve.wait_ge(pT_ready, h * 2 + 2)
                        V.tensor_copy(pTB[:, :], M[2][:, 0:384]).then_inc(pTB_evac, 1)
                        split(tb + 5, off)
                        ada(48 + 2 * cc + 8 * g, i * 4)
                        split(tb + 6, off)
                        ada(49 + 2 * cc + 8 * g, i * 4)
                        split(tb + 7, off)
                        dve.wait_ge(o_ready, h * 2 + 2)
                        V.tensor_copy(oTB[:, bass.ds(h, 1), 0:S].rearrange("p a n -> p (a n)"), M[3][:, 0:S]).then_inc(oB_evac, 1)
                    order.leave(2)

            for b in range(2):
                dve.wait_ge(o_hi, b + 1)
                V.tensor_tensor(sa_lo[:, 4 * b:4 * b + 4, :], oTA[:, 4 * b:4 * b + 4, :], sa_hi[:, 4 * b:4 * b + 4, :].bitcast(F32),
                                ALU.subtract).then_inc(o_lo, 1)
            for b in range(2):
                dve.wait_ge(o_hi, b + 3)
                V.tensor_tensor(sa_lo[:, 8 + 4 * b:12 + 4 * b, :], oTB[:, 4 * b:4 * b + 4, 0:S], sa_hi[:, 8 + 4 * b:12 + 4 * b, :].bitcast(F32),
                                ALU.subtract).then_inc(o_lo, 1)
            scale_ready(SC_F, V_SCF, V_GFFN)
            ada_begin(4)
            dve.wait_ge(o_lo, 4)

            def half(n, side, i=0):
                t0, c0, _, _ = PHASES["proj"]
                dve.wait_ge(tile_used, i * 8 + (t0 + 8 * n + 4 * side + 4))
                dve.wait_ge(gate_loaded[side], i * 16 + 16 * (n + 1))
                dst = merged if side == 0 else gv2
                for t in range(TOK):
                    last = V.tensor_tensor(dst[:, t, :], acc[(c0 + side) % 2][t][:, :], U[:, side, t, :], ALU.mult)
                last.then_inc(chunk_evac, 1)
                if side:
                    dve.wait_ge(chunk_evac, i * 2 + (c0 + 2 * n + 2))
                    V.tensor_tensor(merged, merged, gv2, ALU.add).then_inc(m_ready, 1)
                    dve.wait_ge(m_ready, i + (n + 1))

            def merged_lo(n):
                for q in range(2):
                    dve.wait_ge(m_hi, n * 2 + (q + 1))
                    V.tensor_tensor(sb_lo[:, bass.ds(n * 4 + 2 * q, 2), :], bank2(M[q]),
                                    sb_hi[:, bass.ds(n * 4 + 2 * q, 2), :].bitcast(F32), ALU.subtract).then_inc(m_lo, 1)

            def proj(n, i, first):
                tb, off = PHASES["proj"][0] + RING + 8 * n, i * 8
                for j in range(4):
                    split(tb + j, off)
                if not first:
                    merged_lo(i)
                ada(64 + 4 * n, i * 4)
                ada(65 + 4 * n, i * 4)
                half(n, 0, i)
                for j in range(4, 8):
                    split(tb + j, off)
                ada(66 + 4 * n, i * 4)
                ada(67 + 4 * n, i * 4)
                half(n, 1, i)

            proj(0, 0, True)
            with dve.Fori(0, 3) as i:
                proj(1, i, False)
            merged_lo(3)
            gate_ready(GT_A, 1)
            dve.wait_ge(gt_ready, 1)
            dve.wait_ge(res_landed, 16)

            def update(name, c, i=0):
                t0, c0, _, k = PHASES[name]
                dve.wait_ge(tile_used, i * (2 * k) + (t0 + (c + 1) * k))
                cols = bass.ds(i * 2 * NC + c * NC, NC)
                for t in range(TOK):
                    last = V.tensor_tensor(gv2[:, t, :], acc[(c0 + c) % 2][t][:, :], gt[:, cols], ALU.mult)
                last.then_inc(chunk_evac, 1)
                dve.wait_ge(chunk_evac, i * 2 + (c0 + c + 1))
                V.tensor_tensor(X[:, :, cols], X[:, :, cols], gv2, ALU.add).then_inc(x_updated, 1)
                dve.wait_ge(x_updated, i * 2 + (UPDATES[name] + c + 1))

            def out_product(name, region=None):
                t0, _, _, k = PHASES[name]
                with dve.Fori(0, 2) as i:
                    for c in range(2):
                        for j in range(8):
                            split(t0 + 8 * c + j + RING, i * 16)
                            if region is not None and j % 2:
                                ada(16 * region + 4 * c + j // 2, i * 8)
                        update(name, c, i)

            out_product("wo")
            norm_x(TOK + 4)
            norm_lo(gv2, sa_hi, sa_lo, 0, 8, mod_s, mod_b)

            def conv(side, pg):
                dve.wait_ge(cv_based, pg * 2 + (side + 1))
                for tap, lag in ((1, 1), (0, 2)):
                    for b in range(4):
                        v = cv[:, 4 * side + b, lag:S]
                        last = V.scalar_tensor_tensor(out=v, in0=M[2 * side + b // 2][:, (b % 2) * S:(b % 2) * S + S - lag],
                                                      scalar=cvec[:, tap, bass.ds(pg * 4 + (44 * side + b), 1)], in1=v,
                                                      op0=ALU.mult, op1=ALU.add)
                    if lag == 1:
                        link(last)
                    else:
                        last.then_inc(cv_done, 1)

            def times(pg):
                dve.wait_ge(cv_done, pg * 2 + 2)
                dve.wait_ge(silu_done, pg + 1)
                V.tensor_tensor(gv[:, :, :], cv[:, 0:4, :], cv[:, 4:8, :], ALU.mult).then_inc(gv_ready, 1)

            def ffn_lo(pg, pl):
                dve.wait_ge(f_hi, pg + 1)
                V.tensor_tensor(sb_lo[:, bass.ds(pl * 4, 4), :], gv[:, :, :], sb_hi[:, bass.ds(pl * 4, 4), :].bitcast(F32),
                                ALU.subtract).then_inc(f_lo, 1)

            def up_pair(part, i, shift, first, region):
                t0 = PHASES[f"up{part}"][0] + 16 * shift
                off = i * 16
                n = 16 * region + 4 * shift
                for j in range(4):
                    split(t0 + RING + j, off)
                if not first:
                    conv(1, i + (shift + 4 * part - 1))
                    times(i + (shift + 4 * part - 1))
                split(t0 + RING + 4, off)
                split(t0 + RING + 5, off)
                if not first:
                    ffn_lo(i + (shift + 4 * part - 1), i + (shift - 1))
                split(t0 + RING + 6, off)
                ada(n, i * 4)
                split(t0 + RING + 7, off)
                ada(n + 1, i * 4)
                for j in range(4):
                    split(t0 + RING + 8 + j, off)
                conv(0, i + (shift + 4 * part))
                split(t0 + RING + 12, off)
                ada(n + 2, i * 4)
                split(t0 + RING + 13, off)
                split(t0 + RING + 14, off)
                ada(n + 3, i * 4)
                split(t0 + RING + 15, off)

            for part, (n, region) in enumerate(zip(PAIRS, (GT_F, SH_2, GT_2))):
                ada_begin(region)
                up_pair(part, 0, 0, True, region)
                with dve.Fori(0, n - 1) as i:
                    order.enter(i, 2)
                    up_pair(part, i, 1, False, region)
                    order.leave(n - 1)
                conv(1, 4 * part + n - 1)
                times(4 * part + n - 1)
                ffn_lo(4 * part + n - 1, n - 1)
                if part == 0:
                    gate_ready(GT_F, 2)
                    dve.wait_ge(gt_ready, 2)
                    out_product("down0")
                if part == 1:
                    shift_ready(SH_2, V_SH2)
                    ada_begin(SC_2)
                    out_product("down1", SC_2)
                    scale_ready(SC_2, V_SC2)
            t0 = PHASES["down2"][0]
            for c in range(4):
                for j in range(6):
                    split(t0 + 6 * c + j + RING)
                ada(16 * GT_2 + 12 + c)
                update("down2", c)

            norm_x(TOK + 8)
            norm_lo(gv2, sa_hi, sa_lo, 0, 8, mod_s, mod_b)

            def pooled_lo(c):
                for q in range(2):
                    dve.wait_ge(p_hi, 2 * c + q + 1)
                    k = 4 * c + 2 * q
                    V.tensor_tensor(sb_lo[:, k:k + 2, :], bank2(M[2 * (c % 2) + q]), sb_hi[:, k:k + 2, :].bitcast(F32),
                                    ALU.subtract).then_inc(p_lo, 1)

            t0 = PHASES["pin"][0] + RING
            for c in range(4):
                for j in range(4):
                    split(t0 + 8 * c + j)
                if c:
                    pooled_lo(c - 1)
                for j in range(4, 8):
                    split(t0 + 8 * c + j)
            pooled_lo(3)
            gate_ready(GT_2, 3)
            with dve.Fori(0, 2) as i:
                for j in range(16):
                    split(t0 + 32 + j, i * 16)
            t0, c0, _, _ = PHASES["grp"]
            for g in range(4):
                split(t0 + RING + 2 * g)
                split(t0 + RING + 2 * g + 1)
                dve.wait_ge(tile_used, t0 + 2 * g + 2)
                if g == 0:
                    dve.wait_ge(chunk_evac, c0)
                for t in range(TOK):
                    last = V.tensor_tensor(U[:, g % 2, t, :], acc[(c0 + g) % 2][t][:, :], ada_ring[:, t, g * NC:(g + 1) * NC], ALU.mult)
                last.then_inc(chunk_evac, 1)
                dve.wait_ge(y_turned, 2 * g + 2)
                for b in range(4):
                    last = V.tensor_scalar(gv[:, b, :], M[2 * (g % 2) + b // 2][:, (b % 2) * S:(b % 2 + 1) * S],
                                           vecs[:, V_PSCALE + 4 * g + b:V_PSCALE + 4 * g + b + 1], None, ALU.mult)
                last.then_inc(y_scaled, 1)
                dve.wait_ge(y_hi, g + 1)
                V.tensor_tensor(sa_lo[:, 4 * g:4 * g + 4, :], gv[:, :, :], sa_hi[:, 4 * g:4 * g + 4, :].bitcast(F32),
                                ALU.subtract).then_inc(y_lo, 1)
            t0 = PHASES["pout"][0]
            dve.wait_ge(gt_ready, 3)
            dve.wait_ge(y_lo, 4)
            for c in range(4):
                for j in range(8):
                    split(t0 + 8 * c + j + RING)
                update("pout", c)
            norm_x(TOK + 12, with_diag=False)
            dve.wait_ge(fg_landed, 16)
            for t in range(TOK):
                V.scalar_tensor_tensor(out=X[:, t, :], in0=X[:, t, :], scalar=rstd[:, t:t + 1], in1=fgain,
                                       op0=ALU.mult, op1=ALU.mult).then_inc(out_ready, 1)

        @block.tensor
        def _(pe):
            mm = nc.tensor.matmul

            def tile(tb, off, hi, lo, ks, pair, first, last):
                pe.wait_ge(lo_ready, tb + 1 + off)
                for n, k in enumerate(ks):
                    for t in range(TOK):
                        xh, xl = hi[:, k, t * P:(t + 1) * P], lo[:, k, t * P:(t + 1) * P]
                        wh, wl = whi[:, tb % RING, n, :], wlo[:, tb % RING, n, :]
                        mm(pair[t][:, :], xh, wh, start=first and n == 0, stop=False)
                        mm(pair[t][:, :], xh, wl, start=False, stop=False)
                        end = mm(pair[t][:, :], xl, wh, start=False, stop=last and n == 1)
                end.then_inc(tile_used, 1)

            def bank_free(c, i=0, per=1):
                if c >= 2:
                    pe.wait_ge(chunk_evac, i * per + (c - 1))

            def tiles(name, c, js, hi, lo, i=0, per=1, k0=0, wait=None):
                t0, c0, _, k = PHASES[name]
                for j in js:
                    if j == 0:
                        bank_free(c0 + c, i, per)
                    if wait:
                        wait(j)
                    tile(t0 + c * k + j, i * (per * k), hi, lo, (k0 + 2 * j, k0 + 2 * j + 1), acc[(c0 + c) % 2], j == 0, j == k - 1)

            def sum_cols(r):
                pe.wait_ge(ada_used, 16 * (r + 1))
                for b in range(16):
                    last = mm(M[0][:, b:b + 1], ada_acc[:, b * P:(b + 1) * P], ones[:, 0:1], start=True, stop=True)
                last.then_inc(region_summed, 1)

            def sum_rows(r):
                pe.wait_ge(ada_used, 16 * (r + 1))
                for n in range(4):
                    last = mm(M[n][:, :], ones[:, :], ada_acc[:, n * NC:(n + 1) * NC], start=True, stop=True)
                last.then_inc(region_summed, 1)

            pairs = [0]
            diags = [0]

            def norm_turn(src, npair):
                diags[0] += 1
                pe.wait_ge(diag_ready, diags[0])
                for b in range(npair):
                    if b >= 4:
                        pe.wait_ge(nrm_evac, pairs[0] + b - 3)
                    for kk in range(2):
                        for t in range(TOK):
                            k = 2 * b + kk
                            last = mm(M[b % 4][:, kk * S + t * P:kk * S + (t + 1) * P], src(t, k), diag[:, t, :], start=True, stop=True)
                    last.then_inc(nrm_turned, 1)
                pairs[0] += npair

            pe.wait_ge(ones_ready, 1)
            pe.wait_ge(vec_landed, 16 * 13)
            nc.tensor.transpose(M[1][:, 0:P], vstage[:, 0, :], ident[:, :])
            nc.tensor.transpose(M[1][:, P:P + 22], vstage[0:22, 1, :], ident[0:22, 0:22]).then_inc(vec_turned, 1)
            for j in range(4):
                last = nc.tensor.transpose(M[2][:, 88 * j:88 * (j + 1)], vstage[0:88, 2 + j, :], ident[0:88, 0:88])
            last.then_inc(vec_turned, 1)
            sum_cols(SH_A)
            pe.wait_ge(mod_ready, 1)
            sum_cols(SC_A)
            pe.wait_ge(mod_ready, 2)
            norm_turn(lambda t, k: xs[:, t, k * P:(k + 1) * P], 8)

            tiles("in", 0, range(8), sa_hi, sa_lo, wait=lambda j: pe.wait_ge(nrm_lo, j + 1))
            for c in (1, 2):
                tiles("in", c, range(8), sa_hi, sa_lo)
            with pe.Fori(0, 2) as i:
                for c in (3, 4):
                    tiles("in", c, range(8), sa_hi, sa_lo, i, 2)
            sum_cols(SH_F)
            pe.wait_ge(mod_ready, 3)

            pe.wait_ge(qi_roped, 1)
            for b in range(8):
                for t in range(TOK):
                    last = nc.tensor.transpose(M[b // 2][:, (b % 2) * S + t * P:(b % 2) * S + (t + 1) * P],
                                               qi[:, t, 2 * b:2 * b + 2, :].rearrange("p h d -> p (h d)"), ident[:, :])
                if b % 2:
                    last.then_inc(qi_turned, 1)
            pe.wait_ge(qi_evac, 1)
            for t in range(TOK):
                last = nc.tensor.transpose(M[0][:, t * P:(t + 1) * P], kirep[:, t, :], ident[:, :])
            last.then_inc(qi_turned, 1)
            pe.wait_ge(qi_evac, 5)
            norm_turn(lambda t, k: mql[:, t, k * P:(k + 1) * P], 2)
            pe.wait_ge(nrm_evac, 10)
            norm_turn(lambda t, k: pm[:, t, k * P:(k + 1) * P], 1)
            pe.wait_ge(nrm_evac, 11)
            for h in range(IH):
                if h >= 4:
                    pe.wait_ge(relu_ready, h - 3)
                part = slice(ID * (h % 2), ID * (h % 2 + 1))
                for t in range(TOK):
                    last = mm(M[h % 4][:, t * S:(t + 1) * S], qiT[part, h // 2, t * P:(t + 1) * P], kiT[part, :], start=True, stop=True)
                last.then_inc(dots_ready, 1)
            pe.wait_ge(relu_ready, IH)
            pe.wait_ge(k_normed, 1)
            for g in range(GROUPS):
                for t in range(TOK):
                    last = nc.tensor.transpose(M[0][:, g * S + t * P:g * S + (t + 1) * P], pkv[:, t, g * HD:(g + 1) * HD], ident[:, :])
            last.then_inc(k_turned, 1)
            pe.wait_ge(nrm_lo, 11)
            for c in range(4):
                tiles("mq", c, range(2), lat_hi, lat_lo)
            for c in range(4):
                tiles("mkv", c, range(1), lat_hi, lat_lo, k0=4)

            for g in range(GROUPS):
                with pe.Fori(0, 2) as i:
                    for cc in range(2):
                        c = 4 * g + cc
                        h = i * 2 + c
                        tiles("gate", c, (0,), sa_hi, sa_lo, i, 2)
                        pe.wait_ge(q_staged, h + 1)
                        pe.wait_ge(k_staged, h + 1)
                        for t in range(TOK):
                            at = slice(t * P, (t + 1) * P)
                            nc.tensor.transpose(M[0][:, at], qsA[:, t, :], ident[:, :])
                            nc.tensor.transpose(M[2][:, at], qsB[:, t, 0:NOPE], ident[:, :])
                            nc.tensor.transpose(M[2][:, S + t * P:S + (t + 1) * P], ksB[:, t, 0:NOPE], ident[:, :])
                            nc.tensor.transpose(M[3][0:MROT, at], qsB[:, t, NOPE:MD], ident[:, :])
                            last = nc.tensor.transpose(M[3][0:MROT, S + t * P:S + (t + 1) * P], ksB[:, t, NOPE:MD], ident[:, :])
                        last.then_inc(head_turned, 1)
                        tiles("gate", c, (1, 2), sa_hi, sa_lo, i, 2)
                        pe.wait_ge(turned_act, h + 1)
                        pe.wait_ge(turned_dve, h + 1)
                        for t in range(TOK):
                            last = mm(M[1][:, t * S:(t + 1) * S], qTA[:, t * P:(t + 1) * P], kT[:, g, :], start=True, stop=True)
                        last.then_inc(logits_ready, 1)
                        for t in range(TOK):
                            mm(M[3][:, t * S:(t + 1) * S], nT[:, 0, t * P:(t + 1) * P], nT[:, 1, :], start=True, stop=False)
                            last = mm(M[3][:, t * S:(t + 1) * S], rT[0:MROT, 0, t * P:(t + 1) * P], rT[0:MROT, 1, :], start=False, stop=True)
                        last.then_inc(logits_ready, 1)
                        tiles("gate", c, (3, 4), sa_hi, sa_lo, i, 2)
                        for b, (pr, bank) in enumerate(((prA, M[0]), (prB, M[2]))):
                            pe.wait_ge(probs_ready, h * 2 + (b + 1))
                            nc.tensor.transpose(bank[:, 0:P], pr[:, 0, 0:P], ident[:, :])
                            nc.tensor.transpose(bank[:, P:2 * P], pr[:, 1, 0:P], ident[:, :])
                            nc.tensor.transpose(bank[:, 2 * P:3 * P], pr[:, 1, P:2 * P], ident[:, :]).then_inc(pT_ready, 1)
                        tiles("gate", c, (5, 6), sa_hi, sa_lo, i, 2)
                        for evac, pT, v, bank in ((pTA_evac, pTA, vA, M[1]), (pTB_evac, pTB, vB, M[3])):
                            pe.wait_ge(evac, h + 1)
                            mm(bank[:, 0:S], v[:, 0, :], pT[:, 0:S], start=True, stop=False, skip_group_check=True)
                            mm(bank[:, P:S], v[:, 1, :], pT[:, S:384], start=False, stop=True, skip_group_check=True).then_inc(o_ready, 1)
                        tiles("gate", c, (7,), sa_hi, sa_lo, i, 2)

            pe.wait_ge(oB_evac, H)
            sum_cols(SC_F)
            pe.wait_ge(mod_ready, 4)

            def merged_turn(n):
                pe.wait_ge(m_ready, n + 1)
                for q in range(2):
                    for b in range(2):
                        for t in range(TOK):
                            blk = (2 * q + b) * P
                            last = nc.tensor.transpose(M[q][:, b * S + t * P:b * S + (t + 1) * P], merged[:, t, blk:blk + P], ident[:, :])
                    last.then_inc(m_turned, 1)

            def proj(n, i, first):
                tiles("proj", 2 * n, (0, 1), sa_hi, sa_lo, i, 2)
                if not first:
                    merged_turn(i)
                tiles("proj", 2 * n, (2, 3), sa_hi, sa_lo, i, 2)
                tiles("proj", 2 * n + 1, range(4), sa_hi, sa_lo, i, 2, k0=8)

            pe.wait_ge(o_lo, 4)
            proj(0, 0, True)
            with pe.Fori(0, 3) as i:
                proj(1, i, False)
            merged_turn(3)
            pe.wait_ge(m_lo, 8)
            sum_rows(GT_A)

            def out_product(name, wait=None):
                with pe.Fori(0, 2) as i:
                    for c in range(2):
                        tiles(name, c, range(8), sb_hi, sb_lo, i, 2)

            out_product("wo")
            pe.wait_ge(gt_ready, 1)
            norm_turn(lambda t, k: X[:, t, k * P:(k + 1) * P], 8)

            def turn(side):
                for q in range(2):
                    for b in range(2):
                        for t in range(TOK):
                            blk = (2 * q + b) * P
                            last = nc.tensor.transpose(M[2 * side + q][:, b * S + t * P:b * S + (t + 1) * P],
                                                       U[:, side, t, blk:blk + P], ident[:, :])
                    last.then_inc(u_turned, 1)

            def up_pair(part, i, shift, first, wait=None):
                name = f"up{part}"
                c0 = PHASES[name][1]
                c = 2 * shift
                tiles(name, c, range(4), sa_hi, sa_lo, i, 2, wait=wait)
                if not first:
                    pe.wait_ge(chunk_evac, i * 2 + (c0 + c))
                    turn(1)
                tiles(name, c, range(4, 8), sa_hi, sa_lo, i, 2, wait=wait)
                tiles(name, c + 1, range(4), sa_hi, sa_lo, i, 2)
                pe.wait_ge(chunk_evac, i * 2 + (c0 + c + 1))
                turn(0)
                tiles(name, c + 1, range(4, 8), sa_hi, sa_lo, i, 2)

            for part, n in enumerate(PAIRS):
                up_pair(part, 0, 0, True, (lambda j: pe.wait_ge(nrm_lo, 12 + j)) if part == 0 else None)
                with pe.Fori(0, n - 1) as i:
                    up_pair(part, i, 1, False)
                _, c0, nn, _ = PHASES[f"up{part}"]
                pe.wait_ge(chunk_evac, c0 + nn)
                turn(1)
                pe.wait_ge(f_lo, 4 * part + n)
                if part == 0:
                    sum_rows(GT_F)
                    out_product("down0")
                if part == 1:
                    sum_cols(SH_2)
                    out_product("down1")
                    pe.wait_ge(mod_ready, 5)
                    sum_cols(SC_2)
                    pe.wait_ge(mod_ready, 6)
            for c in range(4):
                tiles("down2", c, range(6), sb_hi, sb_lo)

            norm_turn(lambda t, k: X[:, t, k * P:(k + 1) * P], 8)

            def pooled(c):
                pe.wait_ge(chunk_evac, PHASES["pin"][1] + c + 1)
                pe.wait_ge(pmat_landed, 16)
                if c >= 2:
                    pe.wait_ge(p_lo, 2 * (c - 1))
                for q in range(2):
                    for b in range(2):
                        blk = (2 * q + b) * P
                        for t in range(TOK):
                            last = mm(M[2 * (c % 2) + q][:, b * S:(b + 1) * S], U[:, c % 2, t, blk:blk + P], cv[:, 2 * c + t, :],
                                      start=t == 0, stop=t == TOK - 1)
                    last.then_inc(p_turned, 1)

            for c in range(4):
                wait = (lambda j: pe.wait_ge(nrm_lo, 20 + j)) if c == 0 else None
                tiles("pin", c, range(4), sa_hi, sa_lo, wait=wait)
                if c:
                    pooled(c - 1)
                tiles("pin", c, range(4, 8), sa_hi, sa_lo, wait=wait)
            pooled(3)
            pe.wait_ge(p_lo, 8)
            sum_rows(GT_2)
            with pe.Fori(0, 2) as i:
                for c in (4, 5):
                    tiles("pin", c, range(8), sa_hi, sa_lo, i, 2)
            pe.wait_ge(gt_ready, 3)
            c0 = PHASES["grp"][1]
            for g in range(4):
                tiles("grp", g, range(2), sb_hi, sb_lo, k0=4 * g)
                pe.wait_ge(chunk_evac, c0 + g + 1)
                if g >= 2:
                    pe.wait_ge(y_scaled, g - 1)
                for q in range(2):
                    for b in range(2):
                        for t in range(TOK):
                            blk = (2 * q + b) * P
                            last = nc.tensor.transpose(M[2 * (g % 2) + q][:, b * S + t * P:b * S + (t + 1) * P],
                                                       U[:, g % 2, t, blk:blk + P], ident[:, :])
                    last.then_inc(y_turned, 1)
            pe.wait_ge(y_lo, 4)
            for c in range(4):
                tiles("pout", c, range(8), sa_hi, sa_lo)


_INS = ["x", "c", "positions", "g_attn", "g_ffn", "w_ada", "b_ada", "w_in", "g_qa", "g_ka", "g_mq_lat", "w_mq_up",
        "g_mkv_lat", "w_mkv_up", "g_qm", "g_km", "w_pa", "w_pb", "w_o", "w_up", "w_conv", "b_conv", "w_down",
        "c_2", "w_mod_2", "b_mod_2", "pool_w_in_2", "pool_w_grp_2", "pool_scale_2", "pool_w_out_2", "final_norm_g_2"]


def shape_constants():
    inv = [THETA ** (-np.arange(0, r, 2) / r) for r in (ROT, IROT, MROT)]
    q, k = np.arange(S)[:, None], np.arange(S)[None, :]
    causal = np.where(k <= q, 0.0, MASKED).reshape(TOK, P, S).transpose(1, 0, 2)
    pool = np.zeros((4, S, S))
    for g, w in enumerate(WINDOWS):
        lo, hi = np.maximum(q - w // 2, 0), np.minimum(q + w // 2, S)
        pool[g] = (((k >= lo) & (k < hi)) / (hi - lo) - np.eye(S)).T
    pool = pool.reshape(4, TOK, P, S).transpose(2, 0, 1, 3).reshape(P, 4 * TOK, S)
    return {"identity": np.eye(P, dtype=np.float32), "inv_freq": np.concatenate(inv)[None].astype(np.float32),
            "causal": causal.astype(np.float32), "pool_matrix": np.ascontiguousarray(pool).astype(np.float32)}


def kernel(**inputs):
    import numpy as _np
    import concourse.bacc as _bacc
    from concourse.bass_utils import run_bass_kernel_spmd as _run

    nc = _bacc.Bacc("TRN2", target_bir_lowering=False, num_devices=1)
    arrays, args = {}, {}
    given = {n: _np.ascontiguousarray(inputs[n]) for n in _INS}
    for name, a in {**given, **shape_constants()}.items():
        arrays[f"in_{name}_dram"] = a
        args[name] = nc.dram_tensor(f"in_{name}_dram", a.shape, mybir.dt.from_np(a.dtype), kind="ExternalInput").ap()
    out = nc.dram_tensor("out_0_dram", (1, S, D), F32, kind="ExternalOutput").ap()
    build(nc, args, out)
    r = _run(nc, [arrays], core_ids=[0])
    return r.results[0]["out_0_dram"]
```

```python
from contextlib import ExitStack

import numpy as np

import concourse.bass as bass
from concourse import mybir

F32 = mybir.dt.float32
F32R = mybir.dt.float32r
I32 = mybir.dt.int32
ALU = mybir.AluOpType
ACT = mybir.ActivationFunctionType
AX = mybir.AxisListType.X

P = 128
D = 2048
S = 256
TOK = S // P
NC = 512
RAW, RING = 8, 4
D_FF = 5632
H, HD, ROT = 8, 128, 32
GROUPS = 2
IH, ID, IROT = 16, 64, 16
NOPE, MROT, MV = 128, 64, 128
MD = NOPE + MROT
QLORA, KVLORA = 512, 256
TOPK = 64
THETA = 500000.0
EPS = 1e-6
MASKED = -1e30
TAKEN = -3e38
WINDOWS = (2, 4, 8, 16)
TWO_PI = 6.283185307179586
PI_HI = 6.28125
PI_MID = float(np.float32(TWO_PI - PI_HI))
PI_LO = float(TWO_PI - PI_HI - PI_MID)
ROUND = 12582912.0

C_QA, C_KA, C_QI, C_KI, C_MQ, C_MKV, C_GATE = 0, 1024, 1536, 2560, 2640, 3152, 3472

PHASES = {}
_t = _c = 0
for _name, _n, _k in (("in", 7, 8), ("mq", 4, 2), ("mkv", 4, 1), ("gate", 8, 8), ("proj", 8, 4), ("wo", 4, 8),
                      ("up0", 8, 8), ("down0", 4, 8), ("up1", 8, 8), ("down1", 4, 8), ("up2", 6, 8), ("down2", 4, 6),
                      ("pin", 4, 8), ("gp0", 1, 8), ("grp0", 1, 2), ("gp1", 1, 8), ("grp1", 1, 2), ("gp2", 1, 8),
                      ("grp2", 1, 2), ("gp3", 1, 8), ("grp3", 1, 2), ("pout", 4, 8)):
    PHASES[_name] = (_t, _c, _n, _k)
    _t += _n * _k
    _c += _n
TILES = _t

V_GATTN, V_GFFN, V_SHA, V_SCA, V_SHF, V_SCF, V_SH2, V_SC2 = range(0, 128, 16)
V_PSCALE, V_GMQ, V_GMKV = 128, 144, 148
NVEC = 150

SH_A, SC_A, SH_F, SC_F, GT_A, GT_F, SH_2, SC_2, GT_2 = range(9)
COLS = [SH_A, SC_A, SH_F, SC_F, SH_2, SC_2]
ROWS = [GT_A, GT_F, GT_2]
REGION_SRC = [(0, 0), (0, 1), (0, 3), (0, 4), (0, 2), (0, 5), (1, 0), (1, 1), (1, 2)]


PAIRS = (4, 4, 3)
UPDATES = {"wo": 0, "down0": 4, "down1": 8, "down2": 12, "pout": 16}
PI_IN = 3.1415925


def summed(r):
    return ("cols", COLS.index(r) + 1) if r in COLS else ("rows", 2 * ROWS.index(r) + 2)


class Order:

    def __init__(self, eng, sem):
        self.eng, self.sem, self.base, self.n = eng, sem, 0, 0

    def link(self, ins):
        self.n += 1
        ins.then_inc(self.sem, 1)
        self.eng.wait_ge(self.sem, self.base + self.n)

    def enter(self, i, per):
        self.outer, self.per = self.base + self.n, per
        self.base, self.n = i * per + self.outer, 0

    def leave(self, trips):
        assert self.n == self.per, self.n
        self.base, self.n = self.outer + self.per * trips, 0


def build(nc, A, out):
    ctx = ExitStack()
    with ctx:
        def sb(name, shape, dt=F32, stack=ctx):
            return stack.enter_context(nc.sbuf_tensor(name, shape, dt))

        def sem(name):
            return ctx.enter_context(nc.semaphore(name))

        raw = sb("raw", [P, RAW, 2, NC])
        whi = sb("whi", [P, RING, 2, NC], F32R)
        wlo = sb("wlo", [P, RING, 2, NC], F32R)
        sa_hi = sb("sa_hi", [P, 16, S], F32R)
        sa_lo = sb("sa_lo", [P, 16, S], F32R)
        ada_ring = sb("ada_ring", [P, 2, D])
        ada_acc = sb("ada_acc", [P, D])
        vecs = sb("vecs", [P, NVEC])
        cvec = sb("cvec", [P, 4, 88])
        ident = sb("ident", [P, P])
        ones = sb("ones", [P, P])
        diag = sb("diag", [P, TOK, P])
        cact = sb("cact", [P, 2, 16])
        mod_s = sb("mod_s", [P, 16])
        mod_b = sb("mod_b", [P, 16])
        stat = sb("stat", [P, 2, 2 * TOK])
        ssq = sb("ssq", [P, TOK, 4])
        rstd = sb("rstd", [P, 2 * TOK])
        warm = sb("warm", [P, 1])

        with ExitStack() as st:
            xs = sb("xs", [P, TOK, D], stack=st)
            start_ring = sb("start_ring", [P, 4, D], stack=st)
            vstage = sb("vstage", [P, 6, P], stack=st)
            craw = sb("craw", [P, 2, 16], stack=st)
            start_tmp = sb("start_tmp", [P, 2, 512], stack=st)
            sqdump = sb("sqdump", [P, D], stack=st)
        with ExitStack() as st:
            pq = sb("pq", [P, 2 * H, HD], stack=st)
            pkv = sb("pkv", [P, TOK, 512], stack=st)
            pm = sb("pm", [P, TOK, 400], stack=st)
            p2 = sb("p2", [P, 3072], stack=st)
            mkv = sb("mkv", [P, 2 * H, 256], stack=st)
            gains = sb("gains", [P, 640], stack=st)
            posf = sb("posf", [P, 2, TOK], stack=st)
            tabs = sb("tabs", [P, 2, TOK, 56], stack=st)
            causal = sb("causal", [P, TOK, S], stack=st)
            selbias = sb("selbias", [P, TOK, S], stack=st)
            kT = sb("kT", [P, GROUPS, S], stack=st)
            kbase = sb("kbase", [P, TOK, MROT], stack=st)
            hstat = sb("hstat", [P, 2, 56], stack=st)
            smax = sb("smax", [P, 2, 2, TOK], stack=st)
            gstage = sb("gstage", [P, TOK, NC], stack=st)
            with ExitStack() as prep:
                lat_hi = sb("lat_hi", [P, 6, S], F32R, stack=prep)
                lat_lo = sb("lat_lo", [P, 6, S], F32R, stack=prep)
                tmp = sb("tmp", [P, 2048], stack=prep)
                kirep = sb("kirep", [P, TOK, P], stack=prep)
                kiT = sb("kiT", [P, S], stack=prep)
                m8 = sb("m8", [P, 8], stack=prep)
                dump = sb("dump", [P, NC], stack=prep)
                diag2 = sb("diag2", [P, TOK, P], stack=prep)
            with ExitStack() as hd:
                qsA = sb("qsA", [P, 2, TOK, HD], stack=hd)
                qTA = sb("qTA", [P, 2, S], stack=hd)
                prA = sb("prA", [P, 2, TOK, S], stack=hd)
                pTA = sb("pTA", [P, 2, 384], stack=hd)
                vA = sb("vA", [P, TOK, HD], stack=hd)
                ropeA = sb("ropeA", [P, 4 * TOK * 16], stack=hd)
            with ExitStack() as hd:
                qsB = sb("qsB", [P, 2, TOK, MD], stack=hd)
                ksB = sb("ksB", [P, 2, TOK, MD], stack=hd)
                nT = sb("nT", [P, 2, 2, S], stack=hd)
                rT = sb("rT", [P, 2, 2, S], stack=hd)
                prB = sb("prB", [P, 2, TOK, S], stack=hd)
                pTB = sb("pTB", [P, 2, 384], stack=hd)
                vB = sb("vB", [P, 2, TOK, MV], stack=hd)
                ropeB = sb("ropeB", [P, 4 * TOK * 32], stack=hd)
        sb_hi = sb("sb_hi", [P, 16, S], F32R)
        sb_lo = sb("sb_lo", [P, 16, S], F32R)
        X = sb("X", [P, TOK, D])
        gt = sb("gt", [P, D])
        U = sb("U", [P, 2, TOK, NC])
        cv = sb("cv", [P, 8, S])
        gv = sb("gv", [P, 4, S])

        acc = [[ctx.enter_context(nc.psum_tensor(f"acc{a}{b}", [P, NC], F32)) for b in range(TOK)] for a in range(2)]
        M = [ctx.enter_context(nc.psum_tensor(f"misc{a}", [P, NC], F32)) for a in range(4)]
        gates_dram = nc.dram_tensor("gates_dram", (8, P, TOK, NC), F32, kind="Internal").ap()

        raw_landed = [sem(f"raw_landed{i}") for i in range(RAW)]
        hi_ready, lo_ready, tile_used, chunk_evac = sem("hi_ready"), sem("lo_ready"), sem("tile_used"), sem("chunk_evac")
        ada_landed = [sem(f"ada_landed{i}") for i in range(2)]
        start_landed = [sem(f"start_landed{i}") for i in range(4)]
        ada_used, cols_summed, rows_summed, mod_ready, gt_ready = (sem(n) for n in (
            "ada_used", "cols_summed", "rows_summed", "mod_ready", "gt_ready"))
        consts_landed, vec_landed, x_landed, ones_ready = sem("consts_landed"), sem("vec_landed"), sem("x_landed"), sem("ones_ready")
        vec_turned, vec_ready, c_ready = sem("vec_turned"), sem("vec_ready"), sem("c_ready")
        ssq_cleared, xsq_done, ms_ready, sqrt_ready, diag_ready = (sem(n) for n in (
            "ssq_cleared", "xsq_done", "ms_ready", "sqrt_ready", "diag_ready"))
        nrm_turned, nrm_evac, nrm_hi, nrm_lo = sem("nrm_turned"), sem("nrm_evac"), sem("nrm_hi"), sem("nrm_lo")
        dve_order, att_landed, ang_ready, tab_ready = sem("dve_order"), sem("att_landed"), sem("ang_ready"), sem("tab_ready")
        qi_roped, qi_turned, qi_evac = sem("qi_roped"), sem("qi_turned"), sem("qi_evac")
        dots_ready, relu_ready, relu_used = sem("dots_ready"), sem("relu_ready"), sem("relu_used")
        k_normed, k_turned, k_evac = sem("k_normed"), sem("k_turned"), sem("k_evac")
        hs_ms, hs_sqrt, hs_ready, kbase_ready, act_order = (sem(n) for n in ("hs_ms", "hs_sqrt", "hs_ready", "kbase_ready", "act_order"))
        A_staged, A_turned, A_qT, A_logits, A_maxed, A_probs, A_pT, A_pT_evac, A_o, A_o_evac, A_v = (sem("A_" + n) for n in (
            "staged", "turned", "qT", "logits", "maxed", "probs", "pT", "pT_evac", "o", "o_evac", "v"))
        B_staged, B_turned, B_nT, B_rT, B_logits, B_maxed, B_probs, B_pT, B_pT_evac, B_o, B_o_evac, B_v = (sem("B_" + n) for n in (
            "staged", "turned", "nT", "rT", "logits", "maxed", "probs", "pT", "pT_evac", "o", "o_evac", "v"))
        A_exp, B_exp = sem("A_exp"), sem("B_exp")
        gstage_free = sem("gstage_free")
        gate_loaded = [sem(f"gate_loaded{i}") for i in range(2)]
        o_hi, o_lo, res_landed, bias_landed = sem("o_hi"), sem("o_lo"), sem("res_landed"), sem("bias_landed")
        m_ready, m_turned, m_hi, m_lo, x_updated = (sem(n) for n in ("m_ready", "m_turned", "m_hi", "m_lo", "x_updated"))
        u_ready, u_turned, cv_based, cv_done, silu_done = (sem(n) for n in ("u_ready", "u_turned", "cv_based", "cv_done", "silu_done"))
        gv_ready, f_hi, f_lo = sem("gv_ready"), sem("f_hi"), sem("f_lo")
        pmat_landed, fg_landed, p_turned, p_hi, p_lo = (sem(n) for n in ("pmat_landed", "fg_landed", "p_turned", "p_hi", "p_lo"))
        y_turned, y_scaled, y_hi, y_lo, outA, outD, storedS, storedA, fg_applied = (sem(n) for n in (
            "y_turned", "y_scaled", "y_hi", "y_lo", "outA", "outD", "storedS", "storedA", "fg_applied"))

        W = {n: A[n][0].rearrange("(k p) n -> p k n", p=P) for n in
             ("w_in", "w_mq_up", "w_mkv_up", "w_pa", "w_pb", "w_o", "w_up", "w_down", "pool_w_in_2", "pool_w_out_2")}
        w_grp = A["pool_w_grp_2"][0].rearrange("g (k p) n -> p g k n", p=P)
        ada_src = [A["w_ada"][0].rearrange("(p t) n -> p t n", t=16), A["w_mod_2"][0].rearrange("(p t) n -> p t n", t=16)]
        xv = A["x"][0].rearrange("(t p) n -> p t n", p=P)
        outv = out[0].rearrange("(t p) n -> p t n", p=P)
        qi = p2[:, 0:2048].rearrange("p (t h d) -> p t h d", t=TOK, h=IH)
        mql = p2[:, 2048:3072].rearrange("p (t d) -> p t d", t=TOK)
        mq = p2[:, :].rearrange("p (a d) -> p a d", d=MD)
        oTA = pq[:, :, :].rearrange("p (h t) d -> p h (t d)", t=TOK)
        oTB = p2[:, :].rearrange("p (h x) -> p h x", h=H)
        qiT = mkv
        merged = cv[:, 0:4, :].rearrange("p a n -> p (a n)").rearrange("p (t n) -> p t n", t=TOK)
        gv2 = gv[:, :, :].rearrange("p a n -> p (a n)").rearrange("p (t n) -> p t n", t=TOK)
        fgain = cv[:, :, :].rearrange("p a n -> p (a n)")
        lat_tmp = tmp[:, 0:1024].rearrange("p (a n) -> p a n", a=2)

        def bank2(m):
            return m[:, :].rearrange("p (a n) -> p a n", a=2)

        block = ctx.enter_context(nc.Block())

        @block.sync
        def _(sp):
            def tile_in(tb, off, src):
                if tb >= RAW:
                    sp.wait_ge(lo_ready, tb - RAW + 1 + off)
                sp.dma_start(raw[:, tb % RAW, :, :], src).then_inc(raw_landed[tb % RAW], 16)

            sp.dma_start(craw[:, 0, :], A["c"][0].rearrange("(p t) -> p t", t=16)).then_inc(consts_landed, 16)
            sp.dma_start(craw[:, 1, :], A["c_2"][0].rearrange("(p t) -> p t", t=16)).then_inc(consts_landed, 16)
            for j in range(4):
                sp.dma_start(start_ring[:, j, :], ada_src[0][:, j, 0:D]).then_inc(start_landed[j], 16)
            sp.dma_start(ident[:, :], A["identity"]).then_inc(vec_landed, 16)
            for v, name, lo, n in ((V_GATTN, "g_attn", 0, 16), (V_GFFN, "g_ffn", 0, 16), (V_SHA, "b_ada", 0, 32),
                                   (V_SHF, "b_ada", 3 * D, 32), (V_SH2, "b_mod_2", 0, 32)):
                sp.dma_start(vstage[v:v + n, 0, :],
                             A[name][0, lo:lo + n * P].rearrange("(a b) -> a b", b=P)).then_inc(vec_landed, 16)
            for v, name, n in ((0, "pool_scale_2", 16), (16, "g_mq_lat", 4), (20, "g_mkv_lat", 2)):
                sp.dma_start(vstage[v:v + n, 1, :], A[name][0].rearrange("(a b) -> a b", b=P)).then_inc(vec_landed, 16)
            for j in range(3):
                sp.dma_start(vstage[0:88, 2 + j, :], A["w_conv"][0, j].rearrange("(a b) -> a b", b=P)).then_inc(vec_landed, 16)
            sp.dma_start(vstage[0:88, 5, :], A["b_conv"][0].rearrange("(a b) -> a b", b=P)).then_inc(vec_landed, 16)
            sp.dma_start(xs[:, :, :], xv).then_inc(x_landed, 16)
            for first, trips, lo in ((4, 3, 0), (16, 4, D)):
                with sp.Fori(0, trips) as i:
                    for j in range(4):
                        sp.wait_ge(ada_used, i * 4 + (first + j - 3))
                        sp.dma_start(start_ring[:, j, :],
                                     ada_src[0][:, bass.ds(i * 4 + (first % 16 + j), 1), lo:lo + D]
                                     .rearrange("p a n -> p (a n)")).then_inc(start_landed[j], 16)

            cols = [None, C_QI, C_QI + NC, C_MQ, C_KA, C_QA, C_QA + NC]
            t = 0
            for c in range(7):
                for k in range(8):
                    wk = W["w_in"][:, 2 * k:2 * k + 2, :]
                    if c:
                        tile_in(t, 0, wk[:, :, cols[c]:cols[c] + NC])
                    else:
                        sp.dma_start(raw[:, t, :, 0:432], wk[:, :, C_GATE - 432:C_GATE]).then_inc(raw_landed[t], 16)
                        sp.dma_start(raw[:, t, :, 432:512], wk[:, :, C_KI:C_KI + 80]).then_inc(raw_landed[t], 16)
                    t += 1
            for c in range(4):
                lo = min(2 * MD * c, 8 * MD - NC)
                for k in range(2):
                    tile_in(t, 0, W["w_mq_up"][:, 2 * k:2 * k + 2, lo:lo + NC])
                    t += 1
            for c in range(4):
                tile_in(t, 0, W["w_mkv_up"][:, 0:2, c * NC:(c + 1) * NC])
                t += 1

            def cut(w, j, c, base=0, first=0):
                return w[:, first + 2 * j:first + 2 * j + 2, bass.ds(c * NC + base, NC)]

            def stream(name, w, base=0, first=0):
                t0, _, n, k = PHASES[name]
                assert k == 8
                with sp.Fori(0, n) as i:
                    for j in range(8):
                        tile_in(t0 + j, i * 8, cut(w, j, i, base, first))

            stream("gate", W["w_in"], C_GATE)
            with sp.Fori(0, 4) as i:
                for j in range(8):
                    tile_in(PHASES["proj"][0] + j, i * 8, cut(W["w_pa"] if j < 4 else W["w_pb"], j % 4, i))
            stream("wo", W["w_o"])
            for part, pairs in enumerate(PAIRS):
                with sp.Fori(0, pairs) as i:
                    for j in range(16):
                        tile_in(PHASES[f"up{part}"][0] + j, i * 16,
                                cut(W["w_up"], j % 8, i, 4 * part * NC + (D_FF if j >= 8 else 0)))
                if part < 2:
                    stream(f"down{part}", W["w_down"], 0, 16 * part)
            t = PHASES["down2"][0]
            for c in range(4):
                for j in range(6):
                    tile_in(t, 0, W["w_down"][:, 32 + 2 * j:34 + 2 * j, c * NC:(c + 1) * NC])
                    t += 1
            with sp.Fori(0, 4) as i:
                for j in range(8):
                    tile_in(PHASES["pin"][0] + j, i * 8, cut(W["pool_w_in_2"], j, i))
            t = PHASES["gp0"][0]
            for n in range(4):
                for j in range(8):
                    tile_in(t, 0, W["pool_w_in_2"][:, 2 * j:2 * j + 2, D + n * NC:D + (n + 1) * NC])
                    t += 1
                for j in range(2):
                    tile_in(t, 0, w_grp[:, n, 2 * j:2 * j + 2, :])
                    t += 1
            stream("pout", W["pool_w_out_2"])
            for h in range(2):
                sp.wait_ge(outD, h + 1)
                sp.dma_start(outv[:, 0, h * D // 2:(h + 1) * D // 2], X[:, 0, h * D // 2:(h + 1) * D // 2]).then_inc(storedS, 16)
            sp.wait_ge(storedS, 32)

        @block.gpsimd
        def _(pool):
            nc.gpsimd.memset(ones[:, :], 1.0).then_inc(ones_ready, 1)

            def ada_in(n, off=0):
                src, reg = REGION_SRC[n // 16]
                if n >= 34:
                    pool.wait_ge(ada_used, n - 1 + off)
                tile = ada_src[src][:, bass.ds(off + n % 16, 1), reg * D:(reg + 1) * D].rearrange("p a n -> p (a n)")
                pool.dma_start(ada_ring[:, n % 2, :], tile).then_inc(ada_landed[n % 2], 16)

            ada_in(32)
            ada_in(33)
            pool.wait_ge(nrm_lo, 8)
            pool.dma_start(causal[:, :, :], A["causal"]).then_inc(att_landed, 16)
            col = 0
            for name, n in (("g_qa", HD), ("g_ka", HD), ("g_qm", MD), ("g_km", MD)):
                pool.dma_start(gains[:, col:col + n], A[name].broadcast_to([P, n])).then_inc(att_landed, 16)
                col += n
            pool.dma_start(posf[:, 0, :].bitcast(I32), A["positions"].rearrange("a (t p) -> p (a t)", p=P),
                           allow_slow_non_contiguous=True).then_inc(att_landed, 16)
            pool.dma_start(tabs[:, 1, 0, :], A["inv_freq"].broadcast_to([P, 56])).then_inc(att_landed, 16)
            for n in range(34, 48):
                ada_in(n)
            with pool.Fori(0, 8) as i:
                for j in range(2):
                    ada_in(16 * SC_F + j, i * 2)
            with pool.Fori(0, 4) as i:
                for j in range(2):
                    ada_in(16 * GT_A + j, i * 2)
            pool.wait_ge(o_lo, 4)
            pool.wait_ge(gstage_free, 16 * 9)
            pool.dma_start(U[:, 0, :, :], gates_dram[0]).then_inc(gate_loaded[0], 16)
            pool.dma_start(U[:, 1, :, :], gates_dram[4]).then_inc(gate_loaded[1], 16)
            pool.dma_start(gt[:, :], A["b_ada"][:, 2 * D:3 * D].broadcast_to([P, D])).then_inc(bias_landed, 16)
            pool.dma_start(X[:, :, :], xv).then_inc(res_landed, 16)
            _, c0, _, _ = PHASES["proj"]
            with pool.Fori(0, 3) as i:
                for cc in range(2):
                    ada_in(16 * GT_A + 8 + cc, i * 2)
                    pool.wait_ge(chunk_evac, i * 2 + (c0 + cc + 1))
                    pool.dma_start(U[:, cc, :, :], gates_dram[bass.ds(i + (4 * cc + 1), 1), :, :, :]
                                   .rearrange("a p t n -> p (a t) n")).then_inc(gate_loaded[cc], 16)
            for n in (14, 15):
                ada_in(16 * GT_A + n)
            pool.wait_ge(x_updated, 4)
            pool.dma_start(gt[:, :], A["b_ada"][:, 5 * D:6 * D].broadcast_to([P, D])).then_inc(bias_landed, 16)
            for r in (GT_F, SH_2, SC_2, GT_2):
                with pool.Fori(0, 8) as i:
                    for j in range(2):
                        ada_in(16 * r + j, i * 2)
            pool.wait_ge(f_lo, sum(PAIRS))
            pool.dma_start(cv[:, :, :], A["pool_matrix"]).then_inc(pmat_landed, 16)
            pool.wait_ge(x_updated, 16)
            pool.dma_start(gt[:, :], A["b_mod_2"][:, 2 * D:3 * D].broadcast_to([P, D])).then_inc(bias_landed, 16)
            pool.wait_ge(p_turned, 8)
            pool.dma_start(fgain, A["final_norm_g_2"].rearrange("(a n) -> a n", a=1).broadcast_to([P, D])).then_inc(fg_landed, 16)

        @block.scalar
        def _(act):
            def split(tb, off=0):
                if tb >= TILES:
                    return
                act.wait_ge(raw_landed[tb % RAW], 16 * (tb // RAW + 2) + off * 2)
                if tb >= RING:
                    act.wait_ge(tile_used, tb - RING + 1 + off)
                nc.scalar.copy(whi[:, tb % RING, :, :], raw[:, tb % RAW, :, :]).then_inc(hi_ready, 1)

            norms = [0]

            def sqrt_of_norm():
                norms[0] += 1
                act.wait_ge(ms_ready, norms[0])
                nc.scalar.activation(stat[:, 1, 0:TOK], stat[:, 0, 0:TOK], ACT.Sqrt).then_inc(sqrt_ready, 1)

            pairs = [0]

            def norm_hi(tmpv, hi, k0, npair):
                for b in range(npair):
                    act.wait_ge(nrm_evac, pairs[0] + 1)
                    nc.scalar.copy(hi[:, k0 + 2 * b:k0 + 2 * b + 2, :].rearrange("p a n -> p (a n)"),
                                   tmpv[:, pairs[0] % 2, :]).then_inc(nrm_hi, 1)
                    pairs[0] += 1

            def chunk_of(name, c, i=0, per=1):
                t0, c0, _, k = PHASES[name]
                act.wait_ge(tile_used, i * (per * k) + (t0 + (c + 1) * k))
                return acc[(c0 + c) % 2]

            act.wait_ge(consts_landed, 32)
            nc.scalar.activation(cact[:, :, :], craw[:, :, :], ACT.Silu).then_inc(c_ready, 1)
            act.wait_ge(x_landed, 16)
            act.wait_ge(ssq_cleared, 1)
            for t in range(TOK):
                if t:
                    act.wait_ge(xsq_done, t)
                nc.scalar.activation(sqdump[:, :], xs[:, t, :], ACT.Square, accum_out=ssq[:, t, 0:1]).then_inc(xsq_done, 1)
            sqrt_of_norm()
            for t in range(RING):
                split(t)
            norm_hi(start_tmp, sa_hi, 0, 8)

            order = Order(act, act_order)
            done = [RING]

            def ahead(n):
                while done[0] < n:
                    split(done[0])
                    done[0] += 1

            def evac_in(c):
                pair = chunk_of("in", c)
                for t in range(TOK):
                    ps = pair[t][:, :]
                    if c == 0:
                        dst, ps = pm[:, t, :], pair[t][:, 112:512]
                    elif c < 3:
                        dst, ps = qi[:, t, 8 * (c - 1):8 * c, :], ps.rearrange("p (h d) -> p h d", d=ID)
                    elif c == 3:
                        dst = mql[:, t, :]
                    elif c == 4:
                        dst = pkv[:, t, :]
                    else:
                        dst = pq[:, :, :].rearrange("p (h t) d -> p t h d", t=TOK)[:, t, 4 * (c - 5):4 * (c - 4), :]
                        ps = ps.rearrange("p (h d) -> p h d", d=HD)
                    last = nc.scalar.copy(dst, ps)
                last.then_inc(chunk_evac, 1)
                act.wait_ge(chunk_evac, c + 1)

            def square_sum(v, dst, at):
                return nc.scalar.activation(dump[:, at:at + v.shape[-1]], v, ACT.Square, accum_out=dst)

            ahead(12)
            evac_in(0)
            for t in range(TOK):
                order.link(square_sum(pm[:, t, 0:KVLORA], rstd[:, TOK + t:TOK + t + 1], 0))
            act.wait_ge(ang_ready, 1)
            nc.scalar.activation(tabs[:, :, :, :], tabs[:, :, :, :], ACT.Sin).then_inc(tab_ready, 1)
            ahead(20)
            evac_in(1)
            ahead(28)
            evac_in(2)
            ahead(32)
            for b in range(4):
                act.wait_ge(qi_turned, b + 1)
                nc.scalar.copy(qiT[:, 2 * b:2 * b + 2, :].rearrange("p a n -> p (a n)"), M[b][:, :]).then_inc(qi_evac, 1)
            ahead(33)
            act.wait_ge(qi_turned, 5)
            nc.scalar.copy(kiT[:, :], M[0][:, 0:S]).then_inc(qi_evac, 1)
            ahead(36)
            evac_in(3)
            for t in range(TOK):
                order.link(square_sum(mql[:, t, :], rstd[:, t:t + 1], 0))
            nc.scalar.copy(warm[:, :], rstd[:, 0:1]).then_inc(xsq_done, 1)
            ahead(38)
            norms[0] += 1
            act.wait_ge(ms_ready, norms[0])
            nc.scalar.activation(stat[:, 1, :], stat[:, 0, :], ACT.Sqrt).then_inc(sqrt_ready, 1)
            ahead(42)
            norm_hi(lat_tmp, lat_hi, 0, 3)
            ahead(44)
            evac_in(4)
            for g in range(GROUPS):
                for t in range(TOK):
                    last = square_sum(pkv[:, t, g * HD:(g + 1) * HD], hstat[:, 0, 2 * t + g:2 * t + g + 1], (2 * g + t) * HD)
            order.link(last)
            for b in range(4):
                ahead(46 + 2 * b)
                if b == 3:
                    evac_in(5)
                for h in range(4 * b, 4 * b + 4):
                    act.wait_ge(dots_ready, h + 1)
                    if h >= 4:
                        act.wait_ge(relu_used, h - 3)
                    nc.scalar.activation(tmp[:, 512 * (h % 4):512 * (h % 4 + 1)], M[h % 4][:, :], ACT.Relu).then_inc(relu_ready, 1)

            def query_squares(half):
                for t in range(TOK):
                    for h in range(4):
                        a = 8 * half + 2 * h + t
                        last = square_sum(pq[:, a, :], hstat[:, 0, 4 + a:5 + a], h * HD)
                    order.link(last)

            query_squares(0)
            ahead(58)
            act.wait_ge(hs_ms, 1)
            nc.scalar.activation(hstat[:, 1, 0:4], hstat[:, 0, 0:4], ACT.Sqrt).then_inc(hs_sqrt, 1)
            ahead(60)
            evac_in(6)
            query_squares(1)
            t0 = PHASES["mq"][0]
            for c in range(4):
                ahead(t0 + 2 * c + 2 + RING)
                if c == 1:
                    act.wait_ge(k_turned, 1)
                    nc.scalar.copy(kT[:, :, :].rearrange("p a n -> p (a n)"), M[0][:, :]).then_inc(k_evac, 1)
                pair = chunk_of("mq", c)
                skip = 2 * MD * c - min(2 * MD * c, 8 * MD - NC)
                for t in range(TOK):
                    last = nc.scalar.copy(mq[:, :, :].rearrange("p (h t) d -> p t h d", t=TOK)[:, t, 2 * c:2 * c + 2, :],
                                          pair[t][:, skip:skip + 2 * MD].rearrange("p (h d) -> p h d", d=MD))
                last.then_inc(chunk_evac, 1)
                act.wait_ge(chunk_evac, 8 + c)
                for b in range(2):
                    for a in (4 * c + 2 * b, 4 * c + 2 * b + 1):
                        last = square_sum(mq[:, a, :], hstat[:, 0, 20 + a:21 + a], (a % 2) * MD)
                    order.link(last)
            t0 = PHASES["mkv"][0]
            for c in range(4):
                ahead(t0 + c + 1 + RING)
                pair = chunk_of("mkv", c)
                for t in range(TOK):
                    last = nc.scalar.copy(mkv[:, :, :].rearrange("p (h t) d -> p t h d", t=TOK)[:, t, 2 * c:2 * c + 2, :],
                                          pair[t][:, :].rearrange("p (h d) -> p h d", d=256))
                last.then_inc(chunk_evac, 1)
                act.wait_ge(chunk_evac, 12 + c)
                for a in range(4 * c, 4 * c + 4):
                    last = square_sum(mkv[:, a, 0:NOPE], hstat[:, 0, 36 + a:37 + a], (a % 4) * NOPE)
                order.link(last)
            for t in range(TOK):
                last = square_sum(pm[:, t, KVLORA:KVLORA + MROT], hstat[:, 0, 52 + t:53 + t], t * MROT)
            order.link(last)
            nc.scalar.copy(warm[:, :], hstat[:, 0, 52:53]).then_inc(hs_ready, 1)
            act.wait_ge(hs_ms, 2)
            nc.scalar.activation(hstat[:, 1, 4:52], hstat[:, 0, 4:52], ACT.Sqrt).then_inc(hs_sqrt, 1)
            act.sem_inc(gstage_free, 16)

            def gates_out(c, i):
                _, c0, _, _ = PHASES["gate"]
                pair = chunk_of("gate", c, i, 2)
                act.wait_ge(gstage_free, i * 32 + 16 * (c + 1))
                for t in range(TOK):
                    last = nc.scalar.activation(gstage[:, t, :], pair[t][:, :], ACT.Sigmoid)
                last.then_inc(chunk_evac, 1)
                act.wait_ge(chunk_evac, i * 2 + (c0 + c + 1))
                act.dma_start(gates_dram[bass.ds(i * 2 + c, 1), :, :, :].rearrange("a p t n -> p (a t) n"),
                              gstage[:, :, :]).then_inc(gstage_free, 16)

            def softmax(pr, s, h, maxed, exped, probs):
                act.wait_ge(maxed, 2 * h + 1)
                for t in range(TOK):
                    last = nc.scalar.activation(pr[:, s, t, :], pr[:, s, t, :], ACT.Exp, bias=smax[:, s, 0, t:t + 1],
                                                accum_out=smax[:, s, 1, t:t + 1])
                last.then_inc(exped, 1)

            def normalise(pr, s, h, maxed, probs):
                act.wait_ge(maxed, 2 * h + 2)
                for t in range(TOK):
                    last = nc.scalar.activation(pr[:, s, t, :], pr[:, s, t, :], ACT.Copy, scale=smax[:, s, 1, t:t + 1])
                last.then_inc(probs, 1)

            with act.Fori(0, 2) as i:
                nc.scalar.copy(vA[:, :, :], pkv[:, :, bass.ds(i * HD + 256, HD)]).then_inc(A_v, 1)
                for c in range(2):
                    tb, off, h = PHASES["gate"][0] + 8 * c + RING, i * 16, i * 4 + 2 * c
                    split(tb, off)
                    act.wait_ge(A_turned, h + 1)
                    nc.scalar.copy(qTA[:, 0, :], M[0][:, 0:S]).then_inc(A_qT, 1)
                    split(tb + 1, off)
                    split(tb + 2, off)
                    act.wait_ge(A_turned, h + 2)
                    nc.scalar.copy(qTA[:, 1, :], M[0][:, S:2 * S]).then_inc(A_qT, 1)
                    softmax(prA, 0, h, A_maxed, A_exp, A_probs)
                    split(tb + 3, off)
                    normalise(prA, 0, h, A_maxed, A_probs)
                    softmax(prA, 1, h + 1, A_maxed, A_exp, A_probs)
                    split(tb + 4, off)
                    normalise(prA, 1, h + 1, A_maxed, A_probs)
                    act.wait_ge(A_pT, h + 1)
                    nc.scalar.copy(pTA[:, 0, :], M[3][:, 0:384]).then_inc(A_pT_evac, 1)
                    split(tb + 5, off)
                    act.wait_ge(A_pT, h + 2)
                    nc.scalar.copy(pTA[:, 1, :], M[0][:, 0:384]).then_inc(A_pT_evac, 1)
                    for s in range(2):
                        act.wait_ge(A_o, h + s + 1)
                        nc.scalar.copy(oTA[:, bass.ds(h + s, 1), :].rearrange("p a n -> p (a n)"), M[1 + s][:, 0:S]).then_inc(A_o_evac, 1)
                        split(tb + 6 + s, off)
                    gates_out(c, i)
            act.wait_ge(A_o, H)
            with act.Fori(0, 2) as i:
                for c in range(2):
                    tb, off, h = PHASES["gate"][0] + 32 + 8 * c + RING, i * 16, i * 4 + 2 * c
                    nc.scalar.copy(vB[:, :, :, :].rearrange("p s t d -> p (s t) d"), mkv[:, bass.ds(h * 2, 4), NOPE:NOPE + MV]).then_inc(B_v, 1)
                    split(tb, off)
                    act.wait_ge(B_turned, h + 1)
                    nc.scalar.copy(nT[:, 0, :, :].rearrange("p a n -> p (a n)"), M[0][:, :]).then_inc(B_nT, 1)
                    split(tb + 1, off)
                    split(tb + 2, off)
                    act.wait_ge(B_turned, h + 2)
                    nc.scalar.copy(nT[:, 1, :, :].rearrange("p a n -> p (a n)"), M[2][:, :]).then_inc(B_nT, 1)
                    softmax(prB, 0, h, B_maxed, B_exp, B_probs)
                    split(tb + 3, off)
                    normalise(prB, 0, h, B_maxed, B_probs)
                    softmax(prB, 1, h + 1, B_maxed, B_exp, B_probs)
                    split(tb + 4, off)
                    normalise(prB, 1, h + 1, B_maxed, B_probs)
                    act.wait_ge(B_pT, h + 1)
                    nc.scalar.copy(pTB[:, 0, :], M[0][:, 0:384]).then_inc(B_pT_evac, 1)
                    split(tb + 5, off)
                    act.wait_ge(B_pT, h + 2)
                    nc.scalar.copy(pTB[:, 1, :], M[2][:, 0:384]).then_inc(B_pT_evac, 1)
                    for s in range(2):
                        act.wait_ge(B_o, h + s + 1)
                        nc.scalar.copy(oTB[:, bass.ds(h + s, 1), 0:S].rearrange("p a n -> p (a n)"), M[1 + 2 * s][:, 0:S]).then_inc(B_o_evac, 1)
                        split(tb + 6 + s, off)
                    gates_out(4 + c, i)

            act.wait_ge(B_o_evac, H)
            for b in range(2):
                nc.scalar.copy(sa_hi[:, 4 * b:4 * b + 4, :], oTA[:, 4 * b:4 * b + 4, :]).then_inc(o_hi, 1)
            for b in range(2):
                nc.scalar.copy(sa_hi[:, 8 + 4 * b:12 + 4 * b, :], oTB[:, 4 * b:4 * b + 4, 0:S]).then_inc(o_hi, 1)

            def merged_hi(n):
                for q in range(2):
                    act.wait_ge(m_turned, n * 2 + (q + 1))
                    nc.scalar.copy(sb_hi[:, bass.ds(n * 4 + 2 * q, 2), :], bank2(M[q])).then_inc(m_hi, 1)

            t0 = PHASES["proj"][0] + RING
            for j in range(8):
                split(t0 + j)
            with act.Fori(0, 3) as i:
                for j in range(8):
                    split(t0 + 8 + j, i * 8)
                    if j == 3:
                        merged_hi(i)
            merged_hi(3)

            def squares(name, c, i=0):
                act.wait_ge(x_updated, i * 2 + (UPDATES[name] + c + 1))
                for t in range(TOK):
                    last = nc.scalar.activation(U[:, 0, t, :], X[:, t, bass.ds(i * 2 * NC + c * NC, NC)], ACT.Square,
                                                accum_out=ssq[:, t, bass.ds(i * 2 + c, 1)])
                last.then_inc(xsq_done, 1)

            def out_product(name):
                t0, _, _, k = PHASES[name]
                with act.Fori(0, 2) as i:
                    for c in range(2):
                        for j in range(8):
                            split(t0 + 8 * c + j + RING, i * 16)
                        squares(name, c, i)

            nc.scalar.activation(warm[:, :], ident[:, 0:1], ACT.Sqrt)
            out_product("wo")
            sqrt_of_norm()
            norm_hi(gv2, sa_hi, 0, 8)

            def conv_base(side, pg):
                for q in range(2):
                    act.wait_ge(u_turned, pg * 4 + (2 * side + q + 1))
                    for b in range(2):
                        col = pg * 4 + (44 * side + 2 * q + b)
                        last = nc.scalar.activation(cv[:, 4 * side + 2 * q + b, :], M[2 * side + q][:, b * S:(b + 1) * S],
                                                    ACT.Identity, bias=cvec[:, 3, bass.ds(col, 1)], scale=cvec[:, 2, bass.ds(col, 1)])
                last.then_inc(cv_based, 1)

            def ffn_hi(pg, pl):
                act.wait_ge(gv_ready, pg + 1)
                nc.scalar.copy(sb_hi[:, bass.ds(pl * 4, 4), :], gv[:, :, :]).then_inc(f_hi, 1)

            def up_pair(part, i, shift, first):
                t0 = PHASES[f"up{part}"][0] + 16 * shift
                off = i * 16
                pl = i + shift
                pg = i + (shift + 4 * part)
                for j in range(4):
                    split(t0 + RING + j, off)
                if not first:
                    conv_base(1, i + (shift + 4 * part - 1))
                split(t0 + RING + 4, off)
                split(t0 + RING + 5, off)
                if not first:
                    ffn_hi(i + (shift + 4 * part - 1), i + (shift - 1))
                split(t0 + RING + 6, off)
                split(t0 + RING + 7, off)
                pair = chunk_of(f"up{part}", 2 * shift, i, 2)
                for t in range(TOK):
                    last = nc.scalar.copy(U[:, 0, t, :], pair[t][:, :])
                last.then_inc(chunk_evac, 1)
                for j in range(4):
                    split(t0 + RING + 8 + j, off)
                conv_base(0, pg)
                split(t0 + RING + 12, off)
                split(t0 + RING + 13, off)
                act.wait_ge(cv_done, pg * 2 + 1)
                nc.scalar.activation(cv[:, 0:4, :], cv[:, 0:4, :], ACT.Silu).then_inc(silu_done, 1)
                split(t0 + RING + 14, off)
                split(t0 + RING + 15, off)
                pair = chunk_of(f"up{part}", 2 * shift + 1, i, 2)
                for t in range(TOK):
                    last = nc.scalar.copy(U[:, 1, t, :], pair[t][:, :])
                last.then_inc(chunk_evac, 1)

            for part, n in enumerate(PAIRS):
                up_pair(part, 0, 0, True)
                with act.Fori(0, n - 1) as i:
                    up_pair(part, i, 1, False)
                t0, _, _, k = PHASES[f"down{part}"]
                for c in range(4):
                    for j in range(k):
                        if c == 0 and j == k - 4:
                            conv_base(1, 4 * part + n - 1)
                        if c == 0 and j == k - 2:
                            ffn_hi(4 * part + n - 1, n - 1)
                        split(t0 + c * k + j + RING)
                    if part == 2:
                        if c == 0:
                            nc.scalar.activation(warm[:, :], ident[:, 0:1], ACT.Sqrt)
                        squares("down2", c)

            sqrt_of_norm()
            norm_hi(gv2, sa_hi, 0, 8)

            def pooled_hi(c):
                for q in range(2):
                    act.wait_ge(p_turned, 2 * c + q + 1)
                    nc.scalar.copy(sb_hi[:, 4 * c + 2 * q:4 * c + 2 * q + 2, :], bank2(M[2 * (c % 2) + q])).then_inc(p_hi, 1)

            t0 = PHASES["pin"][0] + RING
            for c in range(4):
                for j in range(4):
                    split(t0 + 8 * c + j)
                if c:
                    pooled_hi(c - 1)
                for j in range(4, 8):
                    split(t0 + 8 * c + j)
                pair = chunk_of("pin", c)
                for t in range(TOK):
                    last = nc.scalar.copy(U[:, c % 2, t, :], pair[t][:, :])
                last.then_inc(chunk_evac, 1)
            act.wait_ge(ada_used, 144)

            def y_high(n):
                act.wait_ge(y_scaled, n + 1)
                nc.scalar.copy(sb_hi[:, 4 * n:4 * n + 4, :], gv[:, :, :]).then_inc(y_hi, 1)

            for n in range(4):
                t0 = PHASES[f"gp{n}"][0] + RING
                for j in range(4):
                    split(t0 + j)
                if n == 0:
                    pooled_hi(3)
                for j in range(4, 8):
                    split(t0 + j)
                if n:
                    y_high(n - 1)
                pair = chunk_of(f"gp{n}", 0)
                for t in range(TOK):
                    last = nc.scalar.activation(ada_ring[:, t, n * NC:(n + 1) * NC], pair[t][:, :], ACT.Silu)
                last.then_inc(chunk_evac, 1)
                split(t0 + 8)
                split(t0 + 9)
            t0 = PHASES["pout"][0] + RING
            for c in range(4):
                for j in range(8):
                    if c == 0 and j == 6:
                        y_high(3)
                    split(t0 + 8 * c + j)
                if c == 0:
                    nc.scalar.activation(warm[:, :], ident[:, 0:1], ACT.Sqrt)
                squares("pout", c)
            sqrt_of_norm()
            act.wait_ge(fg_applied, 4)
            act.wait_ge(diag_ready, 5)
            for h in range(2):
                half = slice(h * D // 2, (h + 1) * D // 2)
                nc.scalar.activation(X[:, 1, half], X[:, 1, half], ACT.Copy, scale=rstd[:, 1:2]).then_inc(outA, 1)
            for h in range(2):
                half = slice(h * D // 2, (h + 1) * D // 2)
                act.wait_ge(outA, h + 1)
                act.dma_start(outv[:, 1, half], X[:, 1, half]).then_inc(storedA, 16)
            act.wait_ge(storedA, 32)

        @block.vector
        def _(dve):
            V = nc.vector
            order = Order(dve, dve_order)
            link = order.link

            def split(tb, off=0):
                if tb >= TILES:
                    return
                dve.wait_ge(hi_ready, tb + 1 + off)
                V.tensor_tensor(wlo[:, tb % RING, :, :], raw[:, tb % RAW, :, :], whi[:, tb % RING, :, :].bitcast(F32),
                                ALU.subtract).then_inc(lo_ready, 1)

            def ada_begin(r):
                if r:
                    kind, count = summed(r - 1)
                    dve.wait_ge(cols_summed if kind == "cols" else rows_summed, count)
                link(V.memset(ada_acc[:, :], 0.0))

            def ada(n, off=0):
                src = REGION_SRC[n // 16][0]
                if n < 32:
                    dve.wait_ge(start_landed[n % 4], 16 * (n // 4 + 1) + off * 4)
                    tile = start_ring[:, n % 4, :]
                else:
                    dve.wait_ge(ada_landed[n % 2], 16 * ((n - 32) // 2 + 1) + off * 8)
                    tile = ada_ring[:, n % 2, :]
                if n:
                    dve.wait_ge(ada_used, n + off)
                V.scalar_tensor_tensor(out=ada_acc[:, :], in0=tile, scalar=cact[:, src, bass.ds(off + n % 16, 1)],
                                       in1=ada_acc[:, :], op0=ALU.mult, op1=ALU.add).then_inc(ada_used, 1)

            def shift_ready(r, v):
                dve.wait_ge(cols_summed, summed(r)[1])
                V.tensor_tensor(mod_b[:, :], M[0][:, 0:16], vecs[:, v:v + 16], ALU.add).then_inc(mod_ready, 1)

            def scale_ready(r, v, gain=None):
                dve.wait_ge(cols_summed, summed(r)[1])
                last = V.scalar_tensor_tensor(out=mod_s[:, :], in0=M[0][:, 0:16], scalar=1.0, in1=vecs[:, v:v + 16],
                                              op0=ALU.add, op1=ALU.add)
                if gain is not None:
                    link(last)
                    last = V.tensor_tensor(mod_s[:, :], mod_s[:, :], vecs[:, gain:gain + 16], ALU.mult)
                last.then_inc(mod_ready, 1)

            def gate_ready(r, half, b):
                k = ROWS.index(r)
                dve.wait_ge(bias_landed, 16 * (k + 1))
                dve.wait_ge(rows_summed, 2 * k + half + 1)
                for n in range(2):
                    cols = slice((2 * half + n) * NC, (2 * half + n + 1) * NC)
                    last = V.tensor_tensor(gt[:, cols], M[b + n][:, :], gt[:, cols], ALU.add)
                last.then_inc(gt_ready, 1)

            norms = [0]

            def diagonals(to, col):
                for t in range(TOK):
                    last = V.tensor_scalar(to[:, t, :], ident[:, :], rstd[:, col + t:col + t + 1], None, ALU.mult)
                return last

            def norm_x(squares):
                dve.wait_ge(xsq_done, squares)
                link(V.reduce_sum(rstd[:, 0:TOK], ssq[:, :, :], AX))
                V.tensor_scalar(stat[:, 0, 0:TOK], rstd[:, 0:TOK], 1.0 / D, EPS, ALU.mult, ALU.add).then_inc(ms_ready, 1)
                norms[0] += 1
                dve.wait_ge(sqrt_ready, norms[0])
                link(V.reciprocal(rstd[:, 0:TOK], stat[:, 1, 0:TOK]))
                diagonals(diag, 0).then_inc(diag_ready, 1)

            pairs = [0]

            def norm_lo(tmpv, hi, lo, k0, npair, scale, bias):
                def low(b, p):
                    dve.wait_ge(nrm_hi, p + 1)
                    V.tensor_tensor(lo[:, k0 + 2 * b:k0 + 2 * b + 2, :].rearrange("p a n -> p (a n)"), tmpv[:, p % 2, :],
                                    hi[:, k0 + 2 * b:k0 + 2 * b + 2, :].rearrange("p a n -> p (a n)").bitcast(F32),
                                    ALU.subtract).then_inc(nrm_lo, 1)

                p0 = pairs[0]
                for b in range(npair):
                    p = p0 + b
                    dve.wait_ge(nrm_turned, p + 1)
                    if b >= 2:
                        dve.wait_ge(nrm_lo, p - 1)
                    for kk in range(2):
                        k = 2 * b + kk
                        if bias is None:
                            last = V.tensor_scalar(tmpv[:, p % 2, kk * S:(kk + 1) * S], M[b % 4][:, kk * S:(kk + 1) * S],
                                                   scale[:, k:k + 1], None, ALU.mult)
                        else:
                            last = V.tensor_scalar(tmpv[:, p % 2, kk * S:(kk + 1) * S], M[b % 4][:, kk * S:(kk + 1) * S],
                                                   scale[:, k:k + 1], bias[:, k:k + 1], ALU.mult, ALU.add)
                    last.then_inc(nrm_evac, 1)
                    if b:
                        low(b - 1, p - 1)
                low(npair - 1, p0 + npair - 1)
                pairs[0] += npair
                dve.wait_ge(nrm_lo, pairs[0])

            V.memset(ssq[:, :, :], 0.0).then_inc(ssq_cleared, 1)
            ada_begin(SH_A)
            dve.wait_ge(c_ready, 1)
            ada(0)
            ada(1)
            ada(2)
            ada(3)
            with dve.Fori(0, 3) as i:
                for j in range(4):
                    ada(4 + j, i * 4)
            dve.wait_ge(vec_turned, 1)
            V.tensor_copy(vecs[:, :], M[1][:, 0:NVEC]).then_inc(vec_ready, 1)
            dve.wait_ge(vec_turned, 2)
            V.tensor_copy(cvec[:, :, :].rearrange("p a n -> p (a n)"), M[2][:, 0:352]).then_inc(vec_ready, 1)
            dve.wait_ge(vec_ready, 2)
            shift_ready(SH_A, V_SHA)
            ada_begin(SC_A)
            with dve.Fori(0, 4) as i:
                for j in range(4):
                    ada(16 + j, i * 4)
            norm_x(TOK)
            scale_ready(SC_A, V_SCA, V_GATTN)
            dve.wait_ge(mod_ready, 2)
            for t in range(RING):
                split(t)
            norm_lo(start_tmp, sa_hi, sa_lo, 0, 8, mod_s, mod_b)

            ada_begin(SH_F)
            done = [RING]

            def ahead(n, adas=0):
                while done[0] < n:
                    split(done[0])
                    done[0] += 1
                for _ in range(adas):
                    ada(ada_next[0])
                    ada_next[0] += 1

            ada_next = [16 * SH_F]

            def rope(v, tab, half, tmpv, axis, shape, done=None):
                co, si = (tabs[:, a, :, tab:tab + half].unsqueeze(axis).broadcast_to([P, *shape, half]) for a in range(2))
                n = shape[0] * shape[1] * half
                a, b, c, d = (tmpv[:, k * n:(k + 1) * n].rearrange("p (x y n) -> p x y n", x=shape[0], y=shape[1]) for k in range(4))
                v1, v2 = v[:, :, :, 0:half], v[:, :, :, half:2 * half]
                V.tensor_tensor(a, v1, co, ALU.mult)
                V.tensor_tensor(b, v2, si, ALU.mult)
                V.tensor_tensor(c, v2, co, ALU.mult)
                link(V.tensor_tensor(d, v1, si, ALU.mult))
                V.tensor_tensor(v1, a, b, ALU.subtract)
                last = V.tensor_tensor(v2, c, d, ALU.add)
                if done is None:
                    link(last)
                else:
                    last.then_inc(done, 1)

            ahead(12, 2)
            dve.wait_ge(att_landed, 16 * 7)
            link(V.tensor_copy(posf[:, 1, :], posf[:, 0, :].bitcast(I32)))
            for t in range(TOK):
                last = V.tensor_scalar(tabs[:, 0, t, :], tabs[:, 1, 0, :], posf[:, 1, t:t + 1], None, ALU.mult)
            link(last)
            link(V.tensor_copy(tabs[:, 1, :, :], tabs[:, 0, :, :]))
            kv = tmp[:, 0:224].rearrange("p (a t n) -> p a t n", a=2, t=TOK)
            for a, turn in ((0, 0.25), (1, 0.0)):
                link(V.tensor_scalar(kv[:, a], tabs[:, a, :, :], 1.0 / TWO_PI, turn, ALU.mult, ALU.add))
            link(V.tensor_scalar(kv, kv, ROUND, None, ALU.add))
            link(V.tensor_scalar(kv, kv, ROUND, None, ALU.subtract))
            flat = tabs[:, :, :, :].rearrange("p a t n -> p (a t n)")
            for part in (PI_HI, PI_MID, PI_LO):
                link(V.scalar_tensor_tensor(out=flat, in0=tmp[:, 0:224], scalar=-part, in1=flat, op0=ALU.mult, op1=ALU.add))
            link(V.tensor_scalar(tabs[:, 0, :, :], tabs[:, 0, :, :], TWO_PI / 4, None, ALU.add))
            V.tensor_scalar(flat, flat, PI_IN, -PI_IN, ALU.min, ALU.max).then_inc(ang_ready, 1)
            ahead(14, 1)
            for n in (17, 20, 23, 26, 28):
                ahead(n, 1)
            ahead(29)
            dve.wait_ge(chunk_evac, 3)
            dve.wait_ge(tab_ready, 1)
            rope(qi, 16, 8, tmp, 2, (TOK, IH))
            ki = pm[:, :, 320:384]
            rope(ki.unsqueeze(2), 16, 8, tmp, 2, (TOK, 1))
            V.tensor_copy(kirep[:, :, 0:ID], ki)
            V.tensor_copy(kirep[:, :, ID:2 * ID], ki).then_inc(qi_roped, 1)
            link(V.tensor_scalar(pm[:, :, 384:400], pm[:, :, 384:400], float(IH * ID) ** -0.5, None, ALU.mult))
            ahead(32, 1)
            ahead(34, 1)
            ahead(37)
            dve.wait_ge(xsq_done, TOK + 1)
            V.tensor_scalar(stat[:, 0, 0:TOK], rstd[:, 0:TOK], 1.0 / QLORA, EPS, ALU.mult, ALU.add)
            V.tensor_scalar(stat[:, 0, TOK:2 * TOK], rstd[:, TOK:2 * TOK], 1.0 / KVLORA, EPS, ALU.mult, ALU.add).then_inc(ms_ready, 1)
            norms[0] += 1
            dve.wait_ge(sqrt_ready, norms[0])
            link(V.reciprocal(rstd[:, :], stat[:, 1, :]))
            diagonals(diag, 0)
            diagonals(diag2, TOK).then_inc(diag_ready, 1)
            ahead(40, 1)
            ahead(42)
            norm_lo(lat_tmp, lat_hi, lat_lo, 0, 3, vecs[:, V_GMQ:V_GMQ + 6], None)
            ahead(44, 1)
            for b in range(4):
                ahead(46 + 2 * b)
                for h in range(4 * b, 4 * b + 4):
                    dve.wait_ge(relu_ready, h + 1)
                    if h:
                        dve.wait_ge(relu_used, h)
                    for t in range(TOK):
                        r = tmp[:, 512 * (h % 4) + S * t:512 * (h % 4) + S * (t + 1)]
                        last = V.scalar_tensor_tensor(out=selbias[:, t, :], in0=r, scalar=pm[:, t, 384 + h:385 + h],
                                                      in1=causal[:, t, :] if h == 0 else selbias[:, t, :], op0=ALU.mult, op1=ALU.add)
                    last.then_inc(relu_used, 1)
            dve.wait_ge(relu_used, IH)
            for b in range(4):
                ahead(53 + b)
                for _ in range(TOPK // 16):
                    link(V.max(out=m8[:, :], in_=selbias[:, b // 2, :]))
                    link(V.match_replace(out=selbias[:, b // 2, :], in_to_replace=m8[:, :], in_values=selbias[:, b // 2, :], imm_value=TAKEN))
            link(V.tensor_scalar(selbias[:, :, :], selbias[:, :, :], TAKEN / 2, MASKED, ALU.is_gt, ALU.mult))
            link(V.tensor_tensor(selbias[:, :, :], selbias[:, :, :], causal[:, :, :], ALU.add))
            ahead(57)
            V.tensor_scalar(hstat[:, 0, 0:4], hstat[:, 0, 0:4], 1.0 / HD, EPS, ALU.mult, ALU.add).then_inc(hs_ms, 1)
            dve.wait_ge(hs_sqrt, 1)
            link(V.reciprocal(hstat[:, 1, 0:4], hstat[:, 1, 0:4]))
            for t in range(TOK):
                for g in range(GROUPS):
                    k = pkv[:, t, g * HD:(g + 1) * HD]
                    last = V.scalar_tensor_tensor(out=k, in0=k, scalar=hstat[:, 1, 2 * t + g:2 * t + g + 1], in1=gains[:, HD:2 * HD],
                                                  op0=ALU.mult, op1=ALU.mult)
            link(last)
            rope(pkv[:, :, 0:256].rearrange("p t (g d) -> p t g d", g=GROUPS), 0, 16, tmp, 2, (TOK, GROUPS), k_normed)
            dve.wait_ge(k_normed, 1)
            kr = pm[:, :, KVLORA:KVLORA + MROT]
            link(V.tensor_tensor(kbase[:, :, :], kr, gains[:, 448 + NOPE:640].unsqueeze(1).broadcast_to([P, TOK, MROT]), ALU.mult))
            rope(kbase[:, :, :].unsqueeze(2), 24, 32, tmp, 2, (TOK, 1), kbase_ready)
            dve.wait_ge(kbase_ready, 1)
            ahead(60, 1)
            ahead(62, 1)
            ahead(64, 1)
            ahead(66, 1)
            assert ada_next[0] == 16 * SC_F, ada_next[0]
            ahead(72)
            shift_ready(SH_F, V_SHF)
            ada_begin(SC_F)
            dve.wait_ge(hs_ready, 1)
            km = hstat[:, 0, 36:52].rearrange("p (h t) -> p h t", t=TOK)
            link(V.tensor_tensor(km, km, hstat[:, 0, 52:54].unsqueeze(1).broadcast_to([P, H, TOK]), ALU.add))
            V.tensor_scalar(hstat[:, 0, 4:20], hstat[:, 0, 4:20], 1.0 / HD, EPS, ALU.mult, ALU.add)
            V.tensor_scalar(hstat[:, 0, 20:52], hstat[:, 0, 20:52], 1.0 / MD, EPS, ALU.mult, ALU.add).then_inc(hs_ms, 1)
            dve.wait_ge(hs_sqrt, 2)
            link(V.reciprocal(hstat[:, 1, 4:52], hstat[:, 1, 4:52]))

            def head_rstd(i, at):
                return hstat[:, 1, bass.ds(i * 8 + at, 1)]

            def row(v, i, at, width):
                return v[:, bass.ds(i * 8 + at, 1), 0:width].rearrange("p a n -> p (a n)")

            def logits_in(pr, s, bank, bias, width, ready, h, maxed):
                dve.wait_ge(ready, h + 1)
                link(V.scalar_tensor_tensor(out=pr[:, s, :, :].rearrange("p a n -> p (a n)"), in0=bank[:, :], scalar=float(width) ** -0.5,
                                            in1=bias[:, :, :].rearrange("p a n -> p (a n)"), op0=ALU.mult, op1=ALU.add))
                V.tensor_reduce(smax[:, s, 0, :], pr[:, s, :, :], AX, ALU.max, negate=True).then_inc(maxed, 1)

            def sums_inverted(s, h, exped, maxed):
                dve.wait_ge(exped, h + 1)
                V.reciprocal(smax[:, s, 1, :], smax[:, s, 1, :]).then_inc(maxed, 1)

            def stage_A(i, c, s):
                for t in range(TOK):
                    a = 4 * c + 2 * s + t
                    last = V.scalar_tensor_tensor(out=qsA[:, s, t, :], in0=row(pq, i, a, HD), scalar=head_rstd(i, 4 + a),
                                                  in1=gains[:, 0:HD], op0=ALU.mult, op1=ALU.mult)
                link(last)
                rope(qsA[:, s, :, :].unsqueeze(2), 0, 16, ropeA, 2, (TOK, 1), A_staged)

            with dve.Fori(0, 2) as i:
                order.enter(i, 12)
                for c in range(2):
                    tb, off, h = PHASES["gate"][0] + 8 * c + RING, i * 16, i * 4 + 2 * c
                    stage_A(i, c, 0)
                    split(tb, off)
                    stage_A(i, c, 1)
                    split(tb + 1, off)
                    logits_in(prA, 0, M[1], selbias, HD, A_logits, h, A_maxed)
                    split(tb + 2, off)
                    split(tb + 3, off)
                    sums_inverted(0, h, A_exp, A_maxed)
                    logits_in(prA, 1, M[2], selbias, HD, A_logits, h + 1, A_maxed)
                    ada(16 * SC_F + 4 * c, i * 8)
                    split(tb + 4, off)
                    sums_inverted(1, h + 1, A_exp, A_maxed)
                    for j in range(1, 4):
                        ada(16 * SC_F + 4 * c + j, i * 8)
                        split(tb + 4 + j, off)
                order.leave(2)
            scale_ready(SC_F, V_SCF, V_GFFN)
            ada_begin(GT_A)

            def stage_B(i, c, s):
                for t in range(TOK):
                    a = 4 * c + 2 * s + t
                    V.scalar_tensor_tensor(out=ksB[:, s, t, 0:NOPE], in0=row(mkv, i, a, NOPE), scalar=head_rstd(i, 36 + a),
                                           in1=gains[:, 448:448 + NOPE], op0=ALU.mult, op1=ALU.mult)
                    V.tensor_scalar(ksB[:, s, t, NOPE:MD], kbase[:, t, :], head_rstd(i, 36 + a), None, ALU.mult)
                    last = V.scalar_tensor_tensor(out=qsB[:, s, t, :], in0=row(mq, i, a, MD), scalar=head_rstd(i, 20 + a),
                                                  in1=gains[:, 256:448], op0=ALU.mult, op1=ALU.mult)
                link(last)
                rope(qsB[:, s, :, NOPE:MD].unsqueeze(2), 24, 32, ropeB, 2, (TOK, 1), B_staged)

            def rotated_out(s, h):
                dve.wait_ge(B_turned, h + 1)
                V.tensor_copy(rT[0:MROT, s, :, :].rearrange("p a n -> p (a n)"), M[1 + 2 * s][0:MROT, :]).then_inc(B_rT, 1)

            with dve.Fori(0, 2) as i:
                order.enter(i, 12)
                for c in range(2):
                    tb, off, h = PHASES["gate"][0] + 32 + 8 * c + RING, i * 16, i * 4 + 2 * c
                    stage_B(i, c, 0)
                    split(tb, off)
                    rotated_out(0, h)
                    stage_B(i, c, 1)
                    split(tb + 1, off)
                    logits_in(prB, 0, M[1], causal, MD, B_logits, h, B_maxed)
                    split(tb + 2, off)
                    rotated_out(1, h + 1)
                    split(tb + 3, off)
                    sums_inverted(0, h, B_exp, B_maxed)
                    logits_in(prB, 1, M[3], causal, MD, B_logits, h + 1, B_maxed)
                    split(tb + 4, off)
                    sums_inverted(1, h + 1, B_exp, B_maxed)
                    split(tb + 5, off)
                    for j in range(2):
                        ada(16 * GT_A + 2 * c + j, i * 4)
                        split(tb + 6 + j, off)
                order.leave(2)

            for b in range(2):
                dve.wait_ge(o_hi, b + 1)
                V.tensor_tensor(sa_lo[:, 4 * b:4 * b + 4, :], oTA[:, 4 * b:4 * b + 4, :], sa_hi[:, 4 * b:4 * b + 4, :].bitcast(F32),
                                ALU.subtract).then_inc(o_lo, 1)
            for b in range(2):
                dve.wait_ge(o_hi, b + 3)
                V.tensor_tensor(sa_lo[:, 8 + 4 * b:12 + 4 * b, :], oTB[:, 4 * b:4 * b + 4, 0:S], sa_hi[:, 8 + 4 * b:12 + 4 * b, :].bitcast(F32),
                                ALU.subtract).then_inc(o_lo, 1)
            dve.wait_ge(o_lo, 4)

            def half(n, side, i=0):
                t0, c0, _, _ = PHASES["proj"]
                dve.wait_ge(tile_used, i * 8 + (t0 + 8 * n + 4 * side + 4))
                dve.wait_ge(gate_loaded[side], i * 16 + 16 * (n + 1))
                dst = merged if side == 0 else gv2
                for t in range(TOK):
                    last = V.tensor_tensor(dst[:, t, :], acc[(c0 + side) % 2][t][:, :], U[:, side, t, :], ALU.mult)
                last.then_inc(chunk_evac, 1)
                if side:
                    dve.wait_ge(chunk_evac, i * 2 + (c0 + 2 * n + 2))
                    V.tensor_tensor(merged, merged, gv2, ALU.add).then_inc(m_ready, 1)
                    dve.wait_ge(m_ready, i + (n + 1))

            def merged_lo(n):
                for q in range(2):
                    dve.wait_ge(m_hi, n * 2 + (q + 1))
                    V.tensor_tensor(sb_lo[:, bass.ds(n * 4 + 2 * q, 2), :], bank2(M[q]),
                                    sb_hi[:, bass.ds(n * 4 + 2 * q, 2), :].bitcast(F32), ALU.subtract).then_inc(m_lo, 1)

            def proj(n, i, first):
                tb, off = PHASES["proj"][0] + RING + 8 * n, i * 8
                for j in range(4):
                    split(tb + j, off)
                if not first:
                    merged_lo(i)
                ada(16 * GT_A + 8 + 2 * n, i * 2)
                half(n, 0, i)
                for j in range(4, 8):
                    split(tb + j, off)
                ada(16 * GT_A + 9 + 2 * n, i * 2)
                half(n, 1, i)

            proj(0, 0, True)
            with dve.Fori(0, 3) as i:
                proj(1, i, False)
            gate_ready(GT_A, 0, 2)
            merged_lo(3)
            gate_ready(GT_A, 1, 2)
            dve.wait_ge(gt_ready, 2)
            dve.wait_ge(res_landed, 16)

            def update(name, c, i=0):
                t0, c0, _, k = PHASES[name]
                dve.wait_ge(tile_used, i * (2 * k) + (t0 + (c + 1) * k))
                cols = bass.ds(i * 2 * NC + c * NC, NC)
                for t in range(TOK):
                    last = V.tensor_tensor(gv2[:, t, :], acc[(c0 + c) % 2][t][:, :], gt[:, cols], ALU.mult)
                last.then_inc(chunk_evac, 1)
                dve.wait_ge(chunk_evac, i * 2 + (c0 + c + 1))
                V.tensor_tensor(X[:, :, cols], X[:, :, cols], gv2, ALU.add).then_inc(x_updated, 1)
                dve.wait_ge(x_updated, i * 2 + (UPDATES[name] + c + 1))

            t0 = PHASES["wo"][0]
            with dve.Fori(0, 2) as i:
                for c in range(2):
                    for j in range(8):
                        split(t0 + 8 * c + j + RING, i * 16)
                    update("wo", c, i)
            norm_x(TOK + 5)
            norm_lo(gv2, sa_hi, sa_lo, 0, 8, mod_s, mod_b)

            def conv(side, pg):
                dve.wait_ge(cv_based, pg * 2 + (side + 1))
                for tap, lag in ((1, 1), (0, 2)):
                    for b in range(4):
                        v = cv[:, 4 * side + b, lag:S]
                        last = V.scalar_tensor_tensor(out=v, in0=M[2 * side + b // 2][:, (b % 2) * S:(b % 2) * S + S - lag],
                                                      scalar=cvec[:, tap, bass.ds(pg * 4 + (44 * side + b), 1)], in1=v,
                                                      op0=ALU.mult, op1=ALU.add)
                    if lag == 1:
                        link(last)
                    else:
                        last.then_inc(cv_done, 1)

            def times(pg):
                dve.wait_ge(cv_done, pg * 2 + 2)
                dve.wait_ge(silu_done, pg + 1)
                V.tensor_tensor(gv[:, :, :], cv[:, 0:4, :], cv[:, 4:8, :], ALU.mult).then_inc(gv_ready, 1)

            def ffn_lo(pg, pl):
                dve.wait_ge(f_hi, pg + 1)
                V.tensor_tensor(sb_lo[:, bass.ds(pl * 4, 4), :], gv[:, :, :], sb_hi[:, bass.ds(pl * 4, 4), :].bitcast(F32),
                                ALU.subtract).then_inc(f_lo, 1)

            def up_pair(part, i, shift, first, region):
                t0 = PHASES[f"up{part}"][0] + 16 * shift
                off = i * 16
                n = 16 * region + 4 * shift
                for j in range(4):
                    split(t0 + RING + j, off)
                if not first:
                    conv(1, i + (shift + 4 * part - 1))
                    times(i + (shift + 4 * part - 1))
                split(t0 + RING + 4, off)
                split(t0 + RING + 5, off)
                if not first:
                    ffn_lo(i + (shift + 4 * part - 1), i + (shift - 1))
                split(t0 + RING + 6, off)
                ada(n, i * 4)
                split(t0 + RING + 7, off)
                ada(n + 1, i * 4)
                for j in range(4):
                    split(t0 + RING + 8 + j, off)
                conv(0, i + (shift + 4 * part))
                split(t0 + RING + 12, off)
                ada(n + 2, i * 4)
                split(t0 + RING + 13, off)
                split(t0 + RING + 14, off)
                ada(n + 3, i * 4)
                split(t0 + RING + 15, off)

            for part, (n, region) in enumerate(zip(PAIRS, (GT_F, SH_2, GT_2))):
                ada_begin(region)
                up_pair(part, 0, 0, True, region)
                with dve.Fori(0, n - 1) as i:
                    order.enter(i, 2)
                    up_pair(part, i, 1, False, region)
                    order.leave(n - 1)
                t0, _, _, k = PHASES[f"down{part}"]
                for c in range(4):
                    for j in range(k):
                        if c == 0 and j == k - 4:
                            conv(1, 4 * part + n - 1)
                            times(4 * part + n - 1)
                            if part == 0:
                                gate_ready(GT_F, 0, 0)
                        if c == 0 and j == k - 2:
                            ffn_lo(4 * part + n - 1, n - 1)
                        if c == 0 and j == k - 1 and part == 0:
                            gate_ready(GT_F, 1, 0)
                            dve.wait_ge(gt_ready, 4)
                        if c == 0 and j == 0 and part == 1:
                            shift_ready(SH_2, V_SH2)
                            ada_begin(SC_2)
                        if part == 1 and j % 2:
                            ada(16 * SC_2 + 4 * c + j // 2)
                        if part == 2 and j == 3:
                            ada(16 * GT_2 + 12 + c)
                        split(t0 + c * k + j + RING)
                    update(f"down{part}", c)
                if part == 1:
                    scale_ready(SC_2, V_SC2)

            norm_x(TOK + 9)
            norm_lo(gv2, sa_hi, sa_lo, 0, 8, mod_s, mod_b)

            def pooled_lo(c):
                for q in range(2):
                    dve.wait_ge(p_hi, 2 * c + q + 1)
                    k = 4 * c + 2 * q
                    V.tensor_tensor(sb_lo[:, k:k + 2, :], bank2(M[2 * (c % 2) + q]), sb_hi[:, k:k + 2, :].bitcast(F32),
                                    ALU.subtract).then_inc(p_lo, 1)

            t0 = PHASES["pin"][0] + RING
            for c in range(4):
                for j in range(4):
                    split(t0 + 8 * c + j)
                if c:
                    pooled_lo(c - 1)
                for j in range(4, 8):
                    split(t0 + 8 * c + j)

            def y_scale(n):
                dve.wait_ge(y_turned, 2 * n + 2)
                for b in range(4):
                    last = V.tensor_scalar(gv[:, b, :], M[2 * (n % 2) + b // 2][:, (b % 2) * S:(b % 2 + 1) * S],
                                           vecs[:, V_PSCALE + 4 * n + b:V_PSCALE + 4 * n + b + 1], None, ALU.mult)
                last.then_inc(y_scaled, 1)

            def y_low(n):
                dve.wait_ge(y_hi, n + 1)
                V.tensor_tensor(sb_lo[:, 4 * n:4 * n + 4, :], gv[:, :, :], sb_hi[:, 4 * n:4 * n + 4, :].bitcast(F32),
                                ALU.subtract).then_inc(y_lo, 1)
                dve.wait_ge(y_lo, n + 1)

            for n in range(4):
                t0, c0, _, _ = PHASES[f"gp{n}"]
                for j in range(8):
                    split(t0 + RING + j)
                    if n == 0 and j == 3:
                        pooled_lo(3)
                    if n == 1 and j in (1, 3):
                        gate_ready(GT_2, j // 2, 2)
                    if n and j == 5:
                        y_scale(n - 1)
                if n:
                    y_low(n - 1)
                split(t0 + RING + 8)
                split(t0 + RING + 9)
                dve.wait_ge(chunk_evac, c0 + 1)
                dve.wait_ge(tile_used, t0 + 10)
                for t in range(TOK):
                    last = V.tensor_tensor(U[:, n % 2, t, :], acc[(c0 + 1) % 2][t][:, :], ada_ring[:, t, n * NC:(n + 1) * NC], ALU.mult)
                last.then_inc(chunk_evac, 1)

            def final_gain(c):
                dve.wait_ge(xsq_done, TOK + 9 + c + 1)
                cols = slice(c * NC, (c + 1) * NC)
                V.tensor_tensor(X[:, :, cols], X[:, :, cols], fgain[:, cols].unsqueeze(1).broadcast_to([P, TOK, NC]), ALU.mult).then_inc(fg_applied, 1)

            t0 = PHASES["pout"][0]
            dve.wait_ge(gt_ready, 6)
            dve.wait_ge(fg_landed, 16)
            for c in range(4):
                for j in range(8):
                    if c == 0 and j == 6:
                        y_low(3)
                    split(t0 + 8 * c + j + RING)
                    if c == 0 and j == 3:
                        y_scale(3)
                    if c and j == 3:
                        final_gain(c - 1)
                update("pout", c)
            dve.wait_ge(xsq_done, TOK + 13)
            link(V.reduce_sum(rstd[:, 0:TOK], ssq[:, :, :], AX))
            V.tensor_scalar(stat[:, 0, 0:TOK], rstd[:, 0:TOK], 1.0 / D, EPS, ALU.mult, ALU.add).then_inc(ms_ready, 1)
            final_gain(3)
            dve.wait_ge(sqrt_ready, norms[0] + 1)
            V.reciprocal(rstd[:, 0:TOK], stat[:, 1, 0:TOK]).then_inc(diag_ready, 1)
            dve.wait_ge(diag_ready, 5)
            for h in range(2):
                half = slice(h * D // 2, (h + 1) * D // 2)
                V.tensor_scalar(X[:, 0, half], X[:, 0, half], rstd[:, 0:1], None, ALU.mult).then_inc(outD, 1)

        @block.tensor
        def _(pe):
            mm = nc.tensor.matmul

            def tile(tb, off, hi, lo, ks, pair, first, last):
                pe.wait_ge(lo_ready, tb + 1 + off)
                for n, k in enumerate(ks):
                    for t in range(TOK):
                        xh, xl = hi[:, k, t * P:(t + 1) * P], lo[:, k, t * P:(t + 1) * P]
                        wh, wl = whi[:, tb % RING, n, :], wlo[:, tb % RING, n, :]
                        mm(pair[t][:, :], xh, wh, start=first and n == 0, stop=False)
                        mm(pair[t][:, :], xh, wl, start=False, stop=False)
                        end = mm(pair[t][:, :], xl, wh, start=False, stop=last and n == 1)
                end.then_inc(tile_used, 1)

            def bank_free(c, i=0, per=1):
                if c >= 2:
                    pe.wait_ge(chunk_evac, i * per + (c - 1))

            def tiles(name, c, js, hi, lo, i=0, per=1, k0=0, wait=None):
                t0, c0, _, k = PHASES[name]
                for j in js:
                    if j == 0:
                        bank_free(c0 + c, i, per)
                    if wait:
                        wait(j)
                    tile(t0 + c * k + j, i * (per * k), hi, lo, (k0 + 2 * j, k0 + 2 * j + 1), acc[(c0 + c) % 2], j == 0, j == k - 1)

            def sum_cols(r):
                pe.wait_ge(ada_used, 16 * (r + 1))
                for b in range(16):
                    last = mm(M[0][:, b:b + 1], ada_acc[:, b * P:(b + 1) * P], ones[:, 0:1], start=True, stop=True)
                last.then_inc(cols_summed, 1)

            def sum_rows(r, half, bank):
                pe.wait_ge(ada_used, 16 * (r + 1))
                for n in range(2):
                    last = mm(M[bank + n][:, :], ones[:, :], ada_acc[:, (2 * half + n) * NC:(2 * half + n + 1) * NC], start=True, stop=True)
                last.then_inc(rows_summed, 1)

            pairs = [0]
            diags = [0]

            def norm_turn(src, npair, scales=lambda k: diag):
                diags[0] += 1
                pe.wait_ge(diag_ready, diags[0])
                for b in range(npair):
                    if b >= 4:
                        pe.wait_ge(nrm_evac, pairs[0] + b - 3)
                    for kk in range(2):
                        for t in range(TOK):
                            k = 2 * b + kk
                            last = mm(M[b % 4][:, kk * S + t * P:kk * S + (t + 1) * P], src(t, k), scales(k)[:, t, :], start=True, stop=True)
                    last.then_inc(nrm_turned, 1)
                pairs[0] += npair

            pe.wait_ge(ones_ready, 1)
            pe.wait_ge(vec_landed, 16 * 13)
            nc.tensor.transpose(M[1][:, 0:P], vstage[:, 0, :], ident[:, :])
            nc.tensor.transpose(M[1][:, P:P + 22], vstage[0:22, 1, :], ident[0:22, 0:22]).then_inc(vec_turned, 1)
            for j in range(4):
                last = nc.tensor.transpose(M[2][:, 88 * j:88 * (j + 1)], vstage[0:88, 2 + j, :], ident[0:88, 0:88])
            last.then_inc(vec_turned, 1)
            sum_cols(SH_A)
            pe.wait_ge(mod_ready, 1)
            sum_cols(SC_A)
            pe.wait_ge(mod_ready, 2)
            norm_turn(lambda t, k: xs[:, t, k * P:(k + 1) * P], 8)

            at = [0]

            def upto(n):
                while at[0] < n:
                    t = at[0]
                    if t < PHASES["mq"][0]:
                        tiles("in", t // 8, (t % 8,), sa_hi, sa_lo, wait=(lambda j: pe.wait_ge(nrm_lo, j + 1)) if t < 8 else None)
                    elif t < PHASES["mkv"][0]:
                        c, j = divmod(t - PHASES["mq"][0], 2)
                        tiles("mq", c, (j,), lat_hi, lat_lo)
                    else:
                        tiles("mkv", t - PHASES["mkv"][0], (0,), lat_hi, lat_lo, k0=4)
                    at[0] += 1

            upto(28)
            pe.wait_ge(qi_roped, 1)
            for b in range(8):
                for t in range(TOK):
                    last = nc.tensor.transpose(M[b // 2][:, (b % 2) * S + t * P:(b % 2) * S + (t + 1) * P],
                                               qi[:, t, 2 * b:2 * b + 2, :].rearrange("p h d -> p (h d)"), ident[:, :])
                if b % 2:
                    last.then_inc(qi_turned, 1)
            upto(29)
            pe.wait_ge(qi_evac, 1)
            for t in range(TOK):
                last = nc.tensor.transpose(M[0][:, t * P:(t + 1) * P], kirep[:, t, :], ident[:, :])
            last.then_inc(qi_turned, 1)
            upto(38)
            pe.wait_ge(qi_evac, 5)
            norm_turn(lambda t, k: mql[:, t, k * P:(k + 1) * P] if k < 4 else pm[:, t, (k - 4) * P:(k - 3) * P], 3,
                      lambda k: diag if k < 4 else diag2)
            for b in range(4):
                upto(42 + 2 * b)
                if b == 0:
                    pe.wait_ge(nrm_lo, 11)
                for h in range(4 * b, 4 * b + 4):
                    if b:
                        pe.wait_ge(relu_ready, h - 3)
                    part = slice(ID * (h % 2), ID * (h % 2 + 1))
                    for t in range(TOK):
                        last = mm(M[h % 4][:, t * S:(t + 1) * S], qiT[part, h // 2, t * P:(t + 1) * P], kiT[part, :], start=True, stop=True)
                    last.then_inc(dots_ready, 1)
            upto(60)
            pe.wait_ge(relu_ready, IH)
            pe.wait_ge(k_normed, 1)
            for g in range(GROUPS):
                for t in range(TOK):
                    last = nc.tensor.transpose(M[0][:, g * S + t * P:g * S + (t + 1) * P], pkv[:, t, g * HD:(g + 1) * HD], ident[:, :])
            last.then_inc(k_turned, 1)
            upto(68)
            pe.wait_ge(k_evac, 1)
            sum_cols(SH_F)
            pe.wait_ge(mod_ready, 3)

            def turn_probs(pr, s, bank, ready, h, done):
                pe.wait_ge(ready, h + 1)
                nc.tensor.transpose(bank[:, 0:P], pr[:, s, 0, 0:P], ident[:, :])
                nc.tensor.transpose(bank[:, P:2 * P], pr[:, s, 1, 0:P], ident[:, :])
                nc.tensor.transpose(bank[:, 2 * P:3 * P], pr[:, s, 1, P:2 * P], ident[:, :]).then_inc(done, 1)

            def weigh(pT, s, v, bank, evac, h, done):
                pe.wait_ge(evac, h + 1)
                mm(bank[:, 0:S], v[0], pT[:, s, 0:S], start=True, stop=False, skip_group_check=True)
                mm(bank[:, P:S], v[1], pT[:, s, S:384], start=False, stop=True, skip_group_check=True).then_inc(done, 1)

            def turn_A(s, h):
                pe.wait_ge(A_staged, h + 1)
                for t in range(TOK):
                    last = nc.tensor.transpose(M[0][:, s * S + t * P:s * S + (t + 1) * P], qsA[:, s, t, :], ident[:, :])
                last.then_inc(A_turned, 1)

            def logits_A(i, s, h):
                pe.wait_ge(A_qT, h + 1)
                for t in range(TOK):
                    last = mm(M[1 + s][:, t * S:(t + 1) * S], qTA[:, s, t * P:(t + 1) * P],
                              kT[:, bass.ds(i, 1), :].rearrange("p a n -> p (a n)"), start=True, stop=True)
                last.then_inc(A_logits, 1)

            values = [vA[:, t, :] for t in range(TOK)]
            with pe.Fori(0, 2) as i:
                for c in range(2):
                    h = i * 4 + 2 * c

                    def gate(*js):
                        tiles("gate", c, js, sa_hi, sa_lo, i, 2)

                    gate(0)
                    turn_A(0, h)
                    gate(1)
                    logits_A(i, 0, h)
                    gate(2)
                    turn_A(1, h + 1)
                    gate(3)
                    logits_A(i, 1, h + 1)
                    gate(4)
                    turn_probs(prA, 0, M[3], A_probs, h, A_pT)
                    gate(5)
                    if c == 0:
                        pe.wait_ge(A_v, i + 1)
                    weigh(pTA, 0, values, M[1], A_pT_evac, h, A_o)
                    turn_probs(prA, 1, M[0], A_probs, h + 1, A_pT)
                    gate(6)
                    weigh(pTA, 1, values, M[2], A_pT_evac, h + 1, A_o)
                    gate(7)
            sum_cols(SC_F)
            pe.wait_ge(mod_ready, 4)

            def turn_B(s, h):
                pe.wait_ge(B_staged, h + 1)
                for x, v in enumerate((qsB, ksB)):
                    for t in range(TOK):
                        at = slice(x * S + t * P, x * S + (t + 1) * P)
                        nc.tensor.transpose(M[2 * s][:, at], v[:, s, t, 0:NOPE], ident[:, :])
                        last = nc.tensor.transpose(M[1 + 2 * s][0:MROT, at], v[:, s, t, NOPE:MD], ident[:, :])
                last.then_inc(B_turned, 1)

            def logits_B(s, h):
                pe.wait_ge(B_nT, h + 1)
                pe.wait_ge(B_rT, h + 1)
                for t in range(TOK):
                    bank = M[1 + 2 * s][:, t * S:(t + 1) * S]
                    mm(bank, nT[:, s, 0, t * P:(t + 1) * P], nT[:, s, 1, :], start=True, stop=False)
                    last = mm(bank, rT[0:MROT, s, 0, t * P:(t + 1) * P], rT[0:MROT, s, 1, :], start=False, stop=True)
                last.then_inc(B_logits, 1)

            with pe.Fori(0, 2) as i:
                for c in range(2):
                    h = i * 4 + 2 * c

                    def gate(*js):
                        tiles("gate", 4 + c, js, sa_hi, sa_lo, i, 2)

                    gate(0)
                    pe.wait_ge(B_v, i * 2 + (c + 1))
                    turn_B(0, h)
                    gate(1)
                    logits_B(0, h)
                    gate(2)
                    turn_B(1, h + 1)
                    gate(3)
                    logits_B(1, h + 1)
                    gate(4)
                    turn_probs(prB, 0, M[0], B_probs, h, B_pT)
                    gate(5)
                    weigh(pTB, 0, [vB[:, 0, t, :] for t in range(TOK)], M[1], B_pT_evac, h, B_o)
                    turn_probs(prB, 1, M[2], B_probs, h + 1, B_pT)
                    gate(6)
                    weigh(pTB, 1, [vB[:, 1, t, :] for t in range(TOK)], M[3], B_pT_evac, h + 1, B_o)
                    gate(7)

            def merged_turn(n):
                pe.wait_ge(m_ready, n + 1)
                for q in range(2):
                    for b in range(2):
                        for t in range(TOK):
                            blk = (2 * q + b) * P
                            last = nc.tensor.transpose(M[q][:, b * S + t * P:b * S + (t + 1) * P], merged[:, t, blk:blk + P], ident[:, :])
                    last.then_inc(m_turned, 1)

            def proj(n, i, first):
                ready = [lambda j, s=s: pe.wait_ge(o_lo, 2 * s + j // 2 + 1) for s in range(2)] if first else [None, None]
                tiles("proj", 2 * n, (0, 1), sa_hi, sa_lo, i, 2, wait=ready[0])
                if not first:
                    merged_turn(i)
                tiles("proj", 2 * n, (2, 3), sa_hi, sa_lo, i, 2, wait=ready[0])
                tiles("proj", 2 * n + 1, range(4), sa_hi, sa_lo, i, 2, k0=8, wait=ready[1])

            proj(0, 0, True)
            with pe.Fori(0, 3) as i:
                proj(1, i, False)
            merged_turn(3)
            sum_rows(GT_A, 0, 2)
            pe.wait_ge(m_lo, 8)
            pe.wait_ge(gt_ready, 1)
            sum_rows(GT_A, 1, 2)
            with pe.Fori(0, 2) as i:
                for c in range(2):
                    tiles("wo", c, range(8), sb_hi, sb_lo, i, 2)
            pe.wait_ge(gt_ready, 2)
            norm_turn(lambda t, k: X[:, t, k * P:(k + 1) * P], 8)

            def turn(side):
                for q in range(2):
                    for b in range(2):
                        for t in range(TOK):
                            blk = (2 * q + b) * P
                            last = nc.tensor.transpose(M[2 * side + q][:, b * S + t * P:b * S + (t + 1) * P],
                                                       U[:, side, t, blk:blk + P], ident[:, :])
                    last.then_inc(u_turned, 1)

            def up_pair(part, i, shift, first, wait=None):
                name = f"up{part}"
                c0 = PHASES[name][1]
                c = 2 * shift
                tiles(name, c, range(4), sa_hi, sa_lo, i, 2, wait=wait)
                if not first:
                    pe.wait_ge(chunk_evac, i * 2 + (c0 + c))
                    turn(1)
                tiles(name, c, range(4, 8), sa_hi, sa_lo, i, 2, wait=wait)
                tiles(name, c + 1, range(4), sa_hi, sa_lo, i, 2)
                pe.wait_ge(chunk_evac, i * 2 + (c0 + c + 1))
                turn(0)
                tiles(name, c + 1, range(4, 8), sa_hi, sa_lo, i, 2)

            for part, n in enumerate(PAIRS):
                up_pair(part, 0, 0, True, (lambda j: pe.wait_ge(nrm_lo, 12 + j)) if part == 0 else None)
                with pe.Fori(0, n - 1) as i:
                    up_pair(part, i, 1, False)
                _, c0, nn, _ = PHASES[f"up{part}"]
                name = f"down{part}"
                k = PHASES[name][3]
                if part == 1:
                    pe.wait_ge(cv_done, 2 * (4 * part + n) - 1)
                    sum_cols(SH_2)
                pe.wait_ge(f_lo, 4 * part + n - 1)
                tiles(name, 0, range(k - 4), sb_hi, sb_lo)
                pe.wait_ge(chunk_evac, c0 + nn)
                turn(1)
                if part == 0:
                    pe.wait_ge(cv_done, 2 * n - 1)
                    sum_rows(GT_F, 0, 0)
                tiles(name, 0, (k - 4, k - 3), sb_hi, sb_lo)
                pe.wait_ge(f_lo, 4 * part + n)
                tiles(name, 0, (k - 2,), sb_hi, sb_lo)
                if part == 0:
                    pe.wait_ge(gt_ready, 3)
                    sum_rows(GT_F, 1, 0)
                tiles(name, 0, (k - 1,), sb_hi, sb_lo)
                for c in range(1, 4):
                    tiles(name, c, range(k), sb_hi, sb_lo)
                if part == 1:
                    pe.wait_ge(mod_ready, 5)
                    sum_cols(SC_2)
                    pe.wait_ge(mod_ready, 6)

            norm_turn(lambda t, k: X[:, t, k * P:(k + 1) * P], 8)

            def pooled(c):
                pe.wait_ge(chunk_evac, PHASES["pin"][1] + c + 1)
                pe.wait_ge(pmat_landed, 16)
                if c >= 2:
                    pe.wait_ge(p_lo, 2 * (c - 1))
                for q in range(2):
                    for b in range(2):
                        blk = (2 * q + b) * P
                        for t in range(TOK):
                            last = mm(M[2 * (c % 2) + q][:, b * S:(b + 1) * S], U[:, c % 2, t, blk:blk + P], cv[:, 2 * c + t, :],
                                      start=t == 0, stop=t == TOK - 1)
                    last.then_inc(p_turned, 1)

            for c in range(4):
                wait = (lambda j: pe.wait_ge(nrm_lo, 20 + j)) if c == 0 else None
                tiles("pin", c, range(4), sa_hi, sa_lo, wait=wait)
                if c:
                    pooled(c - 1)
                tiles("pin", c, range(4, 8), sa_hi, sa_lo, wait=wait)

            def y_turn(n):
                pe.wait_ge(chunk_evac, PHASES[f"grp{n}"][1] + 1)
                if n >= 2:
                    pe.wait_ge(y_scaled, n - 1)
                for q in range(2):
                    for b in range(2):
                        for t in range(TOK):
                            blk = (2 * q + b) * P
                            last = nc.tensor.transpose(M[2 * (n % 2) + q][:, b * S + t * P:b * S + (t + 1) * P],
                                                       U[:, n % 2, t, blk:blk + P], ident[:, :])
                    last.then_inc(y_turned, 1)

            for n in range(4):
                for j in range(8):
                    tiles(f"gp{n}", 0, (j,), sa_hi, sa_lo)
                    if n == 0 and j == 3:
                        pooled(3)
                    if n == 1 and j == 1:
                        pe.wait_ge(p_lo, 8)
                        sum_rows(GT_2, 0, 2)
                    if n == 1 and j == 3:
                        pe.wait_ge(gt_ready, 5)
                        sum_rows(GT_2, 1, 2)
                    if n and j == 5:
                        if n == 2:
                            pe.wait_ge(gt_ready, 6)
                        y_turn(n - 1)
                pe.wait_ge(p_lo, 2 * n + 2)
                tiles(f"grp{n}", 0, range(2), sb_hi, sb_lo, k0=4 * n)
            pe.wait_ge(y_lo, 3)
            tiles("pout", 0, range(4), sb_hi, sb_lo)
            y_turn(3)
            tiles("pout", 0, (4, 5), sb_hi, sb_lo)
            pe.wait_ge(y_lo, 4)
            tiles("pout", 0, (6, 7), sb_hi, sb_lo)
            for c in range(1, 4):
                tiles("pout", c, range(8), sb_hi, sb_lo)


_INS = ["x", "c", "positions", "g_attn", "g_ffn", "w_ada", "b_ada", "w_in", "g_qa", "g_ka", "g_mq_lat", "w_mq_up",
        "g_mkv_lat", "w_mkv_up", "g_qm", "g_km", "w_pa", "w_pb", "w_o", "w_up", "w_conv", "b_conv", "w_down",
        "c_2", "w_mod_2", "b_mod_2", "pool_w_in_2", "pool_w_grp_2", "pool_scale_2", "pool_w_out_2", "final_norm_g_2"]


def shape_constants():
    inv = [THETA ** (-np.arange(0, r, 2) / r) for r in (ROT, IROT, MROT)]
    q, k = np.arange(S)[:, None], np.arange(S)[None, :]
    causal = np.where(k <= q, 0.0, MASKED).reshape(TOK, P, S).transpose(1, 0, 2)
    pool = np.zeros((4, S, S))
    for g, w in enumerate(WINDOWS):
        lo, hi = np.maximum(q - w // 2, 0), np.minimum(q + w // 2, S)
        pool[g] = (((k >= lo) & (k < hi)) / (hi - lo) - np.eye(S)).T
    pool = pool.reshape(4, TOK, P, S).transpose(2, 0, 1, 3).reshape(P, 4 * TOK, S)
    return {"identity": np.eye(P, dtype=np.float32), "inv_freq": np.concatenate(inv)[None].astype(np.float32),
            "causal": causal.astype(np.float32), "pool_matrix": np.ascontiguousarray(pool).astype(np.float32)}


def kernel(**inputs):
    import numpy as _np
    import concourse.bacc as _bacc
    from concourse.bass_utils import run_bass_kernel_spmd as _run

    nc = _bacc.Bacc("TRN2", target_bir_lowering=False, num_devices=1)
    arrays, args = {}, {}
    given = {n: _np.ascontiguousarray(inputs[n]) for n in _INS}
    for name, a in {**given, **shape_constants()}.items():
        arrays[f"in_{name}_dram"] = a
        args[name] = nc.dram_tensor(f"in_{name}_dram", a.shape, mybir.dt.from_np(a.dtype), kind="ExternalInput").ap()
    out = nc.dram_tensor("out_0_dram", (1, S, D), F32, kind="ExternalOutput").ap()
    build(nc, args, out)
    r = _run(nc, [arrays], core_ids=[0])
    return r.results[0]["out_0_dram"]
```

```python
from contextlib import ExitStack

import numpy as np

import concourse.bass as bass
from concourse import mybir

F32 = mybir.dt.float32
F32R = mybir.dt.float32r
I32 = mybir.dt.int32
ALU = mybir.AluOpType
ACT = mybir.ActivationFunctionType
AX = mybir.AxisListType.X

P = 128
D = 2048
S = 256
TOK = S // P
NC = 512
RAW, RING = 8, 4
D_FF = 5632
H, HD, ROT = 8, 128, 32
GROUPS = 2
IH, ID, IROT = 16, 64, 16
NOPE, MROT, MV = 128, 64, 128
MD = NOPE + MROT
QLORA, KVLORA = 512, 256
TOPK = 64
THETA = 500000.0
EPS = 1e-6
MASKED = -1e30
TAKEN = -3e38
WINDOWS = (2, 4, 8, 16)
TWO_PI = 6.283185307179586
PI_HI = 6.28125
PI_MID = float(np.float32(TWO_PI - PI_HI))
PI_LO = float(TWO_PI - PI_HI - PI_MID)
ROUND = 12582912.0

C_QA, C_KA, C_QI, C_KI, C_MQ, C_MKV, C_GATE = 0, 1024, 1536, 2560, 2640, 3152, 3472

PHASES = {}
_t = _c = 0
for _name, _n, _k in (("in", 7, 8), ("mq", 4, 2), ("mkv", 4, 1), ("gate", 8, 8), ("proj", 8, 4), ("wo", 4, 8),
                      ("up0", 8, 8), ("down0", 4, 8), ("up1", 8, 8), ("down1", 4, 8), ("up2", 6, 8), ("down2", 4, 6),
                      ("pin", 4, 8), ("gp0", 1, 8), ("grp0", 1, 2), ("gp1", 1, 8), ("grp1", 1, 2), ("gp2", 1, 8),
                      ("grp2", 1, 2), ("gp3", 1, 8), ("grp3", 1, 2), ("pout", 4, 8)):
    PHASES[_name] = (_t, _c, _n, _k)
    _t += _n * _k
    _c += _n
TILES = _t

TOGETHER = 24


def in_tile(t):
    if t < TOGETHER:
        q, r = divmod(t, 6)
        return r // 2, 2 * q + r % 2
    return divmod(t, 8)


IN_PIECES = {t % RAW: t for t in range(TOGETHER) if in_tile(t)[0] == 0}

V_GATTN, V_GFFN, V_SHA, V_SCA, V_SHF, V_SCF, V_SH2, V_SC2 = range(0, 128, 16)
V_PSCALE, V_GMQ, V_GMKV = 128, 144, 148
NVEC = 150

SH_A, SC_A, SH_F, GT_A, SC_F, GT_F, SH_2, SC_2, GT_2 = range(9)
COLS = [SH_A, SC_A, SH_F, GT_A, SC_F, SH_2, SC_2]
ROWS = [GT_F, GT_2]
REGION_SRC = [(0, 0), (0, 1), (0, 3), (0, 2), (0, 4), (0, 5), (1, 0), (1, 1), (1, 2)]
PAIRS = (4, 4, 3)
UPDATES = {"wo": 0, "down0": 4, "down1": 8, "down2": 12, "pout": 16}
PI_IN = 3.1415925


def summed(r):
    return ("cols", COLS.index(r) + 7) if r in COLS else ("rows", 2 * ROWS.index(r) + 2)


class Order:

    def __init__(self, eng, sem):
        self.eng, self.sem, self.base, self.n = eng, sem, 0, 0

    def link(self, ins):
        self.n += 1
        ins.then_inc(self.sem, 1)
        self.eng.wait_ge(self.sem, self.base + self.n)

    def enter(self, i, per):
        self.outer, self.per = self.base + self.n, per
        self.base, self.n = i * per + self.outer, 0

    def leave(self, trips):
        assert self.n == self.per, self.n
        self.base, self.n = self.outer + self.per * trips, 0


def build(nc, A, out):
    ctx = ExitStack()
    with ctx:
        def sb(name, shape, dt=F32, stack=ctx):
            return stack.enter_context(nc.sbuf_tensor(name, shape, dt))

        def sem(name):
            return ctx.enter_context(nc.semaphore(name))

        raw = sb("raw", [P, RAW, 2, NC])
        whi = sb("whi", [P, RING, 2, NC], F32R)
        wlo = sb("wlo", [P, RING, 2, NC], F32R)
        sa_hi = sb("sa_hi", [P, 16, S], F32R)
        sa_lo = sb("sa_lo", [P, 16, S], F32R)
        ada_ring = sb("ada_ring", [P, 2, D])
        ada_acc = sb("ada_acc", [P, D])
        vecs = sb("vecs", [P, NVEC])
        cvec = sb("cvec", [P, 4, 88])
        ident = sb("ident", [P, P])
        ones = sb("ones", [P, P])
        diag = sb("diag", [P, TOK, P])
        cact = sb("cact", [P, 2, 16])
        mod_s = sb("mod_s", [P, 16])
        mod_b = sb("mod_b", [P, 16])
        gate_a = sb("gate_a", [P, 16])
        stat = sb("stat", [P, 2, 2 * TOK])
        ssq = sb("ssq", [P, TOK, 4])
        rstd = sb("rstd", [P, 2 * TOK])
        warm = sb("warm", [P, 1])

        with ExitStack() as st:
            xs = sb("xs", [P, TOK, D], stack=st)
            start_ring = sb("start_ring", [P, 4, D], stack=st)
            vstage = sb("vstage", [P, 6, P], stack=st)
            craw = sb("craw", [P, 2, 16], stack=st)
            start_tmp = sb("start_tmp", [P, 2, 512], stack=st)
            sqdump = sb("sqdump", [P, D], stack=st)
            start_acc = sb("start_acc", [P, D], stack=st)
        with ExitStack() as st:
            pq = sb("pq", [P, 2 * H, HD], stack=st)
            pkv = sb("pkv", [P, TOK, 512], stack=st)
            pm = sb("pm", [P, TOK, 400], stack=st)
            p2 = sb("p2", [P, 3072], stack=st)
            mkv = sb("mkv", [P, 2 * H, 256], stack=st)
            gains = sb("gains", [P, 640], stack=st)
            posf = sb("posf", [P, 2, TOK], stack=st)
            tabs = sb("tabs", [P, 2, TOK, 56], stack=st)
            causal = sb("causal", [P, TOK, S], stack=st)
            selbias = sb("selbias", [P, TOK, S], stack=st)
            kT = sb("kT", [P, GROUPS, S], stack=st)
            kbase = sb("kbase", [P, TOK, MROT], stack=st)
            hstat = sb("hstat", [P, 2, 56], stack=st)
            smax = sb("smax", [P, 2, 2, TOK], stack=st)
            gstage = sb("gstage", [P, TOK, NC], stack=st)
            with ExitStack() as prep:
                lat_hi = sb("lat_hi", [P, 6, S], F32R, stack=prep)
                lat_lo = sb("lat_lo", [P, 6, S], F32R, stack=prep)
                tmp = sb("tmp", [P, 2048], stack=prep)
                kirep = sb("kirep", [P, TOK, P], stack=prep)
                kiT = sb("kiT", [P, S], stack=prep)
                m8 = sb("m8", [P, 8], stack=prep)
                dump = sb("dump", [P, NC], stack=prep)
                diag2 = sb("diag2", [P, TOK, P], stack=prep)
            with ExitStack() as hd:
                qsA = sb("qsA", [P, 2, TOK, HD], stack=hd)
                qTA = sb("qTA", [P, 2, S], stack=hd)
                prA = sb("prA", [P, 2, TOK, S], stack=hd)
                pTA = sb("pTA", [P, 2, 384], stack=hd)
                vA = sb("vA", [P, TOK, HD], stack=hd)
                ropeA = sb("ropeA", [P, 4 * TOK * 16], stack=hd)
            with ExitStack() as hd:
                qsB = sb("qsB", [P, 2, TOK, MD], stack=hd)
                ksB = sb("ksB", [P, 2, TOK, MD], stack=hd)
                nT = sb("nT", [P, 2, 2, S], stack=hd)
                rT = sb("rT", [P, 2, 2, S], stack=hd)
                prB = sb("prB", [P, 2, TOK, S], stack=hd)
                pTB = sb("pTB", [P, 2, 384], stack=hd)
                vB = sb("vB", [P, 2, TOK, MV], stack=hd)
                ropeB = sb("ropeB", [P, 4 * TOK * 32], stack=hd)
        sb_hi = sb("sb_hi", [P, 16, S], F32R)
        sb_lo = sb("sb_lo", [P, 16, S], F32R)
        X = sb("X", [P, TOK, D])
        gt = sb("gt", [P, D])
        U = sb("U", [P, 2, TOK, NC])
        cv = sb("cv", [P, 8, S])
        gv = sb("gv", [P, 4, S])

        acc = [[ctx.enter_context(nc.psum_tensor(f"acc{a}{b}", [P, NC], F32)) for b in range(TOK)] for a in range(2)]
        M = [ctx.enter_context(nc.psum_tensor(f"misc{a}", [P, NC], F32)) for a in range(4)]
        gates_dram = nc.dram_tensor("gates_dram", (8, P, TOK, NC), F32, kind="Internal").ap()

        raw_landed = [sem(f"raw_landed{i}") for i in range(RAW)]
        hi_ready, lo_ready, tile_used, chunk_evac = sem("hi_ready"), sem("lo_ready"), sem("tile_used"), sem("chunk_evac")
        ada_landed = [sem(f"ada_landed{i}") for i in range(2)]
        start_landed = [sem(f"start_landed{i}") for i in range(4)]
        ada_used, cols_summed, rows_summed, mod_ready, gt_ready = (sem(n) for n in (
            "ada_used", "cols_summed", "rows_summed", "mod_ready", "gt_ready"))
        consts_landed, vec_landed, x_landed, ones_ready = sem("consts_landed"), sem("vec_landed"), sem("x_landed"), sem("ones_ready")
        vec_turned, vec_ready, c_ready = sem("vec_turned"), sem("vec_ready"), sem("c_ready")
        ssq_cleared, xsq_done, ms_ready, sqrt_ready, diag_ready = (sem(n) for n in (
            "ssq_cleared", "xsq_done", "ms_ready", "sqrt_ready", "diag_ready"))
        nrm_turned, nrm_evac, nrm_hi, nrm_lo = sem("nrm_turned"), sem("nrm_evac"), sem("nrm_hi"), sem("nrm_lo")
        dve_order, att_landed, ang_ready, tab_ready = sem("dve_order"), sem("att_landed"), sem("ang_ready"), sem("tab_ready")
        qi_roped, qi_turned, qi_evac = sem("qi_roped"), sem("qi_turned"), sem("qi_evac")
        dots_ready, relu_ready, relu_used = sem("dots_ready"), sem("relu_ready"), sem("relu_used")
        k_normed, k_turned, k_evac = sem("k_normed"), sem("k_turned"), sem("k_evac")
        hs_ms, hs_sqrt, hs_ready, kbase_ready, act_order = (sem(n) for n in ("hs_ms", "hs_sqrt", "hs_ready", "kbase_ready", "act_order"))
        A_staged, A_turned, A_qT, A_logits, A_maxed, A_probs, A_pT, A_pT_evac, A_o, A_o_evac, A_v = (sem("A_" + n) for n in (
            "staged", "turned", "qT", "logits", "maxed", "probs", "pT", "pT_evac", "o", "o_evac", "v"))
        B_staged, B_turned, B_nT, B_rT, B_logits, B_maxed, B_probs, B_pT, B_pT_evac, B_o, B_o_evac, B_v = (sem("B_" + n) for n in (
            "staged", "turned", "nT", "rT", "logits", "maxed", "probs", "pT", "pT_evac", "o", "o_evac", "v"))
        A_exp, B_exp = sem("A_exp"), sem("B_exp")
        gstage_free = sem("gstage_free")
        spread_ready, gate_spread = sem("spread_ready"), sem("gate_spread")
        gate_loaded = [sem(f"gate_loaded{i}") for i in range(2)]
        o_hi, o_lo, res_landed, bias_landed = sem("o_hi"), sem("o_lo"), sem("res_landed"), sem("bias_landed")
        m_ready, m_turned, m_hi, m_lo, x_updated = (sem(n) for n in ("m_ready", "m_turned", "m_hi", "m_lo", "x_updated"))
        u_ready, u_turned, cv_based, cv_done, silu_done = (sem(n) for n in ("u_ready", "u_turned", "cv_based", "cv_done", "silu_done"))
        gv_ready, f_hi, f_lo = sem("gv_ready"), sem("f_hi"), sem("f_lo")
        pmat_landed, fg_landed, p_turned, p_hi, p_lo = (sem(n) for n in ("pmat_landed", "fg_landed", "p_turned", "p_hi", "p_lo"))
        y_turned, y_scaled, y_hi, y_lo, outA, outD, storedS, storedA, fg_applied = (sem(n) for n in (
            "y_turned", "y_scaled", "y_hi", "y_lo", "outA", "outD", "storedS", "storedA", "fg_applied"))

        W = {n: A[n][0].rearrange("(k p) n -> p k n", p=P) for n in
             ("w_in", "w_mq_up", "w_mkv_up", "w_pa", "w_pb", "w_o", "w_up", "w_down", "pool_w_in_2", "pool_w_out_2")}
        w_grp = A["pool_w_grp_2"][0].rearrange("g (k p) n -> p g k n", p=P)
        ada_src = [A["w_ada"][0].rearrange("(p t) n -> p t n", t=16), A["w_mod_2"][0].rearrange("(p t) n -> p t n", t=16)]
        xv = A["x"][0].rearrange("(t p) n -> p t n", p=P)
        outv = out[0].rearrange("(t p) n -> p t n", p=P)
        qi = p2[:, 0:2048].rearrange("p (t h d) -> p t h d", t=TOK, h=IH)
        mql = p2[:, 2048:3072].rearrange("p (t d) -> p t d", t=TOK)
        mq = p2[:, :].rearrange("p (a d) -> p a d", d=MD)
        oTA = pq[:, :, :].rearrange("p (h t) d -> p h (t d)", t=TOK)
        oTB = p2[:, :].rearrange("p (h x) -> p h x", h=H)
        qiT = mkv
        merged = cv[:, 0:4, :].rearrange("p a n -> p (a n)").rearrange("p (t n) -> p t n", t=TOK)
        gv2 = gv[:, :, :].rearrange("p a n -> p (a n)").rearrange("p (t n) -> p t n", t=TOK)
        fgain = cv[:, :, :].rearrange("p a n -> p (a n)")
        lat_tmp = tmp[:, 0:1024].rearrange("p (a n) -> p a n", a=2)

        def banks(chunk):
            return [M[2], M[3]] if chunk == 2 else acc[chunk % 2]

        def bank2(m):
            return m[:, :].rearrange("p (a n) -> p a n", a=2)

        block = ctx.enter_context(nc.Block())

        @block.sync
        def _(sp):
            def tile_in(tb, off, src):
                if tb >= RAW:
                    sp.wait_ge(lo_ready, tb - RAW + 1 + off)
                sp.dma_start(raw[:, tb % RAW, :, :], src).then_inc(raw_landed[tb % RAW], 16)

            def start_in(n):
                q, r, j = n // 8, n // 4 % 2, n % 4
                if n >= 4:
                    sp.wait_ge(ada_used, n - 3)
                sp.dma_start(start_ring[:, n % 4, :].rearrange("p (a n) -> p a n", a=4),
                             ada_src[0][:, 4 * j:4 * j + 4, r * D + q * NC:r * D + (q + 1) * NC]).then_inc(start_landed[n % 4], 16)

            sp.dma_start(craw[:, 0, :], A["c"][0].rearrange("(p t) -> p t", t=16)).then_inc(consts_landed, 16)
            sp.dma_start(craw[:, 1, :], A["c_2"][0].rearrange("(p t) -> p t", t=16)).then_inc(consts_landed, 16)
            for n in range(4):
                start_in(n)
            sp.dma_start(ident[:, :], A["identity"]).then_inc(vec_landed, 16)
            for v, name, lo, n in ((V_GATTN, "g_attn", 0, 16), (V_GFFN, "g_ffn", 0, 16), (V_SHA, "b_ada", 0, 32),
                                   (V_SHF, "b_ada", 3 * D, 32), (V_SH2, "b_mod_2", 0, 32)):
                sp.dma_start(vstage[v:v + n, 0, :],
                             A[name][0, lo:lo + n * P].rearrange("(a b) -> a b", b=P)).then_inc(vec_landed, 16)
            for v, name, n in ((0, "pool_scale_2", 16), (16, "g_mq_lat", 4), (20, "g_mkv_lat", 2)):
                sp.dma_start(vstage[v:v + n, 1, :], A[name][0].rearrange("(a b) -> a b", b=P)).then_inc(vec_landed, 16)
            for j in range(3):
                sp.dma_start(vstage[0:88, 2 + j, :], A["w_conv"][0, j].rearrange("(a b) -> a b", b=P)).then_inc(vec_landed, 16)
            sp.dma_start(vstage[0:88, 5, :], A["b_conv"][0].rearrange("(a b) -> a b", b=P)).then_inc(vec_landed, 16)
            sp.dma_start(xs[:, :, :], xv).then_inc(x_landed, 16)
            for n in range(4, 8):
                start_in(n)

            cols = [None, C_QI, C_QI + NC, C_MQ, C_KA, C_QA, C_QA + NC]
            n = 8
            for t in range(56):
                c, k = in_tile(t)
                wk = W["w_in"][:, 2 * k:2 * k + 2, :]
                if c:
                    tile_in(t, 0, wk[:, :, cols[c]:cols[c] + NC])
                else:
                    if t >= RAW:
                        sp.wait_ge(lo_ready, t - RAW + 1)
                    sp.dma_start(raw[:, t % RAW, :, 0:432], wk[:, :, C_GATE - 432:C_GATE]).then_inc(raw_landed[t % RAW], 16)
                    sp.dma_start(raw[:, t % RAW, :, 432:512], wk[:, :, C_KI:C_KI + 80]).then_inc(raw_landed[t % RAW], 16)
                if t < 18:
                    for _ in range(3 if t % 6 == 5 else 1):
                        start_in(n)
                        n += 1
            assert n == 32
            t = 56
            for c in range(4):
                lo = min(2 * MD * c, 8 * MD - NC)
                for k in range(2):
                    tile_in(t, 0, W["w_mq_up"][:, 2 * k:2 * k + 2, lo:lo + NC])
                    t += 1
            for c in range(4):
                tile_in(t, 0, W["w_mkv_up"][:, 0:2, c * NC:(c + 1) * NC])
                t += 1

            def cut(w, j, c, base=0, first=0):
                return w[:, first + 2 * j:first + 2 * j + 2, bass.ds(c * NC + base, NC)]

            def stream(name, w, base=0, first=0):
                t0, _, n, k = PHASES[name]
                assert k == 8
                with sp.Fori(0, n) as i:
                    for j in range(8):
                        tile_in(t0 + j, i * 8, cut(w, j, i, base, first))

            stream("gate", W["w_in"], C_GATE)
            with sp.Fori(0, 4) as i:
                for j in range(8):
                    tile_in(PHASES["proj"][0] + j, i * 8, cut(W["w_pa"] if j < 4 else W["w_pb"], j % 4, i))
            stream("wo", W["w_o"])
            for part, pairs in enumerate(PAIRS):
                with sp.Fori(0, pairs) as i:
                    for j in range(16):
                        tile_in(PHASES[f"up{part}"][0] + j, i * 16,
                                cut(W["w_up"], j % 8, i, 4 * part * NC + (D_FF if j >= 8 else 0)))
                if part < 2:
                    stream(f"down{part}", W["w_down"], 0, 16 * part)
            t = PHASES["down2"][0]
            for c in range(4):
                for j in range(6):
                    tile_in(t, 0, W["w_down"][:, 32 + 2 * j:34 + 2 * j, c * NC:(c + 1) * NC])
                    t += 1
            with sp.Fori(0, 4) as i:
                for j in range(8):
                    tile_in(PHASES["pin"][0] + j, i * 8, cut(W["pool_w_in_2"], j, i))
            t = PHASES["gp0"][0]
            for n in range(4):
                for j in range(8):
                    tile_in(t, 0, W["pool_w_in_2"][:, 2 * j:2 * j + 2, D + n * NC:D + (n + 1) * NC])
                    t += 1
                for j in range(2):
                    tile_in(t, 0, w_grp[:, n, 2 * j:2 * j + 2, :])
                    t += 1
            stream("pout", W["pool_w_out_2"])
            for h in range(2):
                sp.wait_ge(outD, h + 1)
                sp.dma_start(outv[:, 0, h * D // 2:(h + 1) * D // 2], X[:, 0, h * D // 2:(h + 1) * D // 2]).then_inc(storedS, 16)
            sp.wait_ge(storedS, 32)

        @block.gpsimd
        def _(pool):
            nc.gpsimd.memset(ones[:, :], 1.0).then_inc(ones_ready, 1)

            def ada_in(n, off=0):
                src, reg = REGION_SRC[n // 16]
                if n >= 34:
                    pool.wait_ge(ada_used, n - 1 + off)
                tile = ada_src[src][:, bass.ds(off + n % 16, 1), reg * D:(reg + 1) * D].rearrange("p a n -> p (a n)")
                pool.dma_start(ada_ring[:, n % 2, :], tile).then_inc(ada_landed[n % 2], 16)

            pool.wait_ge(nrm_lo, 6)
            ada_in(32)
            ada_in(33)
            pool.wait_ge(nrm_lo, 8)
            pool.dma_start(causal[:, :, :], A["causal"]).then_inc(att_landed, 16)
            col = 0
            for name, n in (("g_qa", HD), ("g_ka", HD), ("g_qm", MD), ("g_km", MD)):
                pool.dma_start(gains[:, col:col + n], A[name].broadcast_to([P, n])).then_inc(att_landed, 16)
                col += n
            pool.dma_start(posf[:, 0, :].bitcast(I32), A["positions"].rearrange("a (t p) -> p (a t)", p=P),
                           allow_slow_non_contiguous=True).then_inc(att_landed, 16)
            pool.dma_start(tabs[:, 1, 0, :], A["inv_freq"].broadcast_to([P, 56])).then_inc(att_landed, 16)
            for n in range(34, 48):
                ada_in(n)
            with pool.Fori(0, 8) as i:
                for j in range(2):
                    ada_in(16 * GT_A + j, i * 2)
            ada_in(16 * SC_F)
            ada_in(16 * SC_F + 1)
            pool.wait_ge(o_lo, 4)
            pool.wait_ge(gstage_free, 16 * 9)
            pool.dma_start(U[:, 0, :, :], gates_dram[0]).then_inc(gate_loaded[0], 16)
            pool.dma_start(U[:, 1, :, :], gates_dram[4]).then_inc(gate_loaded[1], 16)
            pool.dma_start(gt[:, :], A["b_ada"][:, 2 * D:3 * D].broadcast_to([P, D])).then_inc(bias_landed, 16)
            pool.dma_start(X[:, :, :], xv).then_inc(res_landed, 16)
            _, c0, _, _ = PHASES["proj"]
            with pool.Fori(0, 3) as i:
                for cc in range(2):
                    ada_in(16 * SC_F + 2 + cc, i * 2)
                    pool.wait_ge(chunk_evac, i * 2 + (c0 + cc + 1))
                    pool.dma_start(U[:, cc, :, :], gates_dram[bass.ds(i + (4 * cc + 1), 1), :, :, :]
                                   .rearrange("a p t n -> p (a t) n")).then_inc(gate_loaded[cc], 16)
            with pool.Fori(0, 4) as i:
                for j in range(2):
                    ada_in(16 * SC_F + 8 + j, i * 2)
            pool.wait_ge(x_updated, 4)
            pool.dma_start(gt[:, :], A["b_ada"][:, 5 * D:6 * D].broadcast_to([P, D])).then_inc(bias_landed, 16)
            for r in (GT_F, SH_2, SC_2, GT_2):
                with pool.Fori(0, 8) as i:
                    for j in range(2):
                        ada_in(16 * r + j, i * 2)
            pool.wait_ge(f_lo, sum(PAIRS))
            pool.dma_start(cv[:, :, :], A["pool_matrix"]).then_inc(pmat_landed, 16)
            pool.wait_ge(x_updated, 16)
            pool.dma_start(gt[:, :], A["b_mod_2"][:, 2 * D:3 * D].broadcast_to([P, D])).then_inc(bias_landed, 16)
            pool.wait_ge(p_turned, 8)
            pool.dma_start(fgain, A["final_norm_g_2"].rearrange("(a n) -> a n", a=1).broadcast_to([P, D])).then_inc(fg_landed, 16)

        @block.scalar
        def _(act):
            def split(tb, off=0):
                if tb >= TILES:
                    return
                act.wait_ge(raw_landed[tb % RAW], 16 * (tb // RAW + 1 + (tb >= IN_PIECES[tb % RAW])) + off * 2)
                if tb >= RING:
                    act.wait_ge(tile_used, tb - RING + 1 + off)
                nc.scalar.copy(whi[:, tb % RING, :, :], raw[:, tb % RAW, :, :]).then_inc(hi_ready, 1)

            norms = [0]

            def sqrt_of_norm():
                norms[0] += 1
                act.wait_ge(ms_ready, norms[0])
                nc.scalar.activation(stat[:, 1, 0:TOK], stat[:, 0, 0:TOK], ACT.Sqrt).then_inc(sqrt_ready, 1)

            pairs = [0]

            def norm_hi(tmpv, hi, k0, npair):
                for b in range(npair):
                    act.wait_ge(nrm_evac, pairs[0] + 1)
                    nc.scalar.copy(hi[:, k0 + 2 * b:k0 + 2 * b + 2, :].rearrange("p a n -> p (a n)"),
                                   tmpv[:, pairs[0] % 2, :]).then_inc(nrm_hi, 1)
                    pairs[0] += 1

            def chunk_of(name, c, i=0, per=1):
                t0, c0, _, k = PHASES[name]
                act.wait_ge(tile_used, i * (per * k) + (t0 + (c + 1) * k))
                return acc[(c0 + c) % 2]

            act.wait_ge(consts_landed, 32)
            nc.scalar.activation(cact[:, :, :], craw[:, :, :], ACT.Silu).then_inc(c_ready, 1)
            act.wait_ge(x_landed, 16)
            act.wait_ge(ssq_cleared, 1)
            for t in range(TOK):
                if t:
                    act.wait_ge(xsq_done, t)
                nc.scalar.activation(sqdump[:, :], xs[:, t, :], ACT.Square, accum_out=ssq[:, t, 0:1]).then_inc(xsq_done, 1)
            sqrt_of_norm()
            for q in range(4):
                norm_hi(start_tmp, sa_hi, 4 * q, 2)
                if q < 3:
                    for t in range(6 * q, 6 * q + 6):
                        split(t)

            order = Order(act, act_order)
            done = [18]

            def ahead(n):
                while done[0] < n:
                    split(done[0])
                    done[0] += 1

            def evac_in(c):
                act.wait_ge(tile_used, 20 + 2 * c if c < 3 else 8 * c + 8)
                pair = banks(c)
                for t in range(TOK):
                    ps = pair[t][:, :]
                    if c == 0:
                        dst, ps = pm[:, t, :], pair[t][:, 112:512]
                    elif c < 3:
                        dst, ps = qi[:, t, 8 * (c - 1):8 * c, :], ps.rearrange("p (h d) -> p h d", d=ID)
                    elif c == 3:
                        dst = mql[:, t, :]
                    elif c == 4:
                        dst = pkv[:, t, :]
                    else:
                        dst = pq[:, :, :].rearrange("p (h t) d -> p t h d", t=TOK)[:, t, 4 * (c - 5):4 * (c - 4), :]
                        ps = ps.rearrange("p (h d) -> p h d", d=HD)
                    last = nc.scalar.copy(dst, ps)
                last.then_inc(chunk_evac, 1)
                act.wait_ge(chunk_evac, c + 1)

            def square_sum(v, dst, at):
                return nc.scalar.activation(dump[:, at:at + v.shape[-1]], v, ACT.Square, accum_out=dst)

            ahead(24)
            evac_in(0)
            for t in range(TOK):
                order.link(square_sum(pm[:, t, 0:KVLORA], rstd[:, TOK + t:TOK + t + 1], 0))
            ahead(26)
            evac_in(1)
            act.wait_ge(ang_ready, 1)
            nc.scalar.activation(tabs[:, :, :, :], tabs[:, :, :, :], ACT.Sin).then_inc(tab_ready, 1)
            ahead(28)
            evac_in(2)
            ahead(32)
            for b in range(4):
                act.wait_ge(qi_turned, b + 1)
                nc.scalar.copy(qiT[:, 2 * b:2 * b + 2, :].rearrange("p a n -> p (a n)"), M[b][:, :]).then_inc(qi_evac, 1)
            ahead(33)
            act.wait_ge(qi_turned, 5)
            nc.scalar.copy(kiT[:, :], M[0][:, 0:S]).then_inc(qi_evac, 1)
            ahead(36)
            evac_in(3)
            for t in range(TOK):
                order.link(square_sum(mql[:, t, :], rstd[:, t:t + 1], 0))
            nc.scalar.copy(warm[:, :], rstd[:, 0:1]).then_inc(xsq_done, 1)
            ahead(38)
            norms[0] += 1
            act.wait_ge(ms_ready, norms[0])
            nc.scalar.activation(stat[:, 1, :], stat[:, 0, :], ACT.Sqrt).then_inc(sqrt_ready, 1)
            ahead(42)
            norm_hi(lat_tmp, lat_hi, 0, 3)
            ahead(44)
            evac_in(4)
            for g in range(GROUPS):
                for t in range(TOK):
                    last = square_sum(pkv[:, t, g * HD:(g + 1) * HD], hstat[:, 0, 2 * t + g:2 * t + g + 1], (2 * g + t) * HD)
            order.link(last)
            for b in range(4):
                ahead(46 + 2 * b)
                if b == 3:
                    evac_in(5)
                for h in range(4 * b, 4 * b + 4):
                    act.wait_ge(dots_ready, h + 1)
                    if h >= 4:
                        act.wait_ge(relu_used, h - 3)
                    nc.scalar.activation(tmp[:, 512 * (h % 4):512 * (h % 4 + 1)], M[h % 4][:, :], ACT.Relu).then_inc(relu_ready, 1)

            def query_squares(half):
                for t in range(TOK):
                    for h in range(4):
                        a = 8 * half + 2 * h + t
                        last = square_sum(pq[:, a, :], hstat[:, 0, 4 + a:5 + a], h * HD)
                    order.link(last)

            query_squares(0)
            ahead(58)
            act.wait_ge(hs_ms, 1)
            nc.scalar.activation(hstat[:, 1, 0:4], hstat[:, 0, 0:4], ACT.Sqrt).then_inc(hs_sqrt, 1)
            ahead(60)
            evac_in(6)
            query_squares(1)
            t0 = PHASES["mq"][0]
            for c in range(4):
                ahead(t0 + 2 * c + 2 + RING)
                if c == 1:
                    act.wait_ge(k_turned, 1)
                    nc.scalar.copy(kT[:, :, :].rearrange("p a n -> p (a n)"), M[0][:, :]).then_inc(k_evac, 1)
                pair = chunk_of("mq", c)
                skip = 2 * MD * c - min(2 * MD * c, 8 * MD - NC)
                for t in range(TOK):
                    last = nc.scalar.copy(mq[:, :, :].rearrange("p (h t) d -> p t h d", t=TOK)[:, t, 2 * c:2 * c + 2, :],
                                          pair[t][:, skip:skip + 2 * MD].rearrange("p (h d) -> p h d", d=MD))
                last.then_inc(chunk_evac, 1)
                act.wait_ge(chunk_evac, 8 + c)
                for b in range(2):
                    for a in (4 * c + 2 * b, 4 * c + 2 * b + 1):
                        last = square_sum(mq[:, a, :], hstat[:, 0, 20 + a:21 + a], (a % 2) * MD)
                    order.link(last)
            t0 = PHASES["mkv"][0]
            for c in range(4):
                ahead(t0 + c + 1 + RING)
                pair = chunk_of("mkv", c)
                for t in range(TOK):
                    last = nc.scalar.copy(mkv[:, :, :].rearrange("p (h t) d -> p t h d", t=TOK)[:, t, 2 * c:2 * c + 2, :],
                                          pair[t][:, :].rearrange("p (h d) -> p h d", d=256))
                last.then_inc(chunk_evac, 1)
                act.wait_ge(chunk_evac, 12 + c)
                for a in range(4 * c, 4 * c + 4):
                    last = square_sum(mkv[:, a, 0:NOPE], hstat[:, 0, 36 + a:37 + a], (a % 4) * NOPE)
                order.link(last)
            for t in range(TOK):
                last = square_sum(pm[:, t, KVLORA:KVLORA + MROT], hstat[:, 0, 52 + t:53 + t], t * MROT)
            order.link(last)
            nc.scalar.copy(warm[:, :], hstat[:, 0, 52:53]).then_inc(hs_ready, 1)
            act.wait_ge(hs_ms, 2)
            nc.scalar.activation(hstat[:, 1, 4:52], hstat[:, 0, 4:52], ACT.Sqrt).then_inc(hs_sqrt, 1)
            act.sem_inc(gstage_free, 16)

            def gates_out(c, i):
                _, c0, _, _ = PHASES["gate"]
                pair = chunk_of("gate", c, i, 2)
                act.wait_ge(gstage_free, i * 32 + 16 * (c + 1))
                for t in range(TOK):
                    last = nc.scalar.activation(gstage[:, t, :], pair[t][:, :], ACT.Sigmoid)
                last.then_inc(chunk_evac, 1)
                act.wait_ge(chunk_evac, i * 2 + (c0 + c + 1))
                act.dma_start(gates_dram[bass.ds(i * 2 + c, 1), :, :, :].rearrange("a p t n -> p (a t) n"),
                              gstage[:, :, :]).then_inc(gstage_free, 16)

            def exps(pr, s, h, maxed, exped):
                act.wait_ge(maxed, h + 1)
                for t in range(TOK):
                    last = nc.scalar.activation(pr[:, s, t, :], pr[:, s, t, :], ACT.Exp, bias=smax[:, s, 0, t:t + 1],
                                                accum_out=smax[:, s, 1, t:t + 1])
                last.then_inc(exped, 1)

            def o_out(oT, h, ready, bank, done):
                act.wait_ge(ready, h + 1)
                nc.scalar.copy(oT[:, bass.ds(h, 1), 0:S].rearrange("p a n -> p (a n)"), bank[:, 0:S]).then_inc(done, 1)

            with act.Fori(0, 2) as i:
                nc.scalar.copy(vA[:, :, :], pkv[:, :, bass.ds(i * HD + 256, HD)]).then_inc(A_v, 1)
                for c in range(2):
                    tb, off, h = PHASES["gate"][0] + 8 * c + RING, i * 16, i * 4 + 2 * c
                    split(tb, off)
                    for s in range(2):
                        split(tb + 1 + s, off)
                        act.wait_ge(A_turned, h + s + 1)
                        nc.scalar.copy(qTA[:, s, :], M[0][:, s * S:(s + 1) * S]).then_inc(A_qT, 1)
                    split(tb + 3, off)
                    exps(prA, 0, h, A_maxed, A_exp)
                    split(tb + 4, off)
                    act.wait_ge(A_pT, h + 1)
                    nc.scalar.copy(pTA[:, 0, :], M[3][:, 0:384]).then_inc(A_pT_evac, 1)
                    exps(prA, 1, h + 1, A_maxed, A_exp)
                    split(tb + 5, off)
                    o_out(oTA, h, A_o, M[1], A_o_evac)
                    split(tb + 6, off)
                    act.wait_ge(A_pT, h + 2)
                    nc.scalar.copy(pTA[:, 1, :], M[0][:, 0:384]).then_inc(A_pT_evac, 1)
                    split(tb + 7, off)
                    o_out(oTA, h + 1, A_o, M[2], A_o_evac)
                    gates_out(c, i)
            with act.Fori(0, 2) as i:
                for c in range(2):
                    tb, off, h = PHASES["gate"][0] + 32 + 8 * c + RING, i * 16, i * 4 + 2 * c
                    nc.scalar.copy(vB[:, :, :, :].rearrange("p s t d -> p (s t) d"), mkv[:, bass.ds(h * 2, 4), NOPE:NOPE + MV]).then_inc(B_v, 1)
                    split(tb, off)
                    split(tb + 1, off)
                    act.wait_ge(B_turned, h + 1)
                    nc.scalar.copy(nT[:, 0, :, :].rearrange("p a n -> p (a n)"), M[0][:, :]).then_inc(B_nT, 1)
                    split(tb + 2, off)
                    split(tb + 3, off)
                    act.wait_ge(B_turned, h + 2)
                    nc.scalar.copy(nT[:, 1, :, :].rearrange("p a n -> p (a n)"), M[2][:, :]).then_inc(B_nT, 1)
                    split(tb + 4, off)
                    exps(prB, 0, h, B_maxed, B_exp)
                    split(tb + 5, off)
                    act.wait_ge(B_pT, h + 1)
                    nc.scalar.copy(pTB[:, 0, :], M[0][:, 0:384]).then_inc(B_pT_evac, 1)
                    exps(prB, 1, h + 1, B_maxed, B_exp)
                    split(tb + 6, off)
                    o_out(oTB, h, B_o, M[1], B_o_evac)
                    act.wait_ge(B_pT, h + 2)
                    nc.scalar.copy(pTB[:, 1, :], M[2][:, 0:384]).then_inc(B_pT_evac, 1)
                    split(tb + 7, off)
                    o_out(oTB, h + 1, B_o, M[3], B_o_evac)
                    gates_out(4 + c, i)

            act.wait_ge(B_o_evac, H)
            for b in range(2):
                nc.scalar.copy(sa_hi[:, 8 + 4 * b:12 + 4 * b, :], oTB[:, 4 * b:4 * b + 4, 0:S]).then_inc(o_hi, 1)

            def merged_hi(n):
                for q in range(2):
                    act.wait_ge(m_turned, n * 2 + (q + 1))
                    nc.scalar.copy(sb_hi[:, bass.ds(n * 4 + 2 * q, 2), :], bank2(M[q])).then_inc(m_hi, 1)

            t0 = PHASES["proj"][0] + RING
            for j in range(8):
                split(t0 + j)
            with act.Fori(0, 3) as i:
                for j in range(8):
                    split(t0 + 8 + j, i * 8)
                    if j == 3:
                        merged_hi(i)

            def squares(name, c, i=0):
                act.wait_ge(x_updated, i * 2 + (UPDATES[name] + c + 1))
                for t in range(TOK):
                    last = nc.scalar.activation(U[:, 0, t, :], X[:, t, bass.ds(i * 2 * NC + c * NC, NC)], ACT.Square,
                                                accum_out=ssq[:, t, bass.ds(i * 2 + c, 1)])
                last.then_inc(xsq_done, 1)

            nc.scalar.activation(warm[:, :], ident[:, 0:1], ACT.Sqrt)
            t0 = PHASES["wo"][0] + RING
            for c in range(4):
                for j in range(8):
                    if c == 0 and j == 3:
                        merged_hi(3)
                    split(t0 + 8 * c + j)
                squares("wo", c)
            sqrt_of_norm()
            norm_hi(gv2, sa_hi, 0, 8)

            def conv_base(side, pg):
                for q in range(2):
                    act.wait_ge(u_turned, pg * 4 + (2 * side + q + 1))
                    for b in range(2):
                        col = pg * 4 + (44 * side + 2 * q + b)
                        last = nc.scalar.activation(cv[:, 4 * side + 2 * q + b, :], M[2 * side + q][:, b * S:(b + 1) * S],
                                                    ACT.Identity, bias=cvec[:, 3, bass.ds(col, 1)], scale=cvec[:, 2, bass.ds(col, 1)])
                last.then_inc(cv_based, 1)

            def ffn_hi(pg, pl):
                act.wait_ge(gv_ready, pg + 1)
                nc.scalar.copy(sb_hi[:, bass.ds(pl * 4, 4), :], gv[:, :, :]).then_inc(f_hi, 1)

            def up_pair(part, i, shift, first):
                t0 = PHASES[f"up{part}"][0] + 16 * shift
                off = i * 16
                pl = i + shift
                pg = i + (shift + 4 * part)
                for j in range(4):
                    split(t0 + RING + j, off)
                if not first:
                    conv_base(1, i + (shift + 4 * part - 1))
                split(t0 + RING + 4, off)
                split(t0 + RING + 5, off)
                if not first:
                    ffn_hi(i + (shift + 4 * part - 1), i + (shift - 1))
                split(t0 + RING + 6, off)
                split(t0 + RING + 7, off)
                pair = chunk_of(f"up{part}", 2 * shift, i, 2)
                for t in range(TOK):
                    last = nc.scalar.copy(U[:, 0, t, :], pair[t][:, :])
                last.then_inc(chunk_evac, 1)
                for j in range(4):
                    split(t0 + RING + 8 + j, off)
                conv_base(0, pg)
                split(t0 + RING + 12, off)
                split(t0 + RING + 13, off)
                act.wait_ge(cv_done, pg * 2 + 1)
                nc.scalar.activation(cv[:, 0:4, :], cv[:, 0:4, :], ACT.Silu).then_inc(silu_done, 1)
                split(t0 + RING + 14, off)
                split(t0 + RING + 15, off)
                pair = chunk_of(f"up{part}", 2 * shift + 1, i, 2)
                for t in range(TOK):
                    last = nc.scalar.copy(U[:, 1, t, :], pair[t][:, :])
                last.then_inc(chunk_evac, 1)

            for part, n in enumerate(PAIRS):
                up_pair(part, 0, 0, True)
                with act.Fori(0, n - 1) as i:
                    up_pair(part, i, 1, False)
                t0, _, _, k = PHASES[f"down{part}"]
                for c in range(4):
                    for j in range(k):
                        if c == 0 and j == (2 if k == 8 else 1):
                            conv_base(1, 4 * part + n - 1)
                        if c == 0 and j == k - 3:
                            ffn_hi(4 * part + n - 1, n - 1)
                        split(t0 + c * k + j + RING)
                    if part == 2:
                        if c == 0:
                            nc.scalar.activation(warm[:, :], ident[:, 0:1], ACT.Sqrt)
                        squares("down2", c)

            sqrt_of_norm()
            norm_hi(gv2, sa_hi, 0, 8)

            def pooled_hi(c):
                for q in range(2):
                    act.wait_ge(p_turned, 2 * c + q + 1)
                    nc.scalar.copy(sb_hi[:, 4 * c + 2 * q:4 * c + 2 * q + 2, :], bank2(M[2 * (c % 2) + q])).then_inc(p_hi, 1)

            t0 = PHASES["pin"][0] + RING
            for c in range(4):
                for j in range(4):
                    split(t0 + 8 * c + j)
                if c:
                    pooled_hi(c - 1)
                for j in range(4, 8):
                    split(t0 + 8 * c + j)
                pair = chunk_of("pin", c)
                for t in range(TOK):
                    last = nc.scalar.copy(U[:, c % 2, t, :], pair[t][:, :])
                last.then_inc(chunk_evac, 1)
            act.wait_ge(ada_used, 144)

            def y_high(n):
                act.wait_ge(y_scaled, n + 1)
                nc.scalar.copy(sb_hi[:, 4 * n:4 * n + 4, :], gv[:, :, :]).then_inc(y_hi, 1)

            for n in range(4):
                t0 = PHASES[f"gp{n}"][0] + RING
                for j in range(4):
                    split(t0 + j)
                if n == 0:
                    pooled_hi(3)
                for j in range(4, 8):
                    split(t0 + j)
                if n:
                    y_high(n - 1)
                pair = chunk_of(f"gp{n}", 0)
                for t in range(TOK):
                    last = nc.scalar.activation(ada_ring[:, t, n * NC:(n + 1) * NC], pair[t][:, :], ACT.Silu)
                last.then_inc(chunk_evac, 1)
                split(t0 + 8)
                split(t0 + 9)
            t0 = PHASES["pout"][0] + RING
            for c in range(4):
                for j in range(8):
                    if c == 0 and j == 5:
                        y_high(3)
                    split(t0 + 8 * c + j)
                if c == 0:
                    nc.scalar.activation(warm[:, :], ident[:, 0:1], ACT.Sqrt)
                squares("pout", c)
            sqrt_of_norm()
            act.wait_ge(fg_applied, 4)
            act.wait_ge(diag_ready, 5)
            for h in range(2):
                half = slice(h * D // 2, (h + 1) * D // 2)
                nc.scalar.activation(X[:, 1, half], X[:, 1, half], ACT.Copy, scale=rstd[:, 1:2]).then_inc(outA, 1)
            for h in range(2):
                half = slice(h * D // 2, (h + 1) * D // 2)
                act.wait_ge(outA, h + 1)
                act.dma_start(outv[:, 1, half], X[:, 1, half]).then_inc(storedA, 16)
            act.wait_ge(storedA, 32)

        @block.vector
        def _(dve):
            V = nc.vector
            order = Order(dve, dve_order)
            link = order.link

            def split(tb, off=0):
                if tb >= TILES:
                    return
                dve.wait_ge(hi_ready, tb + 1 + off)
                V.tensor_tensor(wlo[:, tb % RING, :, :], raw[:, tb % RAW, :, :], whi[:, tb % RING, :, :].bitcast(F32),
                                ALU.subtract).then_inc(lo_ready, 1)

            def ada_begin(r):
                kind, count = summed(r - 1)
                dve.wait_ge(cols_summed if kind == "cols" else rows_summed, count)
                link(V.memset(ada_acc[:, :], 0.0))

            def ada(n, off=0):
                src = REGION_SRC[n // 16][0]
                dve.wait_ge(ada_landed[n % 2], 16 * ((n - 32) // 2 + 1) + off * 8)
                tile = ada_ring[:, n % 2, :]
                dve.wait_ge(ada_used, n + off)
                V.scalar_tensor_tensor(out=ada_acc[:, :], in0=tile, scalar=cact[:, src, bass.ds(off + n % 16, 1)],
                                       in1=ada_acc[:, :], op0=ALU.mult, op1=ALU.add).then_inc(ada_used, 1)

            def shift_ready(r, v):
                dve.wait_ge(cols_summed, summed(r)[1])
                V.tensor_tensor(mod_b[:, :], M[0][:, 0:16], vecs[:, v:v + 16], ALU.add).then_inc(mod_ready, 1)

            def scale_ready(r, v, gain=None):
                dve.wait_ge(cols_summed, summed(r)[1])
                last = V.scalar_tensor_tensor(out=mod_s[:, :], in0=M[0][:, 0:16], scalar=1.0, in1=vecs[:, v:v + 16],
                                              op0=ALU.add, op1=ALU.add)
                if gain is not None:
                    link(last)
                    last = V.tensor_tensor(mod_s[:, :], mod_s[:, :], vecs[:, gain:gain + 16], ALU.mult)
                last.then_inc(mod_ready, 1)

            def gate_ready(r, half, b):
                k = ROWS.index(r)
                dve.wait_ge(bias_landed, 16 * (k + 2))
                dve.wait_ge(rows_summed, 2 * k + half + 1)
                for n in range(2):
                    cols = slice((2 * half + n) * NC, (2 * half + n + 1) * NC)
                    last = V.tensor_tensor(gt[:, cols], M[b + n][:, :], gt[:, cols], ALU.add)
                last.then_inc(gt_ready, 1)

            norms = [0]

            def diagonals(to, col):
                for t in range(TOK):
                    last = V.tensor_scalar(to[:, t, :], ident[:, :], rstd[:, col + t:col + t + 1], None, ALU.mult)
                return last

            def norm_x(squares):
                dve.wait_ge(xsq_done, squares)
                link(V.reduce_sum(rstd[:, 0:TOK], ssq[:, :, :], AX))
                V.tensor_scalar(stat[:, 0, 0:TOK], rstd[:, 0:TOK], 1.0 / D, EPS, ALU.mult, ALU.add).then_inc(ms_ready, 1)
                norms[0] += 1
                dve.wait_ge(sqrt_ready, norms[0])
                link(V.reciprocal(rstd[:, 0:TOK], stat[:, 1, 0:TOK]))
                diagonals(diag, 0).then_inc(diag_ready, 1)

            pairs = [0]

            def norm_lo(tmpv, hi, lo, k0, npair, scale, bias, turned=(0, 1, 2, 3)):
                def low(b, p):
                    dve.wait_ge(nrm_hi, p + 1)
                    V.tensor_tensor(lo[:, k0 + 2 * b:k0 + 2 * b + 2, :].rearrange("p a n -> p (a n)"), tmpv[:, p % 2, :],
                                    hi[:, k0 + 2 * b:k0 + 2 * b + 2, :].rearrange("p a n -> p (a n)").bitcast(F32),
                                    ALU.subtract).then_inc(nrm_lo, 1)

                p0 = pairs[0]
                for b in range(npair):
                    p = p0 + b
                    dve.wait_ge(nrm_turned, p + 1)
                    if b >= 2:
                        dve.wait_ge(nrm_lo, p - 1)
                    for kk in range(2):
                        k = 2 * b + kk
                        if bias is None:
                            last = V.tensor_scalar(tmpv[:, p % 2, kk * S:(kk + 1) * S], M[turned[b % len(turned)]][:, kk * S:(kk + 1) * S],
                                                   scale[:, k:k + 1], None, ALU.mult)
                        else:
                            last = V.tensor_scalar(tmpv[:, p % 2, kk * S:(kk + 1) * S], M[turned[b % len(turned)]][:, kk * S:(kk + 1) * S],
                                                   scale[:, k:k + 1], bias[:, k:k + 1], ALU.mult, ALU.add)
                    last.then_inc(nrm_evac, 1)
                    if b:
                        low(b - 1, p - 1)
                low(npair - 1, p0 + npair - 1)
                pairs[0] += npair
                dve.wait_ge(nrm_lo, pairs[0])

            def start_ada(n):
                q, r, j = n // 8, n // 4 % 2, n % 4
                dve.wait_ge(start_landed[n % 4], 16 * (n // 4 + 1))
                if j:
                    dve.wait_ge(ada_used, n)
                elif q >= 2:
                    dve.wait_ge(cols_summed, 2 * q + r - 3)
                for a in range(4):
                    tile, w = start_ring[:, n % 4, a * NC:(a + 1) * NC], cact[:, 0, 4 * j + a:4 * j + a + 1]
                    at = (q % 2) * 2 + a % 2
                    sums = (ada_acc, start_acc)[r][:, at * NC:(at + 1) * NC]
                    if j or a >= 2:
                        last = V.scalar_tensor_tensor(out=sums, in0=tile, scalar=w, in1=sums, op0=ALU.mult, op1=ALU.add)
                    else:
                        last = V.tensor_scalar(sums, tile, w, None, ALU.mult)
                    if a == 1:
                        link(last)
                last.then_inc(ada_used, 1)

            V.memset(ssq[:, :, :], 0.0).then_inc(ssq_cleared, 1)
            dve.wait_ge(c_ready, 1)
            for q in range(4):
                for j in range(8):
                    if q and j >= 2:
                        split(6 * q - 8 + j)
                    if q == 0 or j >= 2:
                        start_ada(8 * q + j)
                if q == 0:
                    dve.wait_ge(vec_turned, 1)
                    V.tensor_copy(vecs[:, :], M[1][:, 0:NVEC]).then_inc(vec_ready, 1)
                    dve.wait_ge(vec_turned, 2)
                    V.tensor_copy(cvec[:, :, :].rearrange("p a n -> p (a n)"), M[2][:, 0:352]).then_inc(vec_ready, 1)
                    dve.wait_ge(vec_ready, 2)
                    norm_x(TOK)
                if q < 3:
                    start_ada(8 * q + 8)
                    start_ada(8 * q + 9)
                at = slice(4 * q, 4 * q + 4)
                dve.wait_ge(cols_summed, 2 * q + 2)
                V.tensor_tensor(mod_b[:, at], M[0][:, 4 * q:4 * q + 4], vecs[:, V_SHA + 4 * q:V_SHA + 4 * q + 4], ALU.add).then_inc(mod_ready, 1)
                link(V.scalar_tensor_tensor(out=mod_s[:, at], in0=M[0][:, 16 + 4 * q:20 + 4 * q], scalar=1.0,
                                            in1=vecs[:, V_SCA + 4 * q:V_SCA + 4 * q + 4], op0=ALU.add, op1=ALU.add))
                V.tensor_tensor(mod_s[:, at], mod_s[:, at], vecs[:, V_GATTN + 4 * q:V_GATTN + 4 * q + 4], ALU.mult).then_inc(mod_ready, 1)
                dve.wait_ge(mod_ready, 2 * q + 2)
                norm_lo(start_tmp, sa_hi, sa_lo, 4 * q, 2, mod_s[:, at], mod_b[:, at], (1, 0))

            done = [18]

            def ahead(n, adas=0):
                while done[0] < n:
                    split(done[0])
                    done[0] += 1
                for _ in range(adas):
                    ada(ada_next[0])
                    ada_next[0] += 1

            ada_next = [16 * SH_F]

            def rope(v, tab, half, tmpv, axis, shape, done=None):
                co, si = (tabs[:, a, :, tab:tab + half].unsqueeze(axis).broadcast_to([P, *shape, half]) for a in range(2))
                n = shape[0] * shape[1] * half
                a, b, c, d = (tmpv[:, k * n:(k + 1) * n].rearrange("p (x y n) -> p x y n", x=shape[0], y=shape[1]) for k in range(4))
                v1, v2 = v[:, :, :, 0:half], v[:, :, :, half:2 * half]
                V.tensor_tensor(a, v1, co, ALU.mult)
                V.tensor_tensor(b, v2, si, ALU.mult)
                V.tensor_tensor(c, v2, co, ALU.mult)
                link(V.tensor_tensor(d, v1, si, ALU.mult))
                V.tensor_tensor(v1, a, b, ALU.subtract)
                last = V.tensor_tensor(v2, c, d, ALU.add)
                if done is None:
                    link(last)
                else:
                    last.then_inc(done, 1)

            ahead(20)
            ada_begin(SH_F)
            ahead(22, 1)
            dve.wait_ge(att_landed, 16 * 7)
            link(V.tensor_copy(posf[:, 1, :], posf[:, 0, :].bitcast(I32)))
            for t in range(TOK):
                last = V.tensor_scalar(tabs[:, 0, t, :], tabs[:, 1, 0, :], posf[:, 1, t:t + 1], None, ALU.mult)
            link(last)
            link(V.tensor_copy(tabs[:, 1, :, :], tabs[:, 0, :, :]))
            kv = tmp[:, 0:224].rearrange("p (a t n) -> p a t n", a=2, t=TOK)
            for a, turn in ((0, 0.25), (1, 0.0)):
                link(V.tensor_scalar(kv[:, a], tabs[:, a, :, :], 1.0 / TWO_PI, turn, ALU.mult, ALU.add))
            link(V.tensor_scalar(kv, kv, ROUND, None, ALU.add))
            link(V.tensor_scalar(kv, kv, ROUND, None, ALU.subtract))
            flat = tabs[:, :, :, :].rearrange("p a t n -> p (a t n)")
            for part in (PI_HI, PI_MID, PI_LO):
                link(V.scalar_tensor_tensor(out=flat, in0=tmp[:, 0:224], scalar=-part, in1=flat, op0=ALU.mult, op1=ALU.add))
            link(V.tensor_scalar(tabs[:, 0, :, :], tabs[:, 0, :, :], TWO_PI / 4, None, ALU.add))
            V.tensor_scalar(flat, flat, PI_IN, -PI_IN, ALU.min, ALU.max).then_inc(ang_ready, 1)
            for n in (23, 24, 26, 28):
                ahead(n, 1)
            ahead(29)
            dve.wait_ge(chunk_evac, 3)
            dve.wait_ge(tab_ready, 1)
            rope(qi, 16, 8, tmp, 2, (TOK, IH))
            ki = pm[:, :, 320:384]
            rope(ki.unsqueeze(2), 16, 8, tmp, 2, (TOK, 1))
            V.tensor_copy(kirep[:, :, 0:ID], ki)
            V.tensor_copy(kirep[:, :, ID:2 * ID], ki).then_inc(qi_roped, 1)
            link(V.tensor_scalar(pm[:, :, 384:400], pm[:, :, 384:400], float(IH * ID) ** -0.5, None, ALU.mult))
            ahead(32, 1)
            ahead(34, 1)
            ahead(36, 1)
            ahead(37)
            dve.wait_ge(xsq_done, TOK + 1)
            V.tensor_scalar(stat[:, 0, 0:TOK], rstd[:, 0:TOK], 1.0 / QLORA, EPS, ALU.mult, ALU.add)
            V.tensor_scalar(stat[:, 0, TOK:2 * TOK], rstd[:, TOK:2 * TOK], 1.0 / KVLORA, EPS, ALU.mult, ALU.add).then_inc(ms_ready, 1)
            norms[0] += 1
            dve.wait_ge(sqrt_ready, norms[0])
            link(V.reciprocal(rstd[:, :], stat[:, 1, :]))
            diagonals(diag, 0)
            diagonals(diag2, TOK).then_inc(diag_ready, 1)
            ahead(40, 1)
            ahead(42)
            norm_lo(lat_tmp, lat_hi, lat_lo, 0, 3, vecs[:, V_GMQ:V_GMQ + 6], None)
            ahead(44, 1)
            for b in range(4):
                ahead(46 + 2 * b)
                for h in range(4 * b, 4 * b + 4):
                    dve.wait_ge(relu_ready, h + 1)
                    if h:
                        dve.wait_ge(relu_used, h)
                    for t in range(TOK):
                        r = tmp[:, 512 * (h % 4) + S * t:512 * (h % 4) + S * (t + 1)]
                        last = V.scalar_tensor_tensor(out=selbias[:, t, :], in0=r, scalar=pm[:, t, 384 + h:385 + h],
                                                      in1=causal[:, t, :] if h == 0 else selbias[:, t, :], op0=ALU.mult, op1=ALU.add)
                    last.then_inc(relu_used, 1)
            dve.wait_ge(relu_used, IH)
            for b in range(4):
                ahead(53 + b)
                for _ in range(TOPK // 16):
                    link(V.max(out=m8[:, :], in_=selbias[:, b // 2, :]))
                    link(V.match_replace(out=selbias[:, b // 2, :], in_to_replace=m8[:, :], in_values=selbias[:, b // 2, :], imm_value=TAKEN))
            link(V.tensor_scalar(selbias[:, :, :], selbias[:, :, :], TAKEN / 2, MASKED, ALU.is_gt, ALU.mult))
            link(V.tensor_tensor(selbias[:, :, :], selbias[:, :, :], causal[:, :, :], ALU.add))
            ahead(57)
            V.tensor_scalar(hstat[:, 0, 0:4], hstat[:, 0, 0:4], 1.0 / HD, EPS, ALU.mult, ALU.add).then_inc(hs_ms, 1)
            dve.wait_ge(hs_sqrt, 1)
            link(V.reciprocal(hstat[:, 1, 0:4], hstat[:, 1, 0:4]))
            for t in range(TOK):
                for g in range(GROUPS):
                    k = pkv[:, t, g * HD:(g + 1) * HD]
                    last = V.scalar_tensor_tensor(out=k, in0=k, scalar=hstat[:, 1, 2 * t + g:2 * t + g + 1], in1=gains[:, HD:2 * HD],
                                                  op0=ALU.mult, op1=ALU.mult)
            link(last)
            rope(pkv[:, :, 0:256].rearrange("p t (g d) -> p t g d", g=GROUPS), 0, 16, tmp, 2, (TOK, GROUPS), k_normed)
            dve.wait_ge(k_normed, 1)
            kr = pm[:, :, KVLORA:KVLORA + MROT]
            link(V.tensor_tensor(kbase[:, :, :], kr, gains[:, 448 + NOPE:640].unsqueeze(1).broadcast_to([P, TOK, MROT]), ALU.mult))
            rope(kbase[:, :, :].unsqueeze(2), 24, 32, tmp, 2, (TOK, 1), kbase_ready)
            dve.wait_ge(kbase_ready, 1)
            for n in (60, 61, 62, 63, 64, 66):
                ahead(n, 1)
            assert ada_next[0] == 16 * GT_A, ada_next[0]
            ahead(72)
            shift_ready(SH_F, V_SHF)
            ada_begin(GT_A)
            dve.wait_ge(hs_ready, 1)
            km = hstat[:, 0, 36:52].rearrange("p (h t) -> p h t", t=TOK)
            link(V.tensor_tensor(km, km, hstat[:, 0, 52:54].unsqueeze(1).broadcast_to([P, H, TOK]), ALU.add))
            V.tensor_scalar(hstat[:, 0, 4:20], hstat[:, 0, 4:20], 1.0 / HD, EPS, ALU.mult, ALU.add)
            V.tensor_scalar(hstat[:, 0, 20:52], hstat[:, 0, 20:52], 1.0 / MD, EPS, ALU.mult, ALU.add).then_inc(hs_ms, 1)
            dve.wait_ge(hs_sqrt, 2)
            link(V.reciprocal(hstat[:, 1, 4:52], hstat[:, 1, 4:52]))

            def head_rstd(i, at):
                return hstat[:, 1, bass.ds(i * 8 + at, 1)]

            def row(v, i, at, width):
                return v[:, bass.ds(i * 8 + at, 1), 0:width].rearrange("p a n -> p (a n)")

            def logits_in(pr, s, bank, bias, width, ready, h, maxed):
                dve.wait_ge(ready, h + 1)
                link(V.scalar_tensor_tensor(out=pr[:, s, :, :].rearrange("p a n -> p (a n)"), in0=bank[:, :], scalar=float(width) ** -0.5,
                                            in1=bias[:, :, :].rearrange("p a n -> p (a n)"), op0=ALU.mult, op1=ALU.add))
                V.tensor_reduce(smax[:, s, 0, :], pr[:, s, :, :], AX, ALU.max, negate=True).then_inc(maxed, 1)

            def normalise(pr, s, h, exped, probs):
                dve.wait_ge(exped, h + 1)
                link(V.reciprocal(smax[:, s, 1, :], smax[:, s, 1, :]))
                for t in range(TOK):
                    last = V.tensor_scalar(pr[:, s, t, :], pr[:, s, t, :], smax[:, s, 1, t:t + 1], None, ALU.mult)
                last.then_inc(probs, 1)

            def stage_A(i, c, s):
                for t in range(TOK):
                    a = 4 * c + 2 * s + t
                    last = V.scalar_tensor_tensor(out=qsA[:, s, t, :], in0=row(pq, i, a, HD), scalar=head_rstd(i, 4 + a),
                                                  in1=gains[:, 0:HD], op0=ALU.mult, op1=ALU.mult)
                link(last)
                rope(qsA[:, s, :, :].unsqueeze(2), 0, 16, ropeA, 2, (TOK, 1), A_staged)

            with dve.Fori(0, 2) as i:
                order.enter(i, 16)
                for c in range(2):
                    tb, off, h = PHASES["gate"][0] + 8 * c + RING, i * 16, i * 4 + 2 * c
                    stage_A(i, c, 0)
                    split(tb, off)
                    stage_A(i, c, 1)
                    split(tb + 1, off)
                    split(tb + 2, off)
                    logits_in(prA, 0, M[1], selbias, HD, A_logits, h, A_maxed)
                    split(tb + 3, off)
                    normalise(prA, 0, h, A_exp, A_probs)
                    logits_in(prA, 1, M[2], selbias, HD, A_logits, h + 1, A_maxed)
                    split(tb + 4, off)
                    normalise(prA, 1, h + 1, A_exp, A_probs)
                    split(tb + 5, off)
                    for j in range(2):
                        ada(16 * GT_A + 2 * c + j, i * 4)
                        split(tb + 6 + j, off)
                order.leave(2)

            def stage_B(i, c, s):
                for t in range(TOK):
                    a = 4 * c + 2 * s + t
                    V.scalar_tensor_tensor(out=ksB[:, s, t, 0:NOPE], in0=row(mkv, i, a, NOPE), scalar=head_rstd(i, 36 + a),
                                           in1=gains[:, 448:448 + NOPE], op0=ALU.mult, op1=ALU.mult)
                    V.tensor_scalar(ksB[:, s, t, NOPE:MD], kbase[:, t, :], head_rstd(i, 36 + a), None, ALU.mult)
                    last = V.scalar_tensor_tensor(out=qsB[:, s, t, :], in0=row(mq, i, a, MD), scalar=head_rstd(i, 20 + a),
                                                  in1=gains[:, 256:448], op0=ALU.mult, op1=ALU.mult)
                link(last)
                rope(qsB[:, s, :, NOPE:MD].unsqueeze(2), 24, 32, ropeB, 2, (TOK, 1), B_staged)

            def rotated_out(s, h):
                dve.wait_ge(B_turned, h + 1)
                V.tensor_copy(rT[0:MROT, s, :, :].rearrange("p a n -> p (a n)"), M[1 + 2 * s][0:MROT, :]).then_inc(B_rT, 1)

            with dve.Fori(0, 2) as i:
                order.enter(i, 16)
                for c in range(2):
                    tb, off, h = PHASES["gate"][0] + 32 + 8 * c + RING, i * 16, i * 4 + 2 * c
                    stage_B(i, c, 0)
                    split(tb, off)
                    stage_B(i, c, 1)
                    split(tb + 1, off)
                    rotated_out(0, h)
                    split(tb + 2, off)
                    split(tb + 3, off)
                    rotated_out(1, h + 1)
                    logits_in(prB, 0, M[1], causal, MD, B_logits, h, B_maxed)
                    split(tb + 4, off)
                    normalise(prB, 0, h, B_exp, B_probs)
                    logits_in(prB, 1, M[3], causal, MD, B_logits, h + 1, B_maxed)
                    split(tb + 5, off)
                    normalise(prB, 1, h + 1, B_exp, B_probs)
                    for j in range(2):
                        split(tb + 6 + j, off)
                        ada(16 * GT_A + 8 + 2 * c + j, i * 4)
                order.leave(2)

            dve.wait_ge(tile_used, PHASES["proj"][0])
            dve.wait_ge(A_o_evac, H)
            for b in range(2):
                at = slice(4 * b, 4 * b + 4)
                link(V.tensor_copy(sa_hi[:, at, :], oTA[:, at, :]))
                V.tensor_tensor(sa_lo[:, at, :], oTA[:, at, :], sa_hi[:, at, :].bitcast(F32), ALU.subtract).then_inc(o_lo, 1)
            for b in range(2):
                dve.wait_ge(o_hi, b + 1)
                V.tensor_tensor(sa_lo[:, 8 + 4 * b:12 + 4 * b, :], oTB[:, 4 * b:4 * b + 4, 0:S], sa_hi[:, 8 + 4 * b:12 + 4 * b, :].bitcast(F32),
                                ALU.subtract).then_inc(o_lo, 1)
            dve.wait_ge(cols_summed, summed(GT_A)[1])
            V.tensor_copy(gate_a[:, :], M[0][:, 0:16]).then_inc(mod_ready, 1)
            ada_begin(SC_F)
            dve.wait_ge(o_lo, 4)

            def half(n, side, i=0):
                t0, c0, _, _ = PHASES["proj"]
                dve.wait_ge(tile_used, i * 8 + (t0 + 8 * n + 4 * side + 4))
                dve.wait_ge(gate_loaded[side], i * 16 + 16 * (n + 1))
                dst = merged if side == 0 else gv2
                for t in range(TOK):
                    last = V.tensor_tensor(dst[:, t, :], acc[(c0 + side) % 2][t][:, :], U[:, side, t, :], ALU.mult)
                last.then_inc(chunk_evac, 1)
                if side:
                    dve.wait_ge(chunk_evac, i * 2 + (c0 + 2 * n + 2))
                    V.tensor_tensor(merged, merged, gv2, ALU.add).then_inc(m_ready, 1)
                    dve.wait_ge(m_ready, i + (n + 1))

            def merged_lo(n):
                for q in range(2):
                    dve.wait_ge(m_hi, n * 2 + (q + 1))
                    V.tensor_tensor(sb_lo[:, bass.ds(n * 4 + 2 * q, 2), :], bank2(M[q]),
                                    sb_hi[:, bass.ds(n * 4 + 2 * q, 2), :].bitcast(F32), ALU.subtract).then_inc(m_lo, 1)

            def proj(n, i, first):
                tb, off = PHASES["proj"][0] + RING + 8 * n, i * 8
                for j in range(4):
                    split(tb + j, off)
                if not first:
                    merged_lo(i)
                ada(16 * SC_F + 2 * n, i * 2)
                half(n, 0, i)
                for j in range(4, 8):
                    split(tb + j, off)
                ada(16 * SC_F + 2 * n + 1, i * 2)
                half(n, 1, i)

            proj(0, 0, True)
            with dve.Fori(0, 3) as i:
                proj(1, i, False)
            spread = gv2.rearrange("p t (k n) -> p (t k) n", n=P)

            def diagonals_of_gate(half):
                for k in range(8):
                    last = V.tensor_scalar(spread[:, k, :], ident[:, :], gate_a[:, 8 * half + k:8 * half + k + 1], None, ALU.mult)
                last.then_inc(spread_ready, 1)

            def gate_a_ready(half):
                dve.wait_ge(bias_landed, 16)
                dve.wait_ge(gate_spread, half + 1)
                for n in range(2):
                    cols = slice((2 * half + n) * NC, (2 * half + n + 1) * NC)
                    last = V.tensor_tensor(gt[:, cols], M[2 + n][:, :], gt[:, cols], ALU.add)
                last.then_inc(gt_ready, 1)

            dve.wait_ge(res_landed, 16)

            def update(name, c, i=0):
                t0, c0, _, k = PHASES[name]
                dve.wait_ge(tile_used, i * (2 * k) + (t0 + (c + 1) * k))
                cols = bass.ds(i * 2 * NC + c * NC, NC)
                for t in range(TOK):
                    last = V.tensor_tensor(gv2[:, t, :], acc[(c0 + c) % 2][t][:, :], gt[:, cols], ALU.mult)
                last.then_inc(chunk_evac, 1)
                dve.wait_ge(chunk_evac, i * 2 + (c0 + c + 1))
                V.tensor_tensor(X[:, :, cols], X[:, :, cols], gv2, ALU.add).then_inc(x_updated, 1)
                dve.wait_ge(x_updated, i * 2 + (UPDATES[name] + c + 1))

            t0 = PHASES["wo"][0]
            n = 16 * SC_F + 8
            for c in range(4):
                for j in range(8):
                    if c == 0 and j == 3:
                        merged_lo(3)
                        dve.wait_ge(mod_ready, 10)
                        diagonals_of_gate(0)
                    if j in ((1, 4), (1, 4, 6), (1, 4, 6), ())[c]:
                        ada(n)
                        n += 1
                    split(t0 + 8 * c + j + RING)
                    if c == 0 and j == 5:
                        gate_a_ready(0)
                        diagonals_of_gate(1)
                    if c == 0 and j == 7:
                        gate_a_ready(1)
                        dve.wait_ge(gt_ready, 2)
                    if c == 3 and j == 3:
                        scale_ready(SC_F, V_SCF, V_GFFN)
                update("wo", c)
            norm_x(TOK + 5)
            norm_lo(gv2, sa_hi, sa_lo, 0, 8, mod_s, mod_b)

            def conv(side, pg):
                dve.wait_ge(cv_based, pg * 2 + (side + 1))
                for tap, lag in ((1, 1), (0, 2)):
                    for b in range(4):
                        v = cv[:, 4 * side + b, lag:S]
                        last = V.scalar_tensor_tensor(out=v, in0=M[2 * side + b // 2][:, (b % 2) * S:(b % 2) * S + S - lag],
                                                      scalar=cvec[:, tap, bass.ds(pg * 4 + (44 * side + b), 1)], in1=v,
                                                      op0=ALU.mult, op1=ALU.add)
                    if lag == 1:
                        link(last)
                    else:
                        last.then_inc(cv_done, 1)

            def times(pg):
                dve.wait_ge(cv_done, pg * 2 + 2)
                dve.wait_ge(silu_done, pg + 1)
                V.tensor_tensor(gv[:, :, :], cv[:, 0:4, :], cv[:, 4:8, :], ALU.mult).then_inc(gv_ready, 1)

            def ffn_lo(pg, pl):
                dve.wait_ge(f_hi, pg + 1)
                V.tensor_tensor(sb_lo[:, bass.ds(pl * 4, 4), :], gv[:, :, :], sb_hi[:, bass.ds(pl * 4, 4), :].bitcast(F32),
                                ALU.subtract).then_inc(f_lo, 1)

            def up_pair(part, i, shift, first, n):
                t0 = PHASES[f"up{part}"][0] + 16 * shift
                off = i * 16
                for j in range(4):
                    split(t0 + RING + j, off)
                if not first:
                    conv(1, i + (shift + 4 * part - 1))
                    times(i + (shift + 4 * part - 1))
                split(t0 + RING + 4, off)
                split(t0 + RING + 5, off)
                if not first:
                    ffn_lo(i + (shift + 4 * part - 1), i + (shift - 1))
                split(t0 + RING + 6, off)
                ada(n, i * 4)
                split(t0 + RING + 7, off)
                split(t0 + RING + 8, off)
                ada(n + 1, i * 4)
                split(t0 + RING + 9, off)
                split(t0 + RING + 10, off)
                ada(n + 2, i * 4)
                split(t0 + RING + 11, off)
                conv(0, i + (shift + 4 * part))
                split(t0 + RING + 12, off)
                split(t0 + RING + 13, off)
                ada(n + 3, i * 4)
                split(t0 + RING + 14, off)
                split(t0 + RING + 15, off)

            for part, n in enumerate(PAIRS):
                first = (16 * GT_F, 16 * SH_2 + 8, 16 * GT_2)[part]
                if part != 1:
                    ada_begin(first // 16)
                up_pair(part, 0, 0, True, first)
                peeled = 1
                if part == 1:
                    up_pair(part, 0, 1, False, first + 4)
                    shift_ready(SH_2, V_SH2)
                    ada_begin(SC_2)
                    peeled = 2
                with dve.Fori(0, n - peeled) as i:
                    order.enter(i, 2)
                    up_pair(part, i, peeled, False, first + 4 * peeled)
                    order.leave(n - peeled)
                t0, _, _, k = PHASES[f"down{part}"]
                for c in range(4):
                    for j in range(k):
                        if c == 0 and j == (2 if k == 8 else 1):
                            conv(1, 4 * part + n - 1)
                            times(4 * part + n - 1)
                            if part == 0:
                                gate_ready(GT_F, 0, 0)
                        if c == 0 and j == k - 3:
                            ffn_lo(4 * part + n - 1, n - 1)
                        if c == 0 and j == k - 1 and part == 0:
                            gate_ready(GT_F, 1, 0)
                            dve.wait_ge(gt_ready, 4)
                        if c == 1 and j == 0 and part == 0:
                            ada_begin(SH_2)
                        if part == 1 and j in ((1, 3) if c else (6, 7)):
                            ada(16 * SC_2 + 8 + 2 * c + (j > (1 if c else 6)))
                        if part == 0 and j in ((), (1, 3, 6), (1, 3, 6), (1, 3))[c]:
                            ada(16 * SH_2 + (0, 0, 3, 6)[c] + (1, 3, 6).index(j))
                        split(t0 + c * k + j + RING)
                    update(f"down{part}", c)
                if part == 1:
                    scale_ready(SC_2, V_SC2)

            norm_x(TOK + 9)
            norm_lo(gv2, sa_hi, sa_lo, 0, 8, mod_s, mod_b)

            def pooled_lo(c):
                for q in range(2):
                    dve.wait_ge(p_hi, 2 * c + q + 1)
                    k = 4 * c + 2 * q
                    V.tensor_tensor(sb_lo[:, k:k + 2, :], bank2(M[2 * (c % 2) + q]), sb_hi[:, k:k + 2, :].bitcast(F32),
                                    ALU.subtract).then_inc(p_lo, 1)

            t0 = PHASES["pin"][0] + RING
            for c in range(4):
                for j in range(8):
                    if c and j == 4:
                        pooled_lo(c - 1)
                    split(t0 + 8 * c + j)
                    if c == 0 and j % 2:
                        ada(16 * GT_2 + 12 + j // 2)

            def y_scale(n):
                dve.wait_ge(y_turned, 2 * n + 2)
                for b in range(4):
                    last = V.tensor_scalar(gv[:, b, :], M[2 * (n % 2) + b // 2][:, (b % 2) * S:(b % 2 + 1) * S],
                                           vecs[:, V_PSCALE + 4 * n + b:V_PSCALE + 4 * n + b + 1], None, ALU.mult)
                last.then_inc(y_scaled, 1)

            def y_low(n):
                dve.wait_ge(y_hi, n + 1)
                V.tensor_tensor(sb_lo[:, 4 * n:4 * n + 4, :], gv[:, :, :], sb_hi[:, 4 * n:4 * n + 4, :].bitcast(F32),
                                ALU.subtract).then_inc(y_lo, 1)
                dve.wait_ge(y_lo, n + 1)

            for n in range(4):
                t0, c0, _, _ = PHASES[f"gp{n}"]
                for j in range(8):
                    split(t0 + RING + j)
                    if n == 0 and j == 3:
                        pooled_lo(3)
                    if n == 1 and j in (1, 3):
                        gate_ready(GT_2, j // 2, 2)
                    if n and j == 5:
                        y_scale(n - 1)
                if n:
                    y_low(n - 1)
                split(t0 + RING + 8)
                split(t0 + RING + 9)
                dve.wait_ge(chunk_evac, c0 + 1)
                dve.wait_ge(tile_used, t0 + 10)
                for t in range(TOK):
                    last = V.tensor_tensor(U[:, n % 2, t, :], acc[(c0 + 1) % 2][t][:, :], ada_ring[:, t, n * NC:(n + 1) * NC], ALU.mult)
                last.then_inc(chunk_evac, 1)

            def final_gain(c):
                dve.wait_ge(xsq_done, TOK + 9 + c + 1)
                cols = slice(c * NC, (c + 1) * NC)
                V.tensor_tensor(X[:, :, cols], X[:, :, cols], fgain[:, cols].unsqueeze(1).broadcast_to([P, TOK, NC]), ALU.mult).then_inc(fg_applied, 1)

            t0 = PHASES["pout"][0]
            dve.wait_ge(gt_ready, 6)
            dve.wait_ge(fg_landed, 16)
            for c in range(4):
                for j in range(8):
                    if c == 0 and j == 5:
                        y_low(3)
                    split(t0 + 8 * c + j + RING)
                    if c == 0 and j == 2:
                        y_scale(3)
                    if c and j == 3:
                        final_gain(c - 1)
                update("pout", c)
            dve.wait_ge(xsq_done, TOK + 13)
            link(V.reduce_sum(rstd[:, 0:TOK], ssq[:, :, :], AX))
            V.tensor_scalar(stat[:, 0, 0:TOK], rstd[:, 0:TOK], 1.0 / D, EPS, ALU.mult, ALU.add).then_inc(ms_ready, 1)
            final_gain(3)
            dve.wait_ge(sqrt_ready, norms[0] + 1)
            V.reciprocal(rstd[:, 0:TOK], stat[:, 1, 0:TOK]).then_inc(diag_ready, 1)
            dve.wait_ge(diag_ready, 5)
            for h in range(2):
                half = slice(h * D // 2, (h + 1) * D // 2)
                V.tensor_scalar(X[:, 0, half], X[:, 0, half], rstd[:, 0:1], None, ALU.mult).then_inc(outD, 1)

        @block.tensor
        def _(pe):
            mm = nc.tensor.matmul

            def tile(tb, off, hi, lo, ks, pair, first, last):
                pe.wait_ge(lo_ready, tb + 1 + off)
                for n, k in enumerate(ks):
                    for t in range(TOK):
                        xh, xl = hi[:, k, t * P:(t + 1) * P], lo[:, k, t * P:(t + 1) * P]
                        wh, wl = whi[:, tb % RING, n, :], wlo[:, tb % RING, n, :]
                        mm(pair[t][:, :], xh, wh, start=first and n == 0, stop=False)
                        mm(pair[t][:, :], xh, wl, start=False, stop=False)
                        end = mm(pair[t][:, :], xl, wh, start=False, stop=last and n == 1)
                end.then_inc(tile_used, 1)

            def bank_free(c, i=0, per=1):
                if c >= 2:
                    pe.wait_ge(chunk_evac, i * per + (c - 1))

            def tiles(name, c, js, hi, lo, i=0, per=1, k0=0, wait=None):
                t0, c0, _, k = PHASES[name]
                for j in js:
                    if j == 0:
                        bank_free(c0 + c, i, per)
                    if wait:
                        wait(j)
                    tile(t0 + c * k + j, i * (per * k), hi, lo, (k0 + 2 * j, k0 + 2 * j + 1), acc[(c0 + c) % 2], j == 0, j == k - 1)

            def sum_cols(r):
                pe.wait_ge(ada_used, 16 * (r + 1))
                for b in range(16):
                    last = mm(M[0][:, b:b + 1], ada_acc[:, b * P:(b + 1) * P], ones[:, 0:1], start=True, stop=True)
                last.then_inc(cols_summed, 1)

            def sum_rows(r, half, bank):
                pe.wait_ge(ada_used, 16 * (r + 1))
                for n in range(2):
                    last = mm(M[bank + n][:, :], ones[:, :], ada_acc[:, (2 * half + n) * NC:(2 * half + n + 1) * NC], start=True, stop=True)
                last.then_inc(rows_summed, 1)

            pairs = [0]
            diags = [0]

            def norm_turn(src, npair, scales=lambda k: diag):
                diags[0] += 1
                pe.wait_ge(diag_ready, diags[0])
                for b in range(npair):
                    if b >= 4:
                        pe.wait_ge(nrm_evac, pairs[0] + b - 3)
                    for kk in range(2):
                        for t in range(TOK):
                            k = 2 * b + kk
                            last = mm(M[b % 4][:, kk * S + t * P:kk * S + (t + 1) * P], src(t, k), scales(k)[:, t, :], start=True, stop=True)
                    last.then_inc(nrm_turned, 1)
                pairs[0] += npair

            pe.wait_ge(ones_ready, 1)
            pe.wait_ge(vec_landed, 16 * 13)
            nc.tensor.transpose(M[1][:, 0:P], vstage[:, 0, :], ident[:, :])
            nc.tensor.transpose(M[1][:, P:P + 22], vstage[0:22, 1, :], ident[0:22, 0:22]).then_inc(vec_turned, 1)
            for j in range(4):
                last = nc.tensor.transpose(M[2][:, 88 * j:88 * (j + 1)], vstage[0:88, 2 + j, :], ident[0:88, 0:88])
            last.then_inc(vec_turned, 1)
            at = [0]

            def upto(n):
                while at[0] < n:
                    t = at[0]
                    if t < PHASES["mq"][0]:
                        c, k = in_tile(t)
                        if k == 0 and c == 2:
                            pe.wait_ge(vec_ready, 2)
                        elif k == 0:
                            bank_free(c)
                        if t < TOGETHER:
                            pe.wait_ge(nrm_lo, k + 1)
                        tile(t, 0, sa_hi, sa_lo, (2 * k, 2 * k + 1), banks(c), k == 0, k == 7)
                    elif t < PHASES["mkv"][0]:
                        c, j = divmod(t - PHASES["mq"][0], 2)
                        tiles("mq", c, (j,), lat_hi, lat_lo)
                    else:
                        tiles("mkv", t - PHASES["mkv"][0], (0,), lat_hi, lat_lo, k0=4)
                    at[0] += 1

            for q in range(4):
                for r, sums in enumerate((ada_acc, start_acc)):
                    if q:
                        upto(6 * q - 2 + 2 * r)
                    if q and r == 0:
                        pe.wait_ge(nrm_evac, 2 * q)
                    pe.wait_ge(ada_used, 8 * q + 4 * r + 4)
                    for b in range(4):
                        for a in range(2):
                            lo = (q % 2 * 2 + a) * NC + b * P
                            last = mm(M[0][:, 16 * r + 4 * q + b:16 * r + 4 * q + b + 1], sums[:, lo:lo + P], ones[:, 0:1],
                                      start=a == 0, stop=a == 1)
                    last.then_inc(cols_summed, 1)
                pe.wait_ge(mod_ready, 2 * q + 2)
                if q == 0:
                    pe.wait_ge(diag_ready, 1)
                for b in range(2):
                    for kk in range(2):
                        for t in range(TOK):
                            k = 4 * q + 2 * b + kk
                            last = mm(M[1 - b][:, kk * S + t * P:kk * S + (t + 1) * P], xs[:, t, k * P:(k + 1) * P], diag[:, t, :],
                                      start=True, stop=True)
                    last.then_inc(nrm_turned, 1)
            upto(24)
            pairs[0], diags[0] = 8, 1

            upto(28)
            pe.wait_ge(qi_roped, 1)
            for b in range(8):
                for t in range(TOK):
                    last = nc.tensor.transpose(M[b // 2][:, (b % 2) * S + t * P:(b % 2) * S + (t + 1) * P],
                                               qi[:, t, 2 * b:2 * b + 2, :].rearrange("p h d -> p (h d)"), ident[:, :])
                if b % 2:
                    last.then_inc(qi_turned, 1)
            upto(29)
            pe.wait_ge(qi_evac, 1)
            for t in range(TOK):
                last = nc.tensor.transpose(M[0][:, t * P:(t + 1) * P], kirep[:, t, :], ident[:, :])
            last.then_inc(qi_turned, 1)
            upto(38)
            pe.wait_ge(qi_evac, 5)
            norm_turn(lambda t, k: mql[:, t, k * P:(k + 1) * P] if k < 4 else pm[:, t, (k - 4) * P:(k - 3) * P], 3,
                      lambda k: diag if k < 4 else diag2)
            for b in range(4):
                upto(42 + 2 * b)
                if b == 0:
                    pe.wait_ge(nrm_lo, 11)
                for h in range(4 * b, 4 * b + 4):
                    if b:
                        pe.wait_ge(relu_ready, h - 3)
                    part = slice(ID * (h % 2), ID * (h % 2 + 1))
                    for t in range(TOK):
                        last = mm(M[h % 4][:, t * S:(t + 1) * S], qiT[part, h // 2, t * P:(t + 1) * P], kiT[part, :], start=True, stop=True)
                    last.then_inc(dots_ready, 1)
            upto(60)
            pe.wait_ge(relu_ready, IH)
            pe.wait_ge(k_normed, 1)
            for g in range(GROUPS):
                for t in range(TOK):
                    last = nc.tensor.transpose(M[0][:, g * S + t * P:g * S + (t + 1) * P], pkv[:, t, g * HD:(g + 1) * HD], ident[:, :])
            last.then_inc(k_turned, 1)
            upto(68)
            pe.wait_ge(k_evac, 1)
            sum_cols(SH_F)
            pe.wait_ge(mod_ready, 9)

            def turn_probs(pr, s, bank, ready, h, done):
                pe.wait_ge(ready, h + 1)
                nc.tensor.transpose(bank[:, 0:P], pr[:, s, 0, 0:P], ident[:, :])
                nc.tensor.transpose(bank[:, P:2 * P], pr[:, s, 1, 0:P], ident[:, :])
                nc.tensor.transpose(bank[:, 2 * P:3 * P], pr[:, s, 1, P:2 * P], ident[:, :]).then_inc(done, 1)

            def weigh(pT, s, v, bank, evac, h, done):
                pe.wait_ge(evac, h + 1)
                mm(bank[:, 0:S], v[0], pT[:, s, 0:S], start=True, stop=False, skip_group_check=True)
                mm(bank[:, P:S], v[1], pT[:, s, S:384], start=False, stop=True, skip_group_check=True).then_inc(done, 1)

            def turn_A(s, h):
                pe.wait_ge(A_staged, h + 1)
                for t in range(TOK):
                    last = nc.tensor.transpose(M[0][:, s * S + t * P:s * S + (t + 1) * P], qsA[:, s, t, :], ident[:, :])
                last.then_inc(A_turned, 1)

            def logits_A(i, s, h):
                pe.wait_ge(A_qT, h + 1)
                for t in range(TOK):
                    last = mm(M[1 + s][:, t * S:(t + 1) * S], qTA[:, s, t * P:(t + 1) * P],
                              kT[:, bass.ds(i, 1), :].rearrange("p a n -> p (a n)"), start=True, stop=True)
                last.then_inc(A_logits, 1)

            values = [vA[:, t, :] for t in range(TOK)]
            with pe.Fori(0, 2) as i:
                for c in range(2):
                    h = i * 4 + 2 * c

                    def gate(*js):
                        tiles("gate", c, js, sa_hi, sa_lo, i, 2)

                    gate(0, 1)
                    turn_A(0, h)
                    gate(2)
                    logits_A(i, 0, h)
                    turn_A(1, h + 1)
                    gate(3)
                    logits_A(i, 1, h + 1)
                    gate(4)
                    turn_probs(prA, 0, M[3], A_probs, h, A_pT)
                    gate(5)
                    if c == 0:
                        pe.wait_ge(A_v, i + 1)
                    weigh(pTA, 0, values, M[1], A_pT_evac, h, A_o)
                    gate(6)
                    turn_probs(prA, 1, M[0], A_probs, h + 1, A_pT)
                    gate(7)
                    weigh(pTA, 1, values, M[2], A_pT_evac, h + 1, A_o)

            def turn_B(s, h):
                pe.wait_ge(B_staged, h + 1)
                for x, v in enumerate((qsB, ksB)):
                    for t in range(TOK):
                        at = slice(x * S + t * P, x * S + (t + 1) * P)
                        nc.tensor.transpose(M[2 * s][:, at], v[:, s, t, 0:NOPE], ident[:, :])
                        last = nc.tensor.transpose(M[1 + 2 * s][0:MROT, at], v[:, s, t, NOPE:MD], ident[:, :])
                last.then_inc(B_turned, 1)

            def logits_B(s, h):
                pe.wait_ge(B_nT, h + 1)
                pe.wait_ge(B_rT, h + 1)
                for t in range(TOK):
                    bank = M[1 + 2 * s][:, t * S:(t + 1) * S]
                    mm(bank, nT[:, s, 0, t * P:(t + 1) * P], nT[:, s, 1, :], start=True, stop=False)
                    last = mm(bank, rT[0:MROT, s, 0, t * P:(t + 1) * P], rT[0:MROT, s, 1, :], start=False, stop=True)
                last.then_inc(B_logits, 1)

            with pe.Fori(0, 2) as i:
                for c in range(2):
                    h = i * 4 + 2 * c

                    def gate(*js):
                        tiles("gate", 4 + c, js, sa_hi, sa_lo, i, 2)

                    gate(0, 1)
                    pe.wait_ge(B_v, i * 2 + (c + 1))
                    turn_B(0, h)
                    gate(2, 3)
                    logits_B(0, h)
                    turn_B(1, h + 1)
                    gate(4)
                    logits_B(1, h + 1)
                    gate(5)
                    turn_probs(prB, 0, M[0], B_probs, h, B_pT)
                    gate(6)
                    weigh(pTB, 0, [vB[:, 0, t, :] for t in range(TOK)], M[1], B_pT_evac, h, B_o)
                    turn_probs(prB, 1, M[2], B_probs, h + 1, B_pT)
                    gate(7)
                    weigh(pTB, 1, [vB[:, 1, t, :] for t in range(TOK)], M[3], B_pT_evac, h + 1, B_o)

            def merged_turn(n):
                pe.wait_ge(m_ready, n + 1)
                for q in range(2):
                    for b in range(2):
                        for t in range(TOK):
                            blk = (2 * q + b) * P
                            last = nc.tensor.transpose(M[q][:, b * S + t * P:b * S + (t + 1) * P], merged[:, t, blk:blk + P], ident[:, :])
                    last.then_inc(m_turned, 1)

            def proj(n, i, first):
                ready = [lambda j, s=s: pe.wait_ge(o_lo, 2 * s + j // 2 + 1) for s in range(2)] if first else [None, None]
                tiles("proj", 2 * n, (0, 1, 2), sa_hi, sa_lo, i, 2, wait=ready[0])
                if not first:
                    merged_turn(i)
                tiles("proj", 2 * n, (3,), sa_hi, sa_lo, i, 2, wait=ready[0])
                tiles("proj", 2 * n + 1, range(4), sa_hi, sa_lo, i, 2, k0=8, wait=ready[1])

            sum_cols(GT_A)
            proj(0, 0, True)
            pe.wait_ge(mod_ready, 10)
            with pe.Fori(0, 3) as i:
                proj(1, i, False)
            pe.wait_ge(m_lo, 6)

            def spread_gate(half):
                pe.wait_ge(spread_ready, half + 1)
                if half:
                    pe.wait_ge(gt_ready, 1)
                for k in range(8):
                    last = mm(M[2 + k // 4][:, (k % 4) * P:(k % 4 + 1) * P], ones[:, :],
                              gv2[:, k // 4, (k % 4) * P:(k % 4 + 1) * P], start=True, stop=True)
                last.then_inc(gate_spread, 1)

            tiles("wo", 0, (0, 1, 2), sb_hi, sb_lo)
            merged_turn(3)
            tiles("wo", 0, range(3, 6), sb_hi, sb_lo)
            spread_gate(0)
            pe.wait_ge(m_lo, 8)
            tiles("wo", 0, (6, 7), sb_hi, sb_lo)
            spread_gate(1)
            for c in (1, 2):
                tiles("wo", c, range(8), sb_hi, sb_lo)
            tiles("wo", 3, (0, 1), sb_hi, sb_lo)
            sum_cols(SC_F)
            tiles("wo", 3, range(2, 8), sb_hi, sb_lo)
            pe.wait_ge(gt_ready, 2)
            pe.wait_ge(mod_ready, 11)
            norm_turn(lambda t, k: X[:, t, k * P:(k + 1) * P], 8)

            def turn(side):
                for q in range(2):
                    for b in range(2):
                        for t in range(TOK):
                            blk = (2 * q + b) * P
                            last = nc.tensor.transpose(M[2 * side + q][:, b * S + t * P:b * S + (t + 1) * P],
                                                       U[:, side, t, blk:blk + P], ident[:, :])
                    last.then_inc(u_turned, 1)

            def up_pair(part, i, shift, first, wait=None):
                name = f"up{part}"
                c0 = PHASES[name][1]
                c = 2 * shift
                tiles(name, c, range(4), sa_hi, sa_lo, i, 2, wait=wait)
                if not first:
                    pe.wait_ge(chunk_evac, i * 2 + (c0 + c))
                    turn(1)
                tiles(name, c, range(4, 8), sa_hi, sa_lo, i, 2, wait=wait)
                tiles(name, c + 1, range(4), sa_hi, sa_lo, i, 2)
                pe.wait_ge(chunk_evac, i * 2 + (c0 + c + 1))
                turn(0)
                tiles(name, c + 1, range(4, 8), sa_hi, sa_lo, i, 2)

            for part, n in enumerate(PAIRS):
                up_pair(part, 0, 0, True, (lambda j: pe.wait_ge(nrm_lo, 12 + j)) if part == 0 else None)
                peeled = 1
                if part == 1:
                    up_pair(part, 0, 1, False)
                    pe.wait_ge(cv_done, 2 * 5 + 1)
                    sum_cols(SH_2)
                    pe.wait_ge(mod_ready, 12)
                    peeled = 2
                with pe.Fori(0, n - peeled) as i:
                    up_pair(part, i, peeled, False)
                _, c0, nn, _ = PHASES[f"up{part}"]
                name = f"down{part}"
                k = PHASES[name][3]
                pe.wait_ge(f_lo, 4 * part + n - 1)
                a = 2 if k == 8 else 1
                tiles(name, 0, range(a), sb_hi, sb_lo)
                pe.wait_ge(chunk_evac, c0 + nn)
                turn(1)
                if part == 0:
                    pe.wait_ge(cv_done, 2 * n - 1)
                    sum_rows(GT_F, 0, 0)
                tiles(name, 0, range(a, k - 2), sb_hi, sb_lo)
                pe.wait_ge(f_lo, 4 * part + n)
                tiles(name, 0, (k - 2,), sb_hi, sb_lo)
                if part == 0:
                    pe.wait_ge(gt_ready, 3)
                    sum_rows(GT_F, 1, 0)
                tiles(name, 0, (k - 1,), sb_hi, sb_lo)
                for c in range(1, 4):
                    tiles(name, c, range(k), sb_hi, sb_lo)
                if part == 1:
                    pe.wait_ge(cv_done, 2 * (4 * part + n) - 1)
                    sum_cols(SC_2)
                    pe.wait_ge(mod_ready, 13)

            norm_turn(lambda t, k: X[:, t, k * P:(k + 1) * P], 8)

            def pooled(c):
                pe.wait_ge(chunk_evac, PHASES["pin"][1] + c + 1)
                pe.wait_ge(pmat_landed, 16)
                if c >= 2:
                    pe.wait_ge(p_lo, 2 * (c - 1))
                for q in range(2):
                    for b in range(2):
                        blk = (2 * q + b) * P
                        for t in range(TOK):
                            last = mm(M[2 * (c % 2) + q][:, b * S:(b + 1) * S], U[:, c % 2, t, blk:blk + P], cv[:, 2 * c + t, :],
                                      start=t == 0, stop=t == TOK - 1)
                    last.then_inc(p_turned, 1)

            for c in range(4):
                wait = (lambda j: pe.wait_ge(nrm_lo, 20 + j)) if c == 0 else None
                tiles("pin", c, range(4), sa_hi, sa_lo, wait=wait)
                if c:
                    pooled(c - 1)
                tiles("pin", c, range(4, 8), sa_hi, sa_lo, wait=wait)

            def y_turn(n):
                pe.wait_ge(chunk_evac, PHASES[f"grp{n}"][1] + 1)
                if n >= 2:
                    pe.wait_ge(y_scaled, n - 1)
                for q in range(2):
                    for b in range(2):
                        for t in range(TOK):
                            blk = (2 * q + b) * P
                            last = nc.tensor.transpose(M[2 * (n % 2) + q][:, b * S + t * P:b * S + (t + 1) * P],
                                                       U[:, n % 2, t, blk:blk + P], ident[:, :])
                    last.then_inc(y_turned, 1)

            for n in range(4):
                for j in range(8):
                    tiles(f"gp{n}", 0, (j,), sa_hi, sa_lo)
                    if n == 0 and j == 3:
                        pooled(3)
                    if n == 1 and j == 1:
                        pe.wait_ge(p_lo, 8)
                        sum_rows(GT_2, 0, 2)
                    if n == 1 and j == 3:
                        pe.wait_ge(gt_ready, 5)
                        sum_rows(GT_2, 1, 2)
                    if n and j == 5:
                        if n == 2:
                            pe.wait_ge(gt_ready, 6)
                        y_turn(n - 1)
                pe.wait_ge(p_lo, 2 * n + 2)
                tiles(f"grp{n}", 0, range(2), sb_hi, sb_lo, k0=4 * n)
            pe.wait_ge(y_lo, 3)
            tiles("pout", 0, range(2), sb_hi, sb_lo)
            y_turn(3)
            tiles("pout", 0, range(2, 6), sb_hi, sb_lo)
            pe.wait_ge(y_lo, 4)
            tiles("pout", 0, (6, 7), sb_hi, sb_lo)
            for c in range(1, 4):
                tiles("pout", c, range(8), sb_hi, sb_lo)


_INS = ["x", "c", "positions", "g_attn", "g_ffn", "w_ada", "b_ada", "w_in", "g_qa", "g_ka", "g_mq_lat", "w_mq_up",
        "g_mkv_lat", "w_mkv_up", "g_qm", "g_km", "w_pa", "w_pb", "w_o", "w_up", "w_conv", "b_conv", "w_down",
        "c_2", "w_mod_2", "b_mod_2", "pool_w_in_2", "pool_w_grp_2", "pool_scale_2", "pool_w_out_2", "final_norm_g_2"]


def shape_constants():
    inv = [THETA ** (-np.arange(0, r, 2) / r) for r in (ROT, IROT, MROT)]
    q, k = np.arange(S)[:, None], np.arange(S)[None, :]
    causal = np.where(k <= q, 0.0, MASKED).reshape(TOK, P, S).transpose(1, 0, 2)
    pool = np.zeros((4, S, S))
    for g, w in enumerate(WINDOWS):
        lo, hi = np.maximum(q - w // 2, 0), np.minimum(q + w // 2, S)
        pool[g] = (((k >= lo) & (k < hi)) / (hi - lo) - np.eye(S)).T
    pool = pool.reshape(4, TOK, P, S).transpose(2, 0, 1, 3).reshape(P, 4 * TOK, S)
    return {"identity": np.eye(P, dtype=np.float32), "inv_freq": np.concatenate(inv)[None].astype(np.float32),
            "causal": causal.astype(np.float32), "pool_matrix": np.ascontiguousarray(pool).astype(np.float32)}


def kernel(**inputs):
    import numpy as _np
    import concourse.bacc as _bacc
    from concourse.bass_utils import run_bass_kernel_spmd as _run

    nc = _bacc.Bacc("TRN2", target_bir_lowering=False, num_devices=1)
    arrays, args = {}, {}
    given = {n: _np.ascontiguousarray(inputs[n]) for n in _INS}
    for name, a in {**given, **shape_constants()}.items():
        arrays[f"in_{name}_dram"] = a
        args[name] = nc.dram_tensor(f"in_{name}_dram", a.shape, mybir.dt.from_np(a.dtype), kind="ExternalInput").ap()
    out = nc.dram_tensor("out_0_dram", (1, S, D), F32, kind="ExternalOutput").ap()
    build(nc, args, out)
    r = _run(nc, [arrays], core_ids=[0])
    return r.results[0]["out_0_dram"]
```
